# Optimizing a Trainium2 kernel written in Bass

```python
import jax
import jax.numpy as jnp
from jax import lax
import numpy as np

D_MODEL = 1024
BATCH = 1
SEQ = 512
DEPTH = 2

GRID_W = 64
CTX_LEN = 256

NA_HEAD_DIM = 64
NA_HEADS = (D_MODEL // 2) // NA_HEAD_DIM
NA_WIDTH = NA_HEADS * NA_HEAD_DIM
NA_KH = 8
NA_KW = 16
ML_HEAD_DIM = 128
ML_HEADS = (D_MODEL // 2) // ML_HEAD_DIM
ML_WIDTH = ML_HEADS * ML_HEAD_DIM
ML_CHUNK = 128
ML_GATE_CAP = 15.0
AB_IN_WIDTH = 3 * NA_WIDTH + 4 * ML_WIDTH + 4 * ML_HEADS
RW_HEAD_DIM = 64
RW_HEADS = D_MODEL // RW_HEAD_DIM
RW_DECAY_LORA = 64
RW_AAA_LORA = 64
RW_GATE_LORA = 160
RW_GN_EPS = 64e-5
D_FF = 4 * D_MODEL
ROPE_BASE = 10000.0
NORM_EPS = 1e-6


def rms_norm(x, eps=NORM_EPS):
    xf = x.astype(jnp.float32)
    return (xf * lax.rsqrt(jnp.mean(xf * xf, axis=-1, keepdims=True) + eps)).astype(x.dtype)

def modulate(x, shift, scale):
    return rms_norm(x) * (1.0 + scale) + shift

def split_heads(t, n_heads, head_dim):
    return t.reshape(*t.shape[:-1], n_heads, head_dim)

def adaln(cond, w, b):
    return jnp.split(jax.nn.silu(cond) @ w + b, 6, axis=-1)

def squared_relu_mlp(h, w1, w2):
    return jnp.square(jax.nn.relu(h @ w1)) @ w2

def axial_rope_angles(n_tokens, head_dim):
    pos = jnp.arange(n_tokens)
    rows = (pos // GRID_W).astype(jnp.float32)
    cols = (pos % GRID_W).astype(jnp.float32)
    n_freq = head_dim // 4
    inv_freq = ROPE_BASE ** (-jnp.arange(n_freq, dtype=jnp.float32) / n_freq)
    return rows[:, None] * inv_freq, cols[:, None] * inv_freq

def rope_rotate(x, ang):
    x1, x2 = jnp.split(x, 2, axis=-1)
    cos = jnp.cos(ang)[:, None, :].astype(x.dtype)
    sin = jnp.sin(ang)[:, None, :].astype(x.dtype)
    return jnp.concatenate([x1 * cos - x2 * sin, x1 * sin + x2 * cos], axis=-1)

def axial_rope(x, ang_r, ang_c):
    x_row, x_col = jnp.split(x, 2, axis=-1)
    return jnp.concatenate([rope_rotate(x_row, ang_r), rope_rotate(x_col, ang_c)], axis=-1)

def context_attention(q, k, v):
    s = jnp.einsum('bqhd,bkhd->bhqk', q, k).astype(jnp.float32) * (q.shape[-1] ** -0.5)
    p = jax.nn.softmax(s, axis=-1).astype(v.dtype)
    return jnp.einsum('bhqk,bkhd->bqhd', p, v)

def neighbourhood_attention(q, k, v, k_ctx, v_ctx, rpb):
    n_b, n_tok, n_h, d_h = q.shape
    rows = n_tok // GRID_W
    kh = min(NA_KH, rows)
    n_win = kh * NA_KW
    scale = d_h ** -0.5
    qg = q.reshape(n_b, rows, GRID_W, n_h, d_h)
    kg = k.reshape(n_b, rows, GRID_W, n_h, d_h)
    vg = v.reshape(n_b, rows, GRID_W, n_h, d_h)
    row_idx = jnp.arange(rows)
    row_start = jnp.clip(row_idx - kh // 2, 0, rows - kh)
    col_idx = jnp.arange(GRID_W)
    col_win = jnp.clip(col_idx - NA_KW // 2, 0, GRID_W - NA_KW)[:, None] + jnp.arange(NA_KW)[None, :]
    rpb_c = rpb[:, :, col_win - col_idx[:, None] + NA_KW - 1]

    def one_row(args):
        r, rs, q_row = args
        k_nb = lax.dynamic_slice_in_dim(kg, rs, kh, axis=1)[:, :, col_win]
        v_nb = lax.dynamic_slice_in_dim(vg, rs, kh, axis=1)[:, :, col_win]
        bias = rpb_c[:, rs + jnp.arange(kh) - r + NA_KH - 1]
        s_nb = jnp.einsum('bchd,bicjhd->bhcij', q_row, k_nb).astype(jnp.float32) * scale + jnp.transpose(bias, (0, 2, 1, 3))
        s_cx = jnp.einsum('bchd,bnhd->bhcn', q_row, k_ctx).astype(jnp.float32) * scale
        p = jax.nn.softmax(jnp.concatenate([s_nb.reshape(n_b, n_h, GRID_W, n_win), s_cx], axis=-1), axis=-1).astype(v.dtype)
        p_nb = p[..., :n_win].reshape(n_b, n_h, GRID_W, kh, NA_KW)
        return jnp.einsum('bhcij,bicjhd->bchd', p_nb, v_nb) + jnp.einsum('bhcn,bnhd->bchd', p[..., n_win:], v_ctx)

    out = lax.map(one_row, (row_idx, row_start, jnp.moveaxis(qg, 1, 0)))
    return jnp.moveaxis(out, 0, 1).reshape(n_b, n_tok, n_h, d_h)

def mlstm_chunked(q, k, v, log_i, log_f, state, with_out):
    n_b, n_h, n_t, _ = q.shape
    n_c = n_t // ML_CHUNK

    def chunks(t):
        return jnp.moveaxis(t.reshape(n_b, n_h, n_c, ML_CHUNK, *t.shape[3:]), 2, 0)

    tril = jnp.tril(jnp.ones((ML_CHUNK, ML_CHUNK), dtype=bool))

    def step(carry, inp):
        c_st, n_st, m_st = carry
        qc, kc, vc, ic, fc = inp
        b = jnp.cumsum(fc, axis=-1)
        log_d = jnp.where(tril, b[..., :, None] - b[..., None, :] + ic[..., None, :], -jnp.inf)
        log_inter = b + m_st[..., None]
        m_t = jnp.maximum(log_inter, jnp.max(log_d, axis=-1))
        m_new = m_t[..., -1]
        w_s = jnp.exp(b[..., -1:] - b + ic - m_new[..., None])
        decay = jnp.exp(b[..., -1] + m_st - m_new)
        c_new = decay[..., None, None] * c_st + jnp.einsum('bhs,bhsd,bhse->bhde', w_s, kc, vc)
        n_new = decay[..., None] * n_st + jnp.einsum('bhs,bhsd->bhd', w_s, kc)
        if not with_out:
            return (c_new, n_new, m_new), None
        d_mat = jnp.exp(log_d - m_t[..., None])
        w_inter = jnp.exp(log_inter - m_t)
        s = jnp.einsum('bhtd,bhsd->bhts', qc, kc) * d_mat
        num = jnp.einsum('bhts,bhse->bhte', s, vc) + w_inter[..., None] * jnp.einsum('bhtd,bhde->bhte', qc, c_st)
        den = jnp.sum(s, axis=-1) + w_inter * jnp.einsum('bhtd,bhd->bht', qc, n_st)
        h = num / jnp.maximum(jnp.abs(den), jnp.exp(-m_t))[..., None]
        return (c_new, n_new, m_new), h

    state, hs = lax.scan(step, state, tuple(chunks(t) for t in (q, k, v, log_i, log_f)))
    if not with_out:
        return None, state
    return jnp.moveaxis(hs, 0, 2).reshape(n_b, n_h, n_t, -1), state

def mlstm_bidir(q_l, k_l, v_l, g_l, q_c, k_c, v_c, g_c, need_ctx):
    def heads_first(t):
        return jnp.swapaxes(t, 1, 2).astype(jnp.float32)

    def gates(g):
        g = ML_GATE_CAP * jnp.tanh(g.astype(jnp.float32) / ML_GATE_CAP)
        i_f, f_f, i_b, f_b = jnp.split(jnp.swapaxes(g, 1, 2), 4, axis=1)
        return i_f, jax.nn.log_sigmoid(f_f), i_b, jax.nn.log_sigmoid(f_b)

    def flip(t):
        return jnp.flip(t, axis=2)

    n_b = q_l.shape[0]
    zero = (jnp.zeros((n_b, ML_HEADS, ML_HEAD_DIM, ML_HEAD_DIM), jnp.float32),
            jnp.zeros((n_b, ML_HEADS, ML_HEAD_DIM), jnp.float32),
            jnp.zeros((n_b, ML_HEADS), jnp.float32))
    qc, kc, vc = heads_first(q_c), heads_first(k_c), heads_first(v_c)
    if_c, lf_c, ib_c, lb_c = gates(g_c)
    hc_f, st_f = mlstm_chunked(qc, kc, vc, if_c, lf_c, zero, need_ctx)
    hc_b, st_b = mlstm_chunked(flip(qc), flip(kc), flip(vc), flip(ib_c), flip(lb_c), zero, need_ctx)
    ql, kl, vl = heads_first(q_l), heads_first(k_l), heads_first(v_l)
    if_l, lf_l, ib_l, lb_l = gates(g_l)
    hl_f, _ = mlstm_chunked(ql, kl, vl, if_l, lf_l, st_f, True)
    hl_b, _ = mlstm_chunked(flip(ql), flip(kl), flip(vl), flip(ib_l), flip(lb_l), st_b, True)
    h_lat = jnp.swapaxes(hl_f + flip(hl_b), 1, 2)
    h_ctx = jnp.swapaxes(hc_f + flip(hc_b), 1, 2) if need_ctx else None
    return h_lat, h_ctx

def ab_mixer(h_l, h_c, w_in, gate_b, q_norm, k_norm, rpb, head_norm, w_out, ang_r, ang_c, need_ctx):
    splits = [NA_WIDTH, 2 * NA_WIDTH, 3 * NA_WIDTH, 3 * NA_WIDTH + ML_WIDTH, 3 * NA_WIDTH + 2 * ML_WIDTH,
              3 * NA_WIDTH + 3 * ML_WIDTH, 3 * NA_WIDTH + 4 * ML_WIDTH]

    def project(h):
        qa, ka, va, qb, kb, vb, ob, g = jnp.split(h @ w_in, splits, axis=-1)
        qa = rms_norm(split_heads(qa, NA_HEADS, NA_HEAD_DIM)) * q_norm
        ka = rms_norm(split_heads(ka, NA_HEADS, NA_HEAD_DIM)) * k_norm
        va = split_heads(va, NA_HEADS, NA_HEAD_DIM)
        qb = split_heads(qb, ML_HEADS, ML_HEAD_DIM)
        kb = split_heads(kb, ML_HEADS, ML_HEAD_DIM) * (ML_HEAD_DIM ** -0.5)
        vb = split_heads(vb, ML_HEADS, ML_HEAD_DIM)
        return qa, ka, va, qb, kb, vb, ob, g + gate_b

    qa_l, ka_l, va_l, qb_l, kb_l, vb_l, ob_l, g_l = project(h_l)
    qa_c, ka_c, va_c, qb_c, kb_c, vb_c, ob_c, g_c = project(h_c)
    qb_l = axial_rope(qb_l, ang_r, ang_c)
    kb_l = axial_rope(kb_l, ang_r, ang_c)
    na_l = neighbourhood_attention(qa_l, ka_l, va_l, ka_c, va_c, rpb)
    ml_l, ml_c = mlstm_bidir(qb_l, kb_l, vb_l, g_l, qb_c, kb_c, vb_c, g_c, need_ctx)

    def merge(na, ml, o):
        ml = (rms_norm(ml) * head_norm).astype(o.dtype) * jax.nn.sigmoid(split_heads(o, ML_HEADS, ML_HEAD_DIM))
        cat = jnp.concatenate([na.reshape(*na.shape[:2], NA_WIDTH), ml.reshape(*ml.shape[:2], ML_WIDTH)], axis=-1)
        return cat @ w_out

    out_l = merge(na_l, ml_l, ob_l)
    out_c = merge(context_attention(qa_c, ka_c, va_c), ml_c, ob_c) if need_ctx else None
    return out_l, out_c

def centred_shift(x):
    xp = jnp.pad(x, ((0, 0), (1, 1), (0, 0)))
    return 0.5 * (xp[:, :-2] + xp[:, 2:])

def rwkv_prepare(h, mu, w_rkv, w0, w1, w2, a0, a1, a2, g1, g2, k_k, k_a):
    xx = centred_shift(h) - h
    xr, xw, xk, xv, xa, xg = h[None] + xx[None] * mu[:, None, None, :]
    r, k, v = jnp.einsum('sbtd,sde->sbte', jnp.stack([xr, xk, xv]), w_rkv)
    w_logit = w0[:, None, None, :] + jnp.einsum('zbtr,zrd->zbtd', jnp.tanh(jnp.einsum('btd,zdr->zbtr', xw, w1)), w2)
    decay = jnp.exp(-jnp.exp(-jax.nn.softplus(-w_logit.astype(jnp.float32)) - 0.5))
    a = jax.nn.sigmoid(a0[:, None, None, :] + jnp.einsum('zbtr,zrd->zbtd', jnp.einsum('btd,zdr->zbtr', xa, a1), a2))
    g = jax.nn.sigmoid(xg @ g1) @ g2
    kk = split_heads((k * k_k).astype(jnp.float32), RW_HEADS, RW_HEAD_DIM)
    kk = (kk / jnp.maximum(jnp.linalg.norm(kk, axis=-1, keepdims=True), 1e-12)).reshape(k.shape)
    k_dir = k[None] * (1.0 + (a - 1.0) * k_a)
    return r, k_dir, v, decay, -kk, kk[None] * a, g

def rwkv7_scan(r, w, k, v, a, b, state, reverse, with_out):
    def time_major(t):
        return jnp.moveaxis(split_heads(t.astype(jnp.float32), RW_HEADS, RW_HEAD_DIM), 1, 0)

    def step(s, inp):
        rt, wt, kt, vt, at, bt = inp
        sa = jnp.einsum('bhij,bhj->bhi', s, at)
        s = s * wt[:, :, None, :] + sa[..., None] * bt[:, :, None, :] + vt[..., None] * kt[:, :, None, :]
        y = jnp.einsum('bhij,bhj->bhi', s, rt) if with_out else None
        return s, y

    state, ys = lax.scan(step, state, tuple(time_major(t) for t in (r, w, k, v, a, b)), reverse=reverse)
    return (jnp.moveaxis(ys, 0, 1) if with_out else None), state

def rwkv_mixer(h_l, h_c, mu, w_rkv, w0, w1, w2, a0, a1, a2, g1, g2, k_k, k_a, r_k, lnx_w, lnx_b, w_o, need_ctx):
    lat = rwkv_prepare(h_l, mu, w_rkv, w0, w1, w2, a0, a1, a2, g1, g2, k_k, k_a)
    cxt = rwkv_prepare(h_c, mu, w_rkv, w0, w1, w2, a0, a1, a2, g1, g2, k_k, k_a)
    s0 = jnp.zeros((h_l.shape[0], RW_HEADS, RW_HEAD_DIM, RW_HEAD_DIM), jnp.float32)

    def bidir(p, s_f, s_b, with_out):
        r, k_dir, v, decay, a, b_dir, _ = p
        y_f, s_f = rwkv7_scan(r, decay[0], k_dir[0], v, a, b_dir[0], s_f, False, with_out)
        y_b, s_b = rwkv7_scan(r, decay[1], k_dir[1], v, a, b_dir[1], s_b, True, with_out)
        return y_f, y_b, s_f, s_b

    yc_f, yc_b, st_f, st_b = bidir(cxt, s0, s0, need_ctx)
    yl_f, yl_b, _, _ = bidir(lat, st_f, st_b, True)

    def readout(p, y_f, y_b):
        r, k_dir, v, _, _, _, g = p
        y = y_f + y_b
        mean = jnp.mean(y, axis=-1, keepdims=True)
        var = jnp.mean(jnp.square(y - mean), axis=-1, keepdims=True)
        y = ((y - mean) * lax.rsqrt(var + RW_GN_EPS)).reshape(r.shape) * lnx_w + lnx_b
        coef = jnp.sum(split_heads(r, RW_HEADS, RW_HEAD_DIM)[None] * split_heads(k_dir, RW_HEADS, RW_HEAD_DIM)
                       * split_heads(r_k, RW_HEADS, RW_HEAD_DIM), axis=(0, -1))[..., None]
        bonus = (coef * split_heads(v, RW_HEADS, RW_HEAD_DIM)).reshape(r.shape)
        return ((y + bonus) * g).astype(h_l.dtype) @ w_o

    out_l = readout(lat, yl_f, yl_b)
    out_c = readout(cxt, yc_f, yc_b) if need_ctx else None
    return out_l, out_c

def first_inputs(seed: int = 0) -> dict:
    key = jax.random.key(seed)
    keys = iter(jax.random.split(key, 48))
    n_even = (DEPTH + 1) // 2
    n_odd = DEPTH // 2
    d = D_MODEL

    def normal(shape, scale):
        return scale * jax.random.normal(next(keys), shape, jnp.float32)

    def uniform(shape, lo, hi):
        return jax.random.uniform(next(keys), shape, jnp.float32, lo, hi)

    ab_gate_b = jnp.concatenate([normal((n_even, ML_HEADS), 0.1), uniform((n_even, ML_HEADS), 3.0, 6.0),
                                 normal((n_even, ML_HEADS), 0.1), uniform((n_even, ML_HEADS), 3.0, 6.0)], axis=-1)
    return {
        'x': normal((BATCH, SEQ, d), 1.0),
        'c': normal((BATCH, d), 1.0),
        'ctx': normal((BATCH, CTX_LEN, d), 1.0),
        'c_ctx': normal((d,), 1.0),
        'ada_w': normal((DEPTH, d, 6 * d), 0.5 * d ** -0.5),
        'ada_b': normal((DEPTH, 6 * d), 0.02),
        'ab_w_in': normal((n_even, d, AB_IN_WIDTH), d ** -0.5),
        'ab_gate_b': ab_gate_b,
        'na_q_norm': 1.0 + normal((n_even, NA_HEAD_DIM), 0.05),
        'na_k_norm': 1.0 + normal((n_even, NA_HEAD_DIM), 0.05),
        'na_rpb': normal((n_even, NA_HEADS, 2 * NA_KH - 1, 2 * NA_KW - 1), 0.1),
        'ml_head_norm': 1.0 + normal((n_even, ML_HEADS, ML_HEAD_DIM), 0.05),
        'ab_w_out': normal((n_even, d, d), d ** -0.5),
        'rw_mu': uniform((n_odd, 6, d), 0.0, 1.0),
        'rw_w_rkv': normal((n_odd, 3, d, d), d ** -0.5),
        'rw_w0': uniform((n_odd, 2, d), -6.0, -1.0),
        'rw_w1': normal((n_odd, 2, d, RW_DECAY_LORA), 0.1 * d ** -0.5),
        'rw_w2': normal((n_odd, 2, RW_DECAY_LORA, d), 0.1 * RW_DECAY_LORA ** -0.5),
        'rw_a0': normal((n_odd, 2, d), 0.1),
        'rw_a1': normal((n_odd, 2, d, RW_AAA_LORA), d ** -0.5),
        'rw_a2': normal((n_odd, 2, RW_AAA_LORA, d), 0.5 * RW_AAA_LORA ** -0.5),
        'rw_g1': normal((n_odd, d, RW_GATE_LORA), d ** -0.5),
        'rw_g2': normal((n_odd, RW_GATE_LORA, d), RW_GATE_LORA ** -0.5),
        'rw_k_k': 0.85 + normal((n_odd, d), 0.05),
        'rw_k_a': 1.0 + normal((n_odd, d), 0.05),
        'rw_r_k': normal((n_odd, d), 0.1),
        'rw_lnx_w': 1.0 + normal((n_odd, d), 0.05),
        'rw_lnx_b': normal((n_odd, d), 0.02),
        'rw_w_o': normal((n_odd, d, d), d ** -0.5),
        'mlp_w1': normal((DEPTH, d, D_FF), d ** -0.5),
        'mlp_w2': normal((DEPTH, D_FF, d), D_FF ** -0.5),
    }

def first_block(x, c, ctx, c_ctx, ada_w, ada_b, ab_w_in, ab_gate_b, na_q_norm, na_k_norm, na_rpb, ml_head_norm,
              ab_w_out, rw_mu, rw_w_rkv, rw_w0, rw_w1, rw_w2, rw_a0, rw_a1, rw_a2, rw_g1, rw_g2, rw_k_k, rw_k_a,
              rw_r_k, rw_lnx_w, rw_lnx_b, rw_w_o, mlp_w1, mlp_w2):
    ang_r, ang_c = axial_rope_angles(x.shape[1], ML_HEAD_DIM)
    for layer in range(DEPTH):
        need_ctx = layer < DEPTH - 1
        j = layer // 2
        sh_a, sc_a, gt_a, sh_m, sc_m, gt_m = adaln(c[:, None, :], ada_w[layer], ada_b[layer])
        csh_a, csc_a, cgt_a, csh_m, csc_m, cgt_m = adaln(c_ctx, ada_w[layer], ada_b[layer])
        h_l = modulate(x, sh_a, sc_a)
        h_c = modulate(ctx, csh_a, csc_a)
        if layer % 2 == 0:
            o_l, o_c = ab_mixer(h_l, h_c, ab_w_in[j], ab_gate_b[j], na_q_norm[j], na_k_norm[j], na_rpb[j],
                                ml_head_norm[j], ab_w_out[j], ang_r, ang_c, need_ctx)
        else:
            o_l, o_c = rwkv_mixer(h_l, h_c, rw_mu[j], rw_w_rkv[j], rw_w0[j], rw_w1[j], rw_w2[j], rw_a0[j],
                                  rw_a1[j], rw_a2[j], rw_g1[j], rw_g2[j], rw_k_k[j], rw_k_a[j], rw_r_k[j],
                                  rw_lnx_w[j], rw_lnx_b[j], rw_w_o[j], need_ctx)
        x = x + gt_a * o_l
        x = x + gt_m * squared_relu_mlp(modulate(x, sh_m, sc_m), mlp_w1[layer], mlp_w2[layer])
        if need_ctx:
            ctx = ctx + cgt_a * o_c
            ctx = ctx + cgt_m * squared_relu_mlp(modulate(ctx, csh_m, csc_m), mlp_w1[layer], mlp_w2[layer])
    return x


DEPTH_2 = 1

GLA_HEADS = 4
GLA_DK = 64
GLA_DV = 128
GLA_KEY = GLA_HEADS * GLA_DK
GLA_VAL = GLA_HEADS * GLA_DV
GLA_RANK = 16
GLA_CHUNK = 64
GATE_NORMALIZER = 16.0
POOL_WINDOWS = (2, 4, 8, 16)
POOL_GROUPS = 4
POOL_CH = 128
POOL_WIDTH = POOL_GROUPS * POOL_CH
N_BRANCHES = 2
N_EXPERTS = 16
D_EXPERT = 1024
EC_CAPACITY = 2
EPS = 1e-6
CTX_COLS = (GLA_KEY, GLA_VAL, GLA_RANK, GLA_RANK)
N_CTX_COLS = GLA_KEY + GLA_VAL + 2 * GLA_RANK
ALL_COLS = (N_CTX_COLS, GLA_KEY, GLA_VAL, POOL_WIDTH, N_BRANCHES * D_MODEL)
D_IN = N_CTX_COLS + GLA_KEY + GLA_VAL + POOL_WIDTH + N_BRANCHES * D_MODEL


def split_cols(u, sizes):
    points, acc = [], 0
    for s in sizes[:-1]:
        acc += s
        points.append(acc)
    return jnp.split(u, points, axis=-1)

def rms_norm_2(x, g):
    xf = x.astype(jnp.float32)
    y = xf * lax.rsqrt(jnp.mean(xf * xf, axis=-1, keepdims=True) + EPS)
    return (y * g.astype(jnp.float32)).astype(x.dtype)

def modulate_2(x, g, shift, scale):
    return rms_norm_2(x, g) * (1 + scale) + shift

def to_heads(u, d):
    b, l, _ = u.shape
    return u.reshape(b, l, GLA_HEADS, d).transpose(0, 2, 1, 3)

def chunked(u):
    b, h, l, d = u.shape
    return u.reshape(b, h, l // GLA_CHUNK, GLA_CHUNK, d)

def gla_scan(q, k, v, log_a, h0, with_output):
    kc = chunked(k.astype(jnp.float32))
    vc = chunked(v.astype(jnp.float32))
    b = jnp.cumsum(chunked(log_a.astype(jnp.float32)), axis=3)
    b_last = b[:, :, :, -1:, :]
    kv = jnp.einsum('bhncd,bhnce->bhnde', kc * jnp.exp(b_last - b), vc)
    decay = jnp.exp(b_last[:, :, :, 0, :])

    def step(state, inp):
        dec_n, kv_n = inp
        return dec_n[..., None] * state + kv_n, state

    final, starts = lax.scan(step, h0, (jnp.moveaxis(decay, 2, 0), jnp.moveaxis(kv, 2, 0)))
    if not with_output:
        return None, final
    starts = jnp.moveaxis(starts, 0, 2)
    qc = chunked(q.astype(jnp.float32))
    inter = jnp.einsum('bhncd,bhnde->bhnce', qc * jnp.exp(b), starts)
    mid = b[:, :, :, GLA_CHUNK // 2 - 1:GLA_CHUNK // 2, :]
    scores = jnp.einsum('bhnid,bhnjd->bhnij', qc * jnp.exp(b - mid), kc * jnp.exp(mid - b))
    lower = jnp.tril(jnp.ones((GLA_CHUNK, GLA_CHUNK), dtype=bool))
    intra = jnp.einsum('bhnij,bhnje->bhnie', jnp.where(lower, scores, 0.0), vc)
    bsz, h, n, cl, dv = intra.shape
    return (inter + intra).reshape(bsz, h, n * cl, dv), final

def gla_bidirectional(q, k, v, la_f, la_b, h0_f, h0_b, with_output):
    rev = lambda u: jnp.flip(u, axis=2)
    o_f, h_f = gla_scan(q, k, v, la_f, h0_f, with_output)
    q_rev = rev(q) if with_output else None
    o_b, h_b = gla_scan(q_rev, rev(k), rev(v), rev(la_b), h0_b, with_output)
    if not with_output:
        return None, h_f, h_b
    return o_f + rev(o_b), h_f, h_b

def kv_and_decay(proj_kvd, w_decay_up, b_decay):
    k, v, r_f, r_b = split_cols(proj_kvd, CTX_COLS)
    la_f = jax.nn.log_sigmoid((r_f @ w_decay_up[0] + b_decay[0]).astype(jnp.float32)) / GATE_NORMALIZER
    la_b = jax.nn.log_sigmoid((r_b @ w_decay_up[1] + b_decay[1]).astype(jnp.float32)) / GATE_NORMALIZER
    return to_heads(k, GLA_DK), to_heads(v, GLA_DV), to_heads(la_f, GLA_DK), to_heads(la_b, GLA_DK)

def context_states(ctx, g1, shift, scale, w_in, w_decay_up, b_decay):
    h = modulate_2(ctx, g1, shift, scale)
    k, v, la_f, la_b = kv_and_decay(h @ w_in[:, :N_CTX_COLS], w_decay_up, b_decay)
    zero = jnp.zeros((ctx.shape[0], GLA_HEADS, GLA_DK, GLA_DV), jnp.float32)
    _, h_f, h_b = gla_bidirectional(None, k, v, la_f, la_b, zero, zero, False)
    return h_f, h_b

def box_sum(u, w, axis):
    n = u.shape[axis]
    pad = [(0, 0)] * u.ndim
    pad[axis] = (1, 0)
    cs = jnp.pad(jnp.cumsum(u, axis=axis), pad)
    pos = jnp.arange(n)
    lo = jnp.clip(pos - w // 2, 0, n)
    hi = jnp.clip(pos + w // 2, 0, n)
    s = jnp.take(cs, hi, axis=axis) - jnp.take(cs, lo, axis=axis)
    return s, (hi - lo).astype(jnp.float32)

def pool_latent(u):
    bsz, l, _ = u.shape
    rows = l // GRID_W
    ug = u.astype(jnp.float32).reshape(bsz, rows, GRID_W, POOL_GROUPS, POOL_CH)
    outs = []
    for gi, w in enumerate(POOL_WINDOWS):
        ugi = ug[:, :, :, gi, :]
        s, cnt_c = box_sum(ugi, w, 2)
        s, cnt_r = box_sum(s, w, 1)
        outs.append(s / (cnt_r[:, None] * cnt_c[None, :])[None, :, :, None] - ugi)
    return jnp.stack(outs, axis=3).reshape(bsz, l, POOL_GROUPS, POOL_CH)

def pool_context(u):
    bsz, l, _ = u.shape
    ug = u.astype(jnp.float32).reshape(bsz, l, POOL_GROUPS, POOL_CH)
    outs = []
    for gi, w in enumerate(POOL_WINDOWS):
        ugi = ug[:, :, gi, :]
        s, cnt = box_sum(ugi, w, 1)
        outs.append(s / cnt[None, :, None] - ugi)
    return jnp.stack(outs, axis=2)

def mixer_sublayer(xs, g1, shift, scale, gate, h0_f, h0_b, pool_fn, w_in, w_decay_up, b_decay,
                   gla_norm_g, w_gla_proj, pool_w, pool_scale, w_pool_proj, w_out):
    bsz, l, _ = xs.shape
    h = modulate_2(xs, g1, shift, scale)
    proj_kvd, q, g, pool_in, merge = split_cols(h @ w_in, ALL_COLS)
    k, v, la_f, la_b = kv_and_decay(proj_kvd, w_decay_up, b_decay)
    q = to_heads(q, GLA_DK) * (GLA_DK ** -0.5)
    o, h_f, h_b = gla_bidirectional(q, k, v, la_f, la_b, h0_f, h0_b, True)
    o = rms_norm_2(o, gla_norm_g).transpose(0, 2, 1, 3).reshape(bsz, l, GLA_VAL).astype(xs.dtype)
    branch_gla = (o * jax.nn.silu(g)) @ w_gla_proj
    pooled = pool_fn(pool_in)
    mixed = jnp.einsum('blgc,gcd->blgd', pooled, pool_w.astype(jnp.float32)).reshape(bsz, l, POOL_WIDTH)
    branch_pool = (mixed * pool_scale.astype(jnp.float32)).astype(xs.dtype) @ w_pool_proj
    gate_gla, gate_pool = split_cols(jax.nn.sigmoid(merge), (D_MODEL, D_MODEL))
    y = (gate_gla * branch_gla + gate_pool * branch_pool) @ w_out
    return xs + gate * y, h_f, h_b

def ec_moe(h, w_router, w_gate_e, w_up_e, w_down_e):
    l = h.shape[1]
    cap = EC_CAPACITY * l // N_EXPERTS
    aff = jax.nn.softmax((h @ w_router).astype(jnp.float32), axis=-1)
    top_aff, top_idx = lax.top_k(jnp.swapaxes(aff, 1, 2), cap)

    def per_set(hs, idx, wgt):
        xs = hs[idx]
        a = jax.nn.silu(jnp.einsum('ecd,edf->ecf', xs, w_gate_e)) * jnp.einsum('ecd,edf->ecf', xs, w_up_e)
        y = jnp.einsum('ecf,efd->ecd', a, w_down_e) * wgt[..., None].astype(hs.dtype)
        return jnp.zeros_like(hs).at[idx.reshape(-1)].add(y.reshape(-1, hs.shape[-1]))

    return jax.vmap(per_set)(h, top_idx, top_aff)

def ffn_sublayer(xs, g2, shift, scale, gate, w_router, w_gate_e, w_up_e, w_down_e):
    return xs + gate * ec_moe(modulate_2(xs, g2, shift, scale), w_router, w_gate_e, w_up_e, w_down_e)

def second_inputs(seed: int = 0) -> dict:
    key = jax.random.key(seed)
    ks = jax.random.split(key, 24)
    nrm = lambda k, shape, s: jax.random.normal(k, shape, jnp.float32) * s
    return {
        'x': nrm(ks[0], (BATCH, SEQ, D_MODEL), 1.0),
        'c': nrm(ks[1], (BATCH, D_MODEL), 1.0),
        'ctx': nrm(ks[2], (BATCH, CTX_LEN, D_MODEL), 1.0),
        'c_ctx': nrm(ks[3], (D_MODEL,), 1.0),
        'ada_w': nrm(ks[4], (DEPTH_2, D_MODEL, 6 * D_MODEL), 0.5 * D_MODEL ** -0.5),
        'ada_b': nrm(ks[5], (DEPTH_2, 6 * D_MODEL), 0.02),
        'norm1_g': 1.0 + nrm(ks[6], (DEPTH_2, D_MODEL), 0.02),
        'norm2_g': 1.0 + nrm(ks[7], (DEPTH_2, D_MODEL), 0.02),
        'w_in': nrm(ks[8], (DEPTH_2, D_MODEL, D_IN), D_MODEL ** -0.5),
        'w_decay_up': nrm(ks[9], (DEPTH_2, 2, GLA_RANK, GLA_KEY), GLA_RANK ** -0.5),
        'b_decay': nrm(ks[10], (DEPTH_2, 2, GLA_KEY), 0.1),
        'gla_norm_g': 1.0 + nrm(ks[11], (DEPTH_2, GLA_DV), 0.02),
        'w_gla_proj': nrm(ks[12], (DEPTH_2, GLA_VAL, D_MODEL), GLA_VAL ** -0.5),
        'pool_w': nrm(ks[13], (DEPTH_2, POOL_GROUPS, POOL_CH, POOL_CH), POOL_CH ** -0.5),
        'pool_scale': 1.0 + nrm(ks[14], (DEPTH_2, POOL_WIDTH), 0.1),
        'w_pool_proj': nrm(ks[15], (DEPTH_2, POOL_WIDTH, D_MODEL), POOL_WIDTH ** -0.5),
        'w_out': nrm(ks[16], (DEPTH_2, D_MODEL, D_MODEL), D_MODEL ** -0.5),
        'w_router': nrm(ks[17], (DEPTH_2, D_MODEL, N_EXPERTS), D_MODEL ** -0.5),
        'w_gate_e': nrm(ks[18], (DEPTH_2, N_EXPERTS, D_MODEL, D_EXPERT), D_MODEL ** -0.5),
        'w_up_e': nrm(ks[19], (DEPTH_2, N_EXPERTS, D_MODEL, D_EXPERT), D_MODEL ** -0.5),
        'w_down_e': nrm(ks[20], (DEPTH_2, N_EXPERTS, D_EXPERT, D_MODEL), D_EXPERT ** -0.5),
        'final_norm_g': 1.0 + nrm(ks[21], (D_MODEL,), 0.02),
    }

def second_block(x, c, ctx, c_ctx, ada_w, ada_b, norm1_g, norm2_g, w_in, w_decay_up, b_decay,
              gla_norm_g, w_gla_proj, pool_w, pool_scale, w_pool_proj, w_out, w_router,
              w_gate_e, w_up_e, w_down_e, final_norm_g):
    zero_state = jnp.zeros((ctx.shape[0], GLA_HEADS, GLA_DK, GLA_DV), jnp.float32)
    for i in range(DEPTH_2):
        sh1, sc1, gt1, sh2, sc2, gt2 = jnp.split((jax.nn.silu(c) @ ada_w[i] + ada_b[i])[:, None, :], 6, axis=-1)
        csh1, csc1, cgt1, csh2, csc2, cgt2 = jnp.split(jax.nn.silu(c_ctx) @ ada_w[i] + ada_b[i], 6, axis=-1)
        mix_w = (w_in[i], w_decay_up[i], b_decay[i], gla_norm_g[i], w_gla_proj[i],
                 pool_w[i], pool_scale[i], w_pool_proj[i], w_out[i])
        moe_w = (w_router[i], w_gate_e[i], w_up_e[i], w_down_e[i])
        if i == DEPTH_2 - 1:
            h_f, h_b = context_states(ctx, norm1_g[i], csh1, csc1, w_in[i], w_decay_up[i], b_decay[i])
        else:
            ctx_mixed, h_f, h_b = mixer_sublayer(ctx, norm1_g[i], csh1, csc1, cgt1, zero_state, zero_state,
                                                 pool_context, *mix_w)
            ctx = ffn_sublayer(ctx_mixed, norm2_g[i], csh2, csc2, cgt2, *moe_w)
        x, _, _ = mixer_sublayer(x, norm1_g[i], sh1, sc1, gt1, h_f, h_b, pool_latent, *mix_w)
        x = ffn_sublayer(x, norm2_g[i], sh2, sc2, gt2, *moe_w)
    return rms_norm_2(x, final_norm_g)


def setup_inputs(seed=0):
    out = dict(first_inputs(seed))
    for name, value in second_inputs(seed + 1).items():
        if name != "x":
            out[name + "_2"] = value
    return out


def reference(
    x, c, ctx, c_ctx, ada_w, ada_b, ab_w_in, ab_gate_b, na_q_norm, na_k_norm, na_rpb,
    ml_head_norm, ab_w_out, rw_mu, rw_w_rkv, rw_w0, rw_w1, rw_w2, rw_a0, rw_a1, rw_a2, rw_g1,
    rw_g2, rw_k_k, rw_k_a, rw_r_k, rw_lnx_w, rw_lnx_b, rw_w_o, mlp_w1, mlp_w2, c_2, ctx_2,
    c_ctx_2, ada_w_2, ada_b_2, norm1_g_2, norm2_g_2, w_in_2, w_decay_up_2, b_decay_2,
    gla_norm_g_2, w_gla_proj_2, pool_w_2, pool_scale_2, w_pool_proj_2, w_out_2, w_router_2,
    w_gate_e_2, w_up_e_2, w_down_e_2, final_norm_g_2,
):
    x = first_block(
        x, c, ctx, c_ctx, ada_w, ada_b, ab_w_in, ab_gate_b, na_q_norm, na_k_norm, na_rpb,
        ml_head_norm, ab_w_out, rw_mu, rw_w_rkv, rw_w0, rw_w1, rw_w2, rw_a0, rw_a1, rw_a2,
        rw_g1, rw_g2, rw_k_k, rw_k_a, rw_r_k, rw_lnx_w, rw_lnx_b, rw_w_o, mlp_w1, mlp_w2,
    )
    return second_block(
        x, c_2, ctx_2, c_ctx_2, ada_w_2, ada_b_2, norm1_g_2, norm2_g_2, w_in_2, w_decay_up_2,
        b_decay_2, gla_norm_g_2, w_gla_proj_2, pool_w_2, pool_scale_2, w_pool_proj_2, w_out_2,
        w_router_2, w_gate_e_2, w_up_e_2, w_down_e_2, final_norm_g_2,
    )


_drawn_inputs = setup_inputs


def setup_inputs(seed=0):
    import zlib

    import numpy as np

    out = dict(_drawn_inputs(seed))
    spreads = {}
    factors = {'na_q_norm': 8.0,
     'na_k_norm': 8.0,
     'na_rpb': 8.0,
     'ml_head_norm': 8.0,
     'rw_w1': 8.0,
     'rw_w2': 8.0,
     'rw_a0': 7.735,
     'rw_lnx_w': 6.684,
     'rw_lnx_b': 8.0,
     'ctx_2': 5.042,
     'c_ctx_2': 6.586,
     'ada_b_2': 3.948,
     'norm1_g_2': 8.0,
     'norm2_g_2': 8.0,
     'b_decay_2': 8.0,
     'gla_norm_g_2': 8.0,
     'pool_scale_2': 3.976,
     'final_norm_g_2': 2.858}
    for name, (base, spread) in spreads.items():
        noise = np.random.default_rng([zlib.crc32(name.encode()), seed]).standard_normal(out[name].shape)
        drawn = base * np.exp(spread * noise) if base else spread * noise
        out[name] = jnp.asarray(drawn.astype(out[name].dtype))
    for name, factor in factors.items():
        out[name] = (out[name] * factor).astype(out[name].dtype)
    return out
```

```python
from contextlib import ExitStack

import numpy as np
import concourse.bass as bass
from concourse import mybir

F32 = mybir.dt.float32
ALU = mybir.AluOpType
ACT = mybir.ActivationFunctionType
AX = mybir.AxisListType
MUL, ADD, SUB, MAX, MIN = ALU.mult, ALU.add, ALU.subtract, ALU.max, ALU.min
EQ, GE, GT = ALU.is_equal, ALU.is_ge, ALU.is_gt
NR = 3
NEG = -1.0e30


class Queue:

    def __init__(self, sem, chained):
        self.sem, self.n, self.items, self.seen, self.chained = sem, 0, [], {}, chained

    def wait(self, *tokens):
        for t in tokens:
            if isinstance(t, list):
                self.wait(*t)
            elif t is not None and self.seen.get(id(t[0]), 0) < t[1]:
                self.seen[id(t[0])] = t[1]
                self.items.append((t[0], t[1]))

    def add(self, fn, *tokens, inc=True, free=False):
        self.wait(*tokens)
        if self.chained and self.n and not free:
            self.wait((self.sem, self.n))
        if inc:
            self.n += 1
        self.items.append((fn, inc))
        return (self.sem, self.n) if inc else None

    def last(self):
        return (self.sem, self.n) if self.n else None

    def play(self, e):
        for a, b in self.items:
            if callable(a):
                i = a(e)
                if b is True:
                    i.then_inc(self.sem, 1)
            else:
                e.wait_ge(a, b)


class Vec(Queue):
    def tt(self, o, a, b, op, *w, **k):
        return self.add(lambda e: e.tensor_tensor(o, a, b, op), *w, **k)

    def ts(self, o, a, s1, s2, op0, op1, *w, **k):
        if s2 is None:
            return self.add(lambda e: e.tensor_scalar(o, a, s1, None, op0), *w, **k)
        return self.add(lambda e: e.tensor_scalar(o, a, s1, s2, op0, op1), *w, **k)

    def stt(self, o, a, s, b, op0, op1, *w, **k):
        return self.add(lambda e: e.scalar_tensor_tensor(out=o, in0=a, scalar=s, in1=b, op0=op0, op1=op1), *w, **k)

    def cp(self, o, a, *w, **k):
        return self.add(lambda e: e.tensor_copy(o, a), *w, **k)

    def rec(self, o, a, *w, **k):
        return self.add(lambda e: e.reciprocal(o, a), *w, **k)

    def red(self, o, a, op, *w, neg=False, **k):
        return self.add(lambda e: e.tensor_reduce(o, a, AX.X, op, negate=neg), *w, **k)

    def scan(self, o, a, b, *w, **k):
        return self.add(lambda e: e.tensor_tensor_scan(o, a, b, 0.0, MUL, ADD), *w, **k)

    def set(self, o, v, *w, **k):
        return self.add(lambda e: e.memset(o, v), *w, **k)


class Act(Queue):
    def f(self, o, a, fn, *w, bias=0.0, scale=1.0, acc=None, **k):
        if acc is not None:
            return self.add(lambda e: e.activation(o, a, fn, bias=bias, scale=scale, accum_out=acc), *w, **k)
        return self.add(lambda e: e.activation(o, a, fn, bias=bias, scale=scale), *w, **k)

    def cp(self, o, a, *w, **k):
        return self.add(lambda e: e.activation(o, a, ACT.Copy), *w, **k)


class Ten(Queue):
    def mm(self, o, l, r, start, stop, *w, inc=False):
        return self.add(lambda e: e.matmul(o, l, r, start=start, stop=stop), *w, inc=inc)

    def mmx(self, o, l, r, start, stop, *w, inc=False):
        return self.add(lambda e: e.matmul(o, l, r, start=start, stop=stop, skip_group_check=True), *w, inc=inc)

    def tr(self, o, a, ident, *w, inc=False):
        return self.add(lambda e: e.transpose(o, a, ident), *w, inc=inc)


class Ring:

    def __init__(self, bufs):
        self.bufs, self.free, self.i = bufs, [[] for _ in bufs], 0

    def get(self):
        i = self.i % len(self.bufs)
        self.i += 1
        w, self.free[i] = self.free[i], None
        if w is None:
            raise RuntimeError("a buffer is taken again before its readers are known")
        return i, self.bufs[i], w

    def done(self, i, *tokens):
        self.free[i] = [t for t in tokens if t is not None]


def layout_constants():
    cols, at = [], {}

    def put(name, a):
        a = np.asarray(a, np.float32).reshape(128, -1)
        at[name] = (sum(c.shape[1] for c in cols), a.shape[1])
        cols.append(a)

    i = np.arange(128)
    ident = np.eye(128)
    put("ident", ident)
    put("ones", np.ones((128, 128)))
    put("blk", (i[:, None] // 64 == i[None, :] // 64))
    le = (i[:, None] <= i[None, :]).astype(np.float32)
    put("le", le)
    put("ge", le.T)
    put("lt", le - ident)
    put("gt", le.T - ident)
    put("mle", np.where(le > 0, 0.0, NEG))
    put("mge", np.where(le.T > 0, 0.0, NEG))
    c = i % 64
    st = np.clip(c - 8, 0, 48)[:, None]
    j = np.arange(64)[None, :]
    put("nam", np.where((j >= st) & (j < st + 16), 0.0, NEG))
    b16 = (i[:, None] // 16 == i[None, :] // 16)
    b32 = (i[:, None] // 32 == i[None, :] // 32)
    b64 = (i[:, None] // 64 == i[None, :] // 64)
    up = le - ident
    dn = up.T
    for n, m in (("0", b16), ("1", b32 & ~b16), ("2", b64 & ~b32), ("3", ~b64)):
        put("u" + n, up * m)
        put("d" + n, dn * m)
    put("le64", le * b64)
    put("ge64", le.T * b64)
    tok = np.arange(512)
    inv = 10000.0 ** (-np.arange(32, dtype=np.float32) / 32)
    ang = np.stack([(tok // 64)[:, None] * inv, (tok % 64)[:, None] * inv], 1)
    rope = np.stack([np.cos(ang), np.sin(ang)], 1).astype(np.float32)
    put("rope", rope.reshape(4, 128, 2 * 2 * 32).transpose(1, 0, 2))
    t = np.arange(768)
    put("r128", np.broadcast_to(t % 128 != 0, (128, 768)))
    put("r64", np.broadcast_to(t % 64 != 0, (128, 768)))
    cnt = []
    for w in (2, 4, 8, 16):
        q = np.arange(64)
        cc = np.clip(q + w // 2, 0, 64) - np.clip(q - w // 2, 0, 64)
        q = np.arange(8)
        cr = np.clip(q + w // 2, 0, 8) - np.clip(q - w // 2, 0, 8)
        cnt.append(1.0 / (cr[:, None] * cc[None, :]))
    put("cnt", np.broadcast_to(np.stack(cnt).reshape(1, -1), (128, 2048)))
    put("iota64", np.broadcast_to(np.arange(64), (128, 64)))
    put("slot", np.stack([i % 64, i % 64], 1))
    e2 = np.zeros((128, 8, 128))
    for p in range(8):
        for q in range(128):
            e2[2 * p + q // 64, p, q] = 1
    put("e2", e2)
    return np.concatenate(cols, 1).astype(np.float32), at


def column(v, n):
    return np.ascontiguousarray(np.asarray(v).reshape(n, 128).T)


def layout_inputs(a):
    A = {k: np.asarray(v) for k, v in a.items()}
    o = {}
    o["xT"] = np.ascontiguousarray(A["x"][0].T)
    o["ctxT"] = np.ascontiguousarray(A["ctx"][0].T)
    o["ctx2T"] = np.ascontiguousarray(A["ctx_2"][0].T)
    o["cc"] = np.stack([column(A["c"][0], 8), column(A["c_ctx"], 8),
                        column(A["c_2"][0], 8), column(A["c_ctx_2"], 8)], 2)
    o["ada_w"] = A["ada_w"]
    o["ada_w_2"] = A["ada_w_2"]
    o["ada_b"] = np.concatenate([column(A["ada_b"][0], 48), column(A["ada_b"][1], 48),
                                 column(A["ada_b_2"][0], 48)], 1)
    o["ab_w_in"] = A["ab_w_in"][0]
    o["ab_w_out"] = A["ab_w_out"][0]
    o["gate_b"] = np.broadcast_to(A["ab_gate_b"][0][None], (128, 16))
    o["qkn"] = np.stack([np.tile(A["na_q_norm"][0], 2), np.tile(A["na_k_norm"][0], 2)], 1)
    rp = np.pad(A["na_rpb"][0], ((0, 0), (0, 0), (64, 64)))
    wide = np.stack([rp[:, :, 79 - c:143 - c] for c in range(64)], 1)
    o["rpb"] = np.concatenate([wide[:, :, 1:15], wide[:, :, 0:14]], 1)
    o["hn"] = np.ascontiguousarray(A["ml_head_norm"][0].T)
    o["mu"] = np.concatenate([column(A["rw_mu"][0, s], 8) for s in range(6)], 1)
    o["rkv"] = A["rw_w_rkv"][0]
    o["w0a0"] = np.concatenate([column(A["rw_w0"][0, 0], 8), column(A["rw_w0"][0, 1], 8),
                                column(A["rw_a0"][0, 0], 8), column(A["rw_a0"][0, 1], 8)], 1)
    o["w1"] = A["rw_w1"][0]
    o["w2"] = A["rw_w2"][0].reshape(128, 1024)
    o["a1"] = A["rw_a1"][0]
    o["a2"] = A["rw_a2"][0].reshape(128, 1024)
    o["g1"] = A["rw_g1"][0]
    o["g2"] = A["rw_g2"][0]
    o["rwv"] = np.concatenate([column(A[n][0], 8) for n in
                               ("rw_k_k", "rw_k_a", "rw_r_k", "rw_lnx_w", "rw_lnx_b")], 1)
    o["w_o"] = A["rw_w_o"][0]
    o["mlp_w1"] = A["mlp_w1"]
    o["mlp_w2"] = A["mlp_w2"]
    o["n2"] = np.concatenate([column(A["norm1_g_2"][0], 8), column(A["norm2_g_2"][0], 8),
                              column(A["final_norm_g_2"], 8), column(A["gla_norm_g_2"][0], 1),
                              column(A["pool_scale_2"][0], 4), column(A["b_decay_2"][0, 0], 2),
                              column(A["b_decay_2"][0, 1], 2)], 1)
    o["w_in_2"] = A["w_in_2"][0]
    o["dup"] = A["w_decay_up_2"][0]
    o["w_gla"] = A["w_gla_proj_2"][0]
    o["pool_w"] = A["pool_w_2"][0]
    o["w_poolp"] = A["w_pool_proj_2"][0]
    o["w_out_2"] = A["w_out_2"][0]
    o["router"] = A["w_router_2"][0]
    o["wg"] = A["w_gate_e_2"][0]
    o["wu"] = A["w_up_e_2"][0]
    o["wd"] = A["w_down_e_2"][0]
    o["consts"] = layout_constants()[0]
    return {k: np.ascontiguousarray(v) for k, v in o.items()}


class Program:
    def __init__(self, nc, D, stages, out):
        self.nc, self.D, self.out = nc, D, out
        self.stages = stages

    def build(self):
        nc = self.nc
        with ExitStack() as ctx:
            self.ctx = ctx
            total = 53200
            self.arena = ctx.enter_context(nc.sbuf_tensor("arena", [128, total], F32))
            self.top, self.size, self.peak, self.starts = 0, total, 0, []
            self.psum = [ctx.enter_context(nc.psum_tensor(f"ps{i}", [128, 512], F32)) for i in range(8)]
            s = {n: ctx.enter_context(nc.semaphore("s_" + n)) for n in ("pe", "dve", "act", "pool", "sp")}
            self.T = Ten(s["pe"], False)
            self.V = Vec(s["dve"], True)
            self.S = Act(s["act"], True)
            self.G = Vec(s["pool"], True)
            self.Q = Queue(s["sp"], False)
            self.ps = Ring([p[:, :] for p in self.psum])
            self.w_at = self.top
            self.wslots = [self.alloc(4096) for _ in range(NR)]
            self.wsem = [ctx.enter_context(nc.semaphore(f"s_w{i}")) for i in range(NR)]
            self.wcount = [0] * NR
            self.wring = Ring(self.wslots)
            self.lsem = [ctx.enter_context(nc.semaphore(f"s_l{i}")) for i in range(24)]
            self.lcount = [0] * 24
            self.li = 0
            self.body()
            block = ctx.enter_context(nc.Block())
            for q, on in ((self.Q, block.sync), (self.T, block.tensor), (self.V, block.vector),
                          (self.S, block.scalar), (self.G, block.gpsimd)):
                on(self.player(q))

    @staticmethod
    def player(q):
        def play(e):
            q.play(e)
        return play

    def alloc(self, *shape):
        n = int(np.prod(shape))
        o = self.top
        self.top += n + n % 2
        self.peak = max(self.peak, self.top)
        if self.top > self.size:
            raise RuntimeError(f"SBUF: {self.top} columns of {self.size}")
        v = self.arena[:, o:o + n]
        if len(shape) == 2:
            v = v.rearrange("p (a b) -> p a b", a=shape[0])
        if len(shape) == 3:
            v = v.rearrange("p (a b c) -> p a b c", a=shape[0], b=shape[1])
        self.starts.append((o, v))
        return v

    def sbring(self, n, *shape):
        return Ring([self.alloc(*shape) for _ in range(n)])

    def fence(self):
        t = [q.last() for q in (self.T, self.V, self.S, self.G)]
        t += [(s, c) for s, c in zip(self.lsem, self.lcount) if c]
        for q in (self.T, self.V, self.S, self.G, self.Q):
            q.wait(t)
        return t

    def load(self, dst, src, *w, q=None):
        i = self.li % len(self.lsem)
        self.li += 1
        q = q or self.Q
        sem = self.lsem[i]
        if self.lcount[i]:
            q.wait((sem, self.lcount[i]))
        self.lcount[i] += 16
        q.wait(*w)
        q.items.append((lambda e: e.dma_start(dst, src).then_inc(sem, 16), "dma"))
        return (sem, self.lcount[i])

    def panel(self, src, kt, cols):
        i, buf, w = self.wring.get()
        v = buf[:, 0:kt * cols].rearrange("p (k c) -> p k c", k=kt)
        self.Q.wait(w)
        self.wcount[i] += 16
        sem = self.wsem[i]
        s = src.rearrange("(k p) c -> p k c", p=128)
        self.Q.items.append((lambda e: e.dma_start(v, s).then_inc(sem, 16), "dma"))
        return i, v, (sem, self.wcount[i])

    def linT(self, h, W, k0, kt, c0, ncol, parts, evac, ready, panel=512):
        last = None
        for c in range(0, ncol, panel):
            n = min(panel, ncol - c)
            i, w, tw = self.panel(W[k0:k0 + kt * 128, c0 + c:c0 + c + n], kt, n)
            for m in range(0, n, 128):
                mw = min(128, n - m)
                for pi, (a, b) in enumerate(parts):
                    bi, ps, free = self.ps.get()
                    for k in range(kt):
                        last = self.T.mm(ps[0:mw, 0:b - a], w[:, k, m:m + mw], h[:, k, a:b], k == 0, k == kt - 1,
                                         free, tw, ready, inc=(k == kt - 1))
                    self.ps.done(bi, evac((c + m) // 128, pi, ps[0:mw, 0:b - a], last))
            self.wring.done(i, last)
        return last

    def linR(self, h, tiles, W, kt, c0, n, evac, ready, starts=None):
        i, w, tw = self.panel(W[0:kt * 128, c0:c0 + n], kt, n)
        last = None
        for x in range(tiles):
            bi, ps, free = self.ps.get()
            for k in range(kt):
                o = starts[x] if starts else x * 128
                last = self.T.mm(ps[:, 0:n], h[:, k, o:o + 128], w[:, k, :], k == 0, k == kt - 1,
                                 free, tw, ready, inc=(k == kt - 1))
            self.ps.done(bi, evac(x, ps[:, 0:n], last))
        self.wring.done(i, last)
        return last

    def ada(self, W, ci, bi, t):
        out = t
        for c in range(12):
            i, w, tw = self.panel(W[:, c * 512:c * 512 + 512], 8, 512)
            b, ps, free = self.ps.get()
            for k in range(8):
                t1 = self.T.mm(ps[0:2, :], self.sc[:, k, ci:ci + 2], w[:, k, :], k == 0, k == 7, free, tw,
                               self.t_sc, inc=(k == 7))
            self.wring.done(i, t1)
            r, row, rf = self.rows.get()
            t2 = self.S.cp(row[0:2, :], ps[0:2, :], t1, rf)
            self.ps.done(b, t2)
            b, ps, free = self.ps.get()
            for m in range(4):
                t3 = self.T.tr(ps[:, m * 2:m * 2 + 2], row[0:2, m * 128:m * 128 + 128], self.ident[0:2, 0:2], free, t2,
                               inc=(m == 3))
            self.rows.done(r, t3)
            t4 = self.V.tt(out[:, c * 4:c * 4 + 4, :], ps[:, 0:8].rearrange("p (m j) -> p m j", j=2),
                           self.adab[:, bi * 48 + c * 4:bi * 48 + c * 4 + 4, None].to_broadcast([128, 4, 2]),
                           ADD, t3, self.t_par)
            self.ps.done(b, t4)
        return self.V.last()

    def rstd(self, dst, ps, n, eps, tok, scr):
        t = self.V.ts(scr, ps, 1.0 / n, eps, MUL, ADD, tok)
        t2 = self.V.rec(scr, scr)
        return t, self.S.f(dst, scr, ACT.Sqrt, t2)

    def modulate(self, h, x, T, s1, sh, ready):
        mark = self.top
        sq = self.sbring(2, T)
        r = self.alloc(T)
        scr = self.alloc(T)
        bi, ps, free = self.ps.get()
        for k in range(8):
            i, s, sf = sq.get()
            t = self.S.f(s, x[:, k, :], ACT.Square, sf, ready)
            t = self.T.mm(ps[:, 0:T], self.ones, s, k == 0, k == 7, t, free, self.t_con, inc=True)
            sq.done(i, t)
        t, t2 = self.rstd(r, ps[:, 0:T], 1024, 1e-6, t, scr)
        self.ps.done(bi, t)
        for k in range(8):
            t = self.V.stt(h[:, k, :], x[:, k, :], s1[:, k:k + 1], r, MUL, MUL, t2, ready)
            if sh is not None:
                t = self.S.f(h[:, k, :], h[:, k, :], ACT.Identity, t, bias=sh[:, k:k + 1])
        self.top = mark
        return t, [self.V.last(), self.S.last(), self.T.last()]

    def mlp(self, l, parts, hs, xs, gates, ready):
        mark = self.top
        T = sum(b - a for a, b in parts)
        hid = self.sbring(2, 8, T)
        tmp = self.sbring(2, 512)
        h, W1, W2 = hs, self.D["mlp_w1"][l], self.D["mlp_w2"][l]
        for q in range(4):
            hi, hd, hf = hid.get()

            def evac(m, pi, ps, tok):
                a, b = parts[pi]
                i, s, sf = tmp.get()
                t = self.S.f(s[:, 0:b - a], ps, ACT.Relu, tok, sf)
                t2 = self.V.tt(hd[:, m, a:b], s[:, 0:b - a], s[:, 0:b - a], MUL, t, hf)
                tmp.done(i, t2)
                return t

            self.linT(h, W1, 0, 8, q * 1024, 1024, parts, evac, ready)
            th = self.V.last()

            def evac2(m, pi, ps, tok):
                return self.V.stt(xs[pi][:, m, :], ps, gates[pi][:, m:m + 1], xs[pi][:, m, :], MUL, ADD, tok)

            t = self.linT(hd, W2, q * 1024, 8, 0, 1024, parts, evac2, th)
            hid.done(hi, t)
        self.top = mark
        return self.V.last()

    def body(self):
        D, T, V, S, G = self.D, self.T, self.V, self.S, self.G
        _, at = layout_constants()
        self.at = at

        def const(name):
            o, n = at[name]
            v = self.alloc(n)
            self.load(v, D["consts"][:, o:o + n])
            return v

        self.const = const
        self.ident, self.ones, self.blk = const("ident"), const("ones"), const("blk")
        self.X = self.alloc(8, 512)
        adab = self.alloc(144)
        self.adab = adab
        cc = self.alloc(8, 4)
        self.load(adab, D["ada_b"])
        self.load(cc, D["cc"])
        self.load(self.X, D["xT"].rearrange("(k p) t -> p k t", p=128))
        tl = self.all_loads()
        self.t_con = self.t_par = tl
        self.sc = self.alloc(8, 4)
        sg = self.alloc(8, 4)
        t = S.f(sg, cc, ACT.Sigmoid, tl)
        self.t_sc = V.tt(self.sc, cc, sg, MUL, t, tl)
        V.wait(tl), T.wait(tl), G.wait(tl)
        self.rows = self.sbring(2, 512)
        self.ada_out = self.alloc(48, 2)
        base = self.top
        if "L0" in self.stages or "L1" in self.stages:
            self.C = self.alloc(8, 256)
            tc = self.load(self.C, D["ctxT"].rearrange("(k p) t -> p k t", p=128))
            m = self.top
            if "L0" in self.stages:
                self.layer0(tc)
                self.fence()
            self.top = m
            if "L1" in self.stages:
                self.layer1(tc)
                self.fence()
        self.top = base
        if "L2" in self.stages:
            self.block2()
        else:
            self.finish(self.X, self.V.last())

    def finish(self, x, tok):
        t = self.load(self.out.rearrange("(k p) t -> p k t", p=128), x, tok)
        self.Q.wait(t)

    def all_loads(self):
        return [(s, c) for s, c in zip(self.lsem, self.lcount) if c]

    def adaln(self, W, ci, bi):
        o = self.ada_out
        self.ada(W, ci, bi, o)
        p = self.alloc(2, 48)
        t = self.V.cp(p, o.rearrange("p m j -> p j m"))
        for j in range(2):
            for s in (8, 32):
                t = self.V.ts(p[:, j, s:s + 8], p[:, j, s:s + 8], 1.0, None, ADD, None)
        return p, t

    def layer0(self, tc):
        D, T, V, S, G = self.D, self.T, self.V, self.S, self.G
        X, C = self.X, self.C
        p, tp = self.adaln(D["ada_w"][0], 0, 0)
        LP, CP = p[:, 0, :], p[:, 1, :]
        PARTS = [(0, 512), (512, 768)]
        self.h_at = self.top
        h = self.alloc(8, 768)
        cat = self.alloc(8, 768)
        th1, _ = self.modulate(h[:, :, 0:512], X, 512, LP[:, 8:16], LP[:, 0:8], tp)
        self.fence()
        th2, _ = self.modulate(h[:, :, 512:768], C, 256, CP[:, 8:16], CP[:, 0:8], [tp, tc])
        th = [th1, th2]
        self.fence()
        W = D["ab_w_in"]
        mark = self.top
        qk = self.alloc(8, 768)
        va = self.alloc(6, 512)
        qkn = self.alloc(2)
        nam = self.const("nam")
        self.load(qkn, D["qkn"])
        tl = self.all_loads()
        mark2 = self.top
        sq = self.sbring(2, 512)
        rr = self.sbring(2, 512)

        def ev_qk(m, pi, ps, tok):
            a, b = PARTS[pi]
            n = b - a
            i, s, sf = sq.get()
            j, r, rf = rr.get()
            t0 = V.cp(qk[:, m, a:b], ps, tok)
            t = S.f(s[:, 0:n], qk[:, m, a:b], ACT.Square, t0, sf)
            bi, p2, free = self.ps.get()
            t = T.mm(p2[:, 0:n], self.blk, s[:, 0:n], True, True, t, free, inc=True)
            ta, tb = self.rstd(r[:, 0:n], p2[:, 0:n], 64, 1e-6, t, r[:, 0:n])
            self.ps.done(bi, ta)
            g = qkn[:, 0:1] if m < 4 else qkn[:, 1:2]
            t = V.stt(qk[:, m, a:b], qk[:, m, a:b], g, r[:, 0:n], MUL, MUL, tb, tl)
            sq.done(i, t)
            rr.done(j, t)
            return t0

        self.linT(h, W, 0, 8, 0, 1024, PARTS, ev_qk, th)
        self.linR(h, 6, W, 8, 1024, 512, lambda x, ps, tok: S.cp(va[:, x, :], ps, tok), th)
        tqk, tva = V.last(), S.last()
        self.fence()
        self.top = mark2
        SS = self.sbring(3, 768)
        PTr = self.sbring(2, 6, 512)
        BM = self.sbring(2, 14, 64)
        st = self.sbring(4, 4)

        def softmax_rows(n, parts_ps, tps, bias, tb):
            i, s, sf = SS.get()
            off = 0
            reads = []
            for (ps, w), bm in zip(parts_ps, bias):
                if bm is not None:
                    t = V.stt(s[:, off:off + w].rearrange("p (a b) -> p a b", b=64),
                              ps[:, 0:w].rearrange("p (a b) -> p a b", b=64), 0.125, bm, MUL, ADD, tps, tb, sf)
                else:
                    t = V.ts(s[:, off:off + w], ps[:, 0:w], 0.125, None, MUL, None, tps, sf)
                reads.append(t)
                off += w
            k, z, zf = st.get()
            t = V.red(z[:, 0:1], s[:, 0:n], MAX, zf, neg=True)
            t = S.f(s[:, 0:n], s[:, 0:n], ACT.Exp, t, bias=z[:, 0:1], acc=z[:, 1:2])
            t = V.rec(z[:, 2:3], z[:, 1:2], t)
            t = V.ts(s[:, 0:n], s[:, 0:n], z[:, 2:3], None, MUL, None)
            st.done(k, t)
            return i, s, t, reads

        for hd in range(8):
            m, o = hd // 2, 64 * (hd % 2)
            bi, bm, bf = BM.get()
            tb = self.load(bm, D["rpb"][hd], bf)
            tb = V.tt(bm, bm, nam[:, None, :].to_broadcast([128, 14, 64]), ADD, tb, tl)
            for lat in (True, False):
                nq, nk = (4, 6) if lat else (2, 2)
                pi, PT, pf = PTr.get()
                tev = []
                for qt in range(nq):
                    q0 = qt * 128 if lat else 512 + qt * 128
                    segs = [(0, 512), (512, 768)] if lat else [(512, 768)]
                    got = []
                    for a, b in segs:
                        x, ps, free = self.ps.get()
                        t = T.mm(ps[:, 0:b - a], qk[o:o + 64, m, q0:q0 + 128], qk[o:o + 64, 4 + m, a:b], True, True,
                                 free, tqk, inc=True)
                        got.append((x, ps, b - a))
                    bias = [bm[:, 6 - 2 * qt:14 - 2 * qt, :], None] if lat else [None]
                    si, s, tsm, reads = softmax_rows(128 * nk, [(ps, w) for _, ps, w in got], t, bias, tb)
                    for (x, _, _), r in zip(got, reads):
                        self.ps.done(x, r)
                    tt = None
                    for k0 in range(0, nk, 4):
                        kn = min(4, nk - k0)
                        x, ps, free = self.ps.get()
                        for k in range(kn):
                            tt = T.tr(ps[:, k * 128:k * 128 + 128], s[:, (k0 + k) * 128:(k0 + k) * 128 + 128], self.ident,
                                      free, tsm, inc=(k == kn - 1))
                        dst = PT[:, k0:k0 + kn, qt * 128:qt * 128 + 128]
                        sv = ps[:, 0:kn * 128].rearrange("p (k c) -> p k c", c=128)
                        te = (S if k0 == 0 else V).cp(dst, sv, tt, pf)
                        tev.append(te)
                        self.ps.done(x, te)
                    SS.done(si, tt)
                n = nq * 128
                x, ps, free = self.ps.get()
                for k in range(nk):
                    kt = k if lat else 4 + k
                    t = T.mm(ps[o:o + 64, 0:n], va[:, kt, hd * 64:hd * 64 + 64], PT[:, k, 0:n], k == 0, k == nk - 1,
                             free, tev, tva, inc=(k == nk - 1))
                PTr.done(pi, t)
                c0 = 0 if lat else 512
                t = S.cp(cat[o:o + 64, m, c0:c0 + n], ps[o:o + 64, 0:n], t)
                self.ps.done(x, t)
            BM.done(bi, V.last())
        self.fence()
        self.top = mark
        self.mlstm(h, cat, th)
        self.fence()
        self.top = mark

        def ev_o(m, pi, ps, tok):
            xs, g = (X, LP) if pi == 0 else (C, CP)
            return V.stt(xs[:, m, :], ps, g[:, 16 + m:17 + m], xs[:, m, :], MUL, ADD, tok)

        self.linT(cat, D["ab_w_out"], 0, 8, 0, 1024, PARTS, ev_o, [V.last(), S.last()])
        tx = V.last()
        self.fence()
        th1, _ = self.modulate(h[:, :, 0:512], X, 512, LP[:, 32:40], LP[:, 24:32], tx)
        self.fence()
        th2, _ = self.modulate(h[:, :, 512:768], C, 256, CP[:, 32:40], CP[:, 24:32], tx)
        self.fence()
        self.top = mark - 8 * 768
        self.mlp(0, PARTS, h, [X, C], [LP[:, 40:48], CP[:, 40:48]], [th1, th2])

    def mlstm(self, h, cat, th):
        D, T, V, S, G = self.D, self.T, self.V, self.S, self.G
        W = D["ab_w_in"]
        R = 768
        kr = self.alloc(6, 512)
        vr = self.alloc(6, 512)
        og = self.alloc(4, 768)
        qT = self.alloc(4, 768)
        kT = self.alloc(4, 768)
        Gt = self.alloc(6, 16)
        cn = {n: self.const(n) for n in ("le", "ge", "mle", "mge")}
        gb, hn = self.alloc(16), self.alloc(4)
        mark = self.top
        gw = self.alloc(8, 16)
        rope = self.const("rope")
        rope = rope.rearrange("p (x c d) -> p x c d", x=4, c=2)
        self.load(gb, D["gate_b"])
        self.load(hn, D["hn"])
        self.load(gw, W[:, 3584:3600].rearrange("(k p) c -> p k c", p=128))
        tl = self.all_loads()
        qr = self.sbring(2, 512)
        tp = self.alloc(4, 256)

        def v4(x, half):
            return x.rearrange("p (h r u d) -> p h r u d", h=4, r=2, u=2)[:, :, :, half, :]

        def rope_to(dst, x, ps, tok, w):
            cs = [rope[:, x, c, :].rearrange("p (r d) -> p r d", r=2) for c in range(2)]
            a = tp
            ts = []
            for hh in range(4):
                xv = ps[:, hh * 128:hh * 128 + 128].rearrange("p (r u d) -> p r u d", r=2, u=2)
                tv = a[:, :, hh * 64:hh * 64 + 64].rearrange("p j (r d) -> p j r d", r=2)
                for j, (u, c) in enumerate(((0, 0), (1, 1), (0, 1), (1, 0))):
                    t = V.tt(tv[:, j, :, :], xv[:, :, u, :], cs[c], MUL, tok, tl)
            dv = dst.rearrange("p (g u d) -> p g u d", u=2, d=32)
            av = a.rearrange("p j (g d) -> p j g d", d=32)
            V.tt(dv[:, :, 0, :], av[:, 0, :, :], av[:, 1, :, :], SUB, w)
            V.tt(dv[:, :, 1, :], av[:, 2, :, :], av[:, 3, :, :], ADD)
            return t

        def to_T(dst, x, src, t, scale):
            b, ps, free = self.ps.get()
            for hh in range(4):
                tt = T.tr(ps[:, hh * 128:hh * 128 + 128], src[:, hh * 128:hh * 128 + 128], self.ident, free, t,
                          inc=(hh == 3))
            te = S.f(dst[:, :, x * 128:x * 128 + 128], ps.rearrange("p (h c) -> p h c", h=4), ACT.Copy, tt, scale=scale)
            self.ps.done(b, te)
            return tt

        def ev_q(x, ps, tok):
            i, q, qf = qr.get()
            if x < 4:
                t = rope_to(q, x, ps, tok, qf)
            else:
                t = V.cp(q, ps, tok, qf)
            qr.done(i, to_T(qT, x, q, V.last(), 128.0 ** -0.5))
            return t

        def ev_k(x, ps, tok):
            t = rope_to(kr[:, x, :], x, ps, tok, None) if x < 4 else V.cp(kr[:, x, :], ps, tok)
            to_T(kT, x, kr[:, x, :], V.last(), 1.0)
            return t

        self.linR(h, 6, W, 8, 1536, 512, ev_q, th)
        self.linR(h, 6, W, 8, 2048, 512, ev_k, th)
        self.linR(h, 6, W, 8, 2560, 512, lambda x, ps, tok: S.cp(vr[:, x, :], ps, tok), th)
        PARTS = [(0, 512), (512, 768)]

        def ev_o(m, pi, ps, tok):
            a, b = PARTS[pi]
            t = S.f(og[:, m, a:b], ps, ACT.Sigmoid, tok)
            V.ts(og[:, m, a:b], og[:, m, a:b], hn[:, m:m + 1], None, MUL, None, t, tl)
            return t

        self.linT(h, W, 0, 8, 3072, 512, PARTS, ev_o, th)
        for x in range(6):
            b, ps, free = self.ps.get()
            for k in range(8):
                t = T.mm(ps[:, 0:16], h[:, k, x * 128:x * 128 + 128], gw[:, k, :], k == 0, k == 7, free, tl, inc=(k == 7))
            t = V.tt(Gt[:, x, :], ps[:, 0:16], gb, ADD, t, tl)
            self.ps.done(b, t)
        self.fence()
        self.top = mark
        keep = self.top, self.size
        self.top, self.size = self.h_at, self.h_at + 6144
        HS = self.alloc(6, 512)
        dg = self.sbring(2, 4, 128)
        ex = self.sbring(2, 4, 128)
        pp = self.sbring(2, 4, 128)
        self.top, self.size = keep
        A = lambda: self.alloc(6, 8)
        I, Fg, B, BT, IB, M1, MA, MX, ML, MS, WI, WS, DC, EM, NMX = (A() for _ in range(15))
        g4 = lambda a: a.rearrange("p x (d h) -> p x d h", d=2)
        t = S.f(Gt, Gt, ACT.Tanh, V.last(), scale=1.0 / 15.0)
        gv = Gt.rearrange("p x (d k h) -> p x d k h", d=2, k=2)
        for d in range(2):
            V.ts(g4(I)[:, :, d, :], gv[:, :, d, 0, :], 15.0, None, MUL, None, t)
            t2 = S.f(g4(Fg)[:, :, d, :], gv[:, :, d, 1, :], ACT.Exp, scale=-15.0)
        t = S.f(Fg, Fg, ACT.Ln, bias=1.0)
        t = V.ts(Fg, Fg, -1.0, None, MUL, None, t)
        b, ps, free = self.ps.get()
        bv = ps[:, 0:96].rearrange("p (j x h) -> p j x h", j=4, h=4)
        for d, n in ((0, "le"), (1, "ge")):
            T.mmx(bv[:, d, :, :], cn[n], g4(Fg)[:, :, d, :], True, True, free, t, tl)
            t1 = T.mmx(bv[:, 2 + d, :, :], self.ones, g4(Fg)[:, :, d, :], True, True, inc=True)
        for d in range(2):
            V.cp(g4(B)[:, :, d, :], bv[:, d, :, :], t1)
            t = V.cp(g4(BT)[:, :, d, :], bv[:, 2 + d, :, :])
        self.ps.done(b, t)
        t = V.tt(IB, I, B, SUB)

        def rows_of(col):
            i, d, df = dg.get()
            t = V.tt(d, self.ident[:, None, :].to_broadcast([128, 4, 128]), col[:, :, None].to_broadcast([128, 4, 128]),
                     MUL, df)
            b, ps, free = self.ps.get()
            t = T.mm(ps, self.ones, d.rearrange("p h c -> p (h c)"), True, True, t, free, inc=True)
            dg.done(i, t)
            return b, ps.rearrange("p (h c) -> p h c", h=4), t

        for x in range(6):
            for d in range(2):
                b, ps, t = rows_of(g4(IB)[:, x, d, :])
                V.red(g4(MA)[:, x, d, :], ps, MAX, t)
                i, e, ef = ex.get()
                t = V.tt(e, ps, cn["mge" if d == 0 else "mle"][:, None, :].to_broadcast([128, 4, 128]), ADD, ef)
                self.ps.done(b, t)
                t = V.red(g4(M1)[:, x, d, :], e, MAX)
                ex.done(i, t)
        order = {0: [4, 5, 0, 1, 2, 3], 1: [5, 4, 3, 2, 1, 0]}
        for d in range(2):
            for n, x in enumerate(order[d]):
                ms = g4(MS)[:, x, d, :]
                if n == 0:
                    V.set(ms, 0.0)
                V.tt(g4(ML)[:, x, d, :], g4(MA)[:, x, d, :], ms, MAX)
                if n < 5:
                    V.tt(g4(MS)[:, order[d][n + 1], d, :], g4(BT)[:, x, d, :], g4(ML)[:, x, d, :], ADD)
        V.tt(MX, M1, MS, MAX)
        V.tt(WI, MS, MX, SUB)
        V.tt(WS, IB, ML, SUB)
        V.tt(DC, MS, ML, SUB)
        V.tt(EM, B, MX, ADD)
        t = V.ts(NMX, MX, -1.0, None, MUL, None)
        S.f(WI, WI, ACT.Exp, t)
        S.f(WS, WS, ACT.Exp)
        S.f(DC, DC, ACT.Exp)
        tg = S.f(EM, EM, ACT.Exp, scale=-1.0)
        V.wait(tg)
        Cst = self.alloc(8, 128)
        Nst = self.alloc(8)
        V.set(Cst, 0.0)
        tz = V.set(Nst, 0.0)
        nm = self.sbring(2, 4, 128)
        kw = self.sbring(2, 4, 128)
        dn = self.sbring(2, 8)
        done = set()
        tst = [tz, tz]
        for n in range(6):
            for d in range(2):
                x = order[d][n]
                xs = slice(x * 128, x * 128 + 128)
                c = lambda a: g4(a)[:, x, d, :]
                b, ps, t = rows_of(c(MX))
                i, e, ef = ex.get()
                t = V.tt(e, cn["mle" if d == 0 else "mge"][:, None, :].to_broadcast([128, 4, 128]), ps, SUB, t, ef)
                self.ps.done(b, t)
                for hh in range(4):
                    te = S.f(e[:, hh, :], e[:, hh, :], ACT.Exp, t, bias=c(IB)[:, hh:hh + 1])
                b, ps, free = self.ps.get()
                for hh in range(4):
                    t = T.mm(ps[:, hh * 128:hh * 128 + 128], kT[:, hh, xs], qT[:, hh, xs], True, True, free, S.last(),
                             inc=(hh == 3))
                j, p, pf = pp.get()
                tpp = V.tt(p, ps.rearrange("p (h c) -> p h c", h=4), e, MUL, t, te, pf)
                self.ps.done(b, tpp)
                ex.done(i, tpp)
                k, w, wf = kw.get()
                tkw = V.tt(w, kr[:, x, :].rearrange("p (h c) -> p h c", h=4), c(WS)[:, :, None].to_broadcast([128, 4, 128]),
                           MUL, wf)
                b1, p1, f1 = self.ps.get()
                b2, p2, f2 = self.ps.get()
                b3, p3, f3 = self.ps.get()
                for hh in range(4):
                    hs = slice(hh * 128, hh * 128 + 128)
                    T.mm(p1[:, hs], p[:, hh, :], vr[:, x, hs], True, True, tpp, f1)
                    T.mm(p2[:, hs], qT[:, hh, xs], Cst[:, 4 * d + hh, :], True, True, tst[d], f2)
                    T.mm(p3[:, hh:hh + 1], p[:, hh, :], self.ones[:, 0:1], True, True, f3)
                    tm = T.mm(p3[:, 4 + hh:5 + hh], qT[:, hh, xs], Nst[:, 4 * d + hh:4 * d + hh + 1], True, True, inc=True)
                pp.done(j, tm)
                b4, p4, f4 = self.ps.get()
                b5, p5, f5 = self.ps.get()
                for hh in range(4):
                    hs = slice(hh * 128, hh * 128 + 128)
                    T.mm(p4[:, hs], w[:, hh, :], vr[:, x, hs], True, True, tkw, f4)
                    tu = T.mm(p5[:, hh:hh + 1], w[:, hh, :], self.ones[:, 0:1], True, True, f5, inc=True)
                kw.done(k, tu)
                cs = Cst[:, 4 * d:4 * d + 4, :]
                V.tt(cs, cs, c(DC)[:, :, None].to_broadcast([128, 4, 128]), MUL, tm)
                t = V.tt(cs, cs, p4.rearrange("p (h c) -> p h c", h=4), ADD, tu)
                self.ps.done(b4, t)
                ns = Nst[:, 4 * d:4 * d + 4]
                V.tt(ns, ns, c(DC), MUL)
                t = V.tt(ns, ns, p5[:, 0:4], ADD)
                self.ps.done(b5, t)
                tst[d] = t
                j, q, qf = nm.get()
                t = V.tt(q, p2.rearrange("p (h c) -> p h c", h=4), c(WI)[:, :, None].to_broadcast([128, 4, 128]), MUL, qf)
                self.ps.done(b2, t)
                t = V.tt(q, q, p1.rearrange("p (h c) -> p h c", h=4), ADD)
                self.ps.done(b1, t)
                z, dd, df = dn.get()
                V.tt(dd[:, 0:4], p3[:, 4:8], c(WI), MUL, df)
                t = V.tt(dd[:, 0:4], dd[:, 0:4], p3[:, 0:4], ADD)
                self.ps.done(b3, t)
                t = S.f(dd[:, 0:4], dd[:, 0:4], ACT.Abs, t)
                V.tt(dd[:, 0:4], dd[:, 0:4], c(EM), MAX, t)
                V.rec(dd[:, 0:4], dd[:, 0:4])
                rd = dd[:, 0:4, None].to_broadcast([128, 4, 128])
                hv = HS[:, x, :].rearrange("p (h c) -> p h c", h=4)
                if x in done:
                    V.tt(q, q, rd, MUL)
                    t = V.tt(hv, hv, q, ADD)
                else:
                    t = V.tt(hv, q, rd, MUL)
                    done.add(x)
                nm.done(j, t)
                dn.done(z, t)
        for x in range(6):
            hv = HS[:, x, :].rearrange("p (h c) -> p h c", h=4)
            j, q, qf = nm.get()
            z, dd, df = dn.get()
            V.tt(q, hv, hv, MUL, qf)
            V.red(dd[:, 0:4], q, ADD, df)
            V.ts(dd[:, 0:4], dd[:, 0:4], 1.0 / 128, 1e-6, MUL, ADD)
            t = V.rec(dd[:, 0:4], dd[:, 0:4])
            t = S.f(dd[:, 4:8], dd[:, 0:4], ACT.Sqrt, t)
            t = V.tt(q, hv, dd[:, 4:8, None].to_broadcast([128, 4, 128]), MUL, t)
            dn.done(z, t)
            b, ps, free = self.ps.get()
            for hh in range(4):
                t2 = T.tr(ps[:, hh * 128:hh * 128 + 128], q[:, hh, :], self.ident, t, free, inc=(hh == 3))
            nm.done(j, t2)
            xs = slice(x * 128, x * 128 + 128)
            t = V.tt(cat[:, 4:8, xs], ps.rearrange("p (h c) -> p h c", h=4), og[:, :, xs], MUL, t2)
            self.ps.done(b, t)


    def layer1(self, tc):
        D, T, V, S, G = self.D, self.T, self.V, self.S, self.G
        X, C = self.X, self.C
        p, tp = self.adaln(D["ada_w"][1], 0, 1)
        LP, CP = p[:, 0, :], p[:, 1, :]
        vec = self.alloc(40)
        wa0 = self.alloc(32)
        self.load(vec, D["rwv"])
        self.load(wa0, D["w0a0"])
        gh = self.alloc(2, 512)
        mix = self.alloc(8, 772)
        rT = self.alloc(8, 768)
        k_at = self.top
        kT = self.alloc(8, 768)
        mark = self.top
        hp = self.alloc(8, 772)
        xx_at = self.top
        keep = self.top
        self.top = k_at
        w1 = self.alloc(8, 128)
        a1 = self.alloc(8, 128)
        g1 = self.alloc(8, 160)
        mu = self.alloc(48)
        self.top = keep
        for d in range(2):
            self.load(w1[:, :, d * 64:d * 64 + 64], D["w1"][d].rearrange("(k p) r -> p k r", p=128))
            self.load(a1[:, :, d * 64:d * 64 + 64], D["a1"][d].rearrange("(k p) r -> p k r", p=128))
        self.load(g1, D["g1"].rearrange("(k p) r -> p k r", p=128))
        for c in (0, 513, 514, 771):
            tz = V.set(hp[:, :, c:c + 1], 0.0)
        self.modulate(hp[:, :, 1:513], X, 512, LP[:, 8:16], LP[:, 0:8], tp)
        self.fence()
        self.modulate(hp[:, :, 515:771], C, 256, CP[:, 8:16], CP[:, 0:8], [tp, tc])
        self.fence()
        xx = self.alloc(8, 772)
        mu = self.C_view(0, 48)
        self.load(mu, D["mu"], S.last())
        wh, ah = self.C_view(64, 768), self.C_view(832, 768)
        tl = self.all_loads()
        for k in range(8):
            V.tt(xx[:, k, 1:771], hp[:, k, 0:770], hp[:, k, 2:772], ADD)
            V.stt(xx[:, k, 1:771], xx[:, k, 1:771], 0.5, hp[:, k, 1:771], MUL, SUB)

        def blend(dst, s, w):
            for k in range(8):
                t = V.stt(dst[:, k, 1:771], xx[:, k, 1:771], mu[:, s * 8 + k:s * 8 + k + 1], hp[:, k, 1:771], MUL, ADD,
                          w, tl)
            return t

        def hidden(w, m0, mw, dst, fn, parts, t):
            for a, b, o in parts:
                bi, ps, free = self.ps.get()
                for k in range(8):
                    tm = T.mm(ps[0:mw, 0:b - a], w[:, k, m0:m0 + mw], mix[:, k, a:b], k == 0, k == 7, free, t, tl,
                              inc=(k == 7))
                self.ps.done(bi, S.f(dst[0:mw, o:o + b - a], ps[0:mw, 0:b - a], fn, tm))
            return tm

        HP = [(1, 513, 0), (515, 771, 512)]
        t = blend(mix, 1, None)
        t = hidden(w1, 0, 128, wh, ACT.Tanh, HP, t)
        t = blend(mix, 4, t)
        t = hidden(a1, 0, 128, ah, ACT.Copy, HP, t)
        t = blend(mix, 5, t)
        hidden(g1, 0, 128, gh[:, 0, :], ACT.Sigmoid, HP[:1], t)
        t = hidden(g1, 128, 32, gh[:, 1, :], ACT.Sigmoid, HP[:1], t)
        parts = [(1, 513), (515, 771)]
        for s, dst, W in ((0, rT, D["rkv"][0]), (2, kT, D["rkv"][1])):
            t = blend(mix, s, t)

            def ev(m, pi, ps, tok):
                a, b = ((0, 512), (512, 768))[pi]
                return S.cp(dst[:, m, a:b], ps, tok)

            t = self.linT(mix, W, 0, 8, 0, 1024, parts, ev, t)
        tv = blend(xx, 3, None)
        self.fence()
        vR = self.region(mix, 6144).rearrange("p (x c) -> p x c", x=6)
        for c in range(2):
            self.linR(xx, 6, D["rkv"][2], 8, c * 512, 512,
                      lambda x, ps, tok: S.cp(vR[:, x, c * 512:c * 512 + 512], ps, tok), tv,
                      starts=[1, 129, 257, 385, 515, 643])
            self.fence()
        self.top = mark
        self.rwkv(rT, kT, vR, wh, ah, vec, wa0)
        self.fence()
        self.top = mark
        g2 = self.alloc(2, 1024)
        t = [self.load(g2[:, 0, :], D["g2"][0:128, :]), self.load(g2[0:32, 1, :], D["g2"][128:160, :])]
        for m in range(8):
            bi, ps, free = self.ps.get()
            T.mm(ps, g2[:, 0, m * 128:m * 128 + 128], gh[:, 0, :], True, False, t, free)
            tm = T.mm(ps, g2[0:32, 1, m * 128:m * 128 + 128], gh[0:32, 1, :], False, True, inc=True)
            tg = V.tt(rT[:, m, 0:512], rT[:, m, 0:512], ps, MUL, tm)
            self.ps.done(bi, tg)

        def ev_o(m, pi, ps, tok):
            return V.stt(X[:, m, :], ps, LP[:, 16 + m:17 + m], X[:, m, :], MUL, ADD, tok)

        self.linT(rT, D["w_o"], 0, 8, 0, 1024, [(0, 512)], ev_o, tg)
        tx = V.last()
        self.fence()
        self.top = mark
        h = self.region(kT, 4096).rearrange("p (k t) -> p k t", k=8)
        th, _ = self.modulate(h, X, 512, LP[:, 32:40], LP[:, 24:32], tx)
        self.fence()
        self.mlp(1, [(0, 512)], h, [X], [LP[:, 40:48]], th)

    def C_view(self, o, n):
        return self.region(self.C, 2048)[:, o:o + n]

    def region(self, v, n):
        for start, a in self.starts:
            if a is v:
                return self.arena[:, start:start + n]
        raise RuntimeError("not a buffer")

    def rwkv(self, rT, kT, vR, wh, ah, vec, wa0):
        D, T, V, S, G = self.D, self.T, self.V, self.S, self.G
        C0 = float(np.exp(np.float32(-0.5)))
        cn = {n: self.const(n) for n in ("u0", "d0", "u1", "d1", "u2", "d2", "u3", "d3", "lt", "gt", "le", "ge", "r128")}
        self.load_wait = self.all_loads()
        tl = self.load_wait
        wm = self.sbring(2, 2, 128)
        one = lambda: self.alloc(768)
        sg, B, av, kk, e2, kd, bb, aa, ks, rr = (one() for _ in range(10))
        ksum, yT, tA, tB = (self.alloc(512) for _ in range(4))
        mid, end = self.alloc(2, 6), self.alloc(2, 6)
        keep = self.top, self.size
        self.top, self.size = self.w_at, self.w_at + NR * 4096
        mat = lambda: self.alloc(4, 128)
        N, Pw, Pf, Xm, XT, Aak, Ark, Arb = (mat() for _ in range(8))
        BK = self.alloc(2, 2, 128)
        RH = self.sbring(2, 128)
        UU = self.sbring(2, 128)
        ZZ = self.sbring(3, 128)
        zt = self.alloc(128)
        em = self.alloc(6)
        self.top, self.size = keep
        kkv, kav, rkv, lnw, lnb = (vec[:, i * 8:i * 8 + 8] for i in range(5))
        c3 = lambda v: v.rearrange("p (c t) -> p c t", t=128)
        m4 = lambda v: v.rearrange("p g c -> p (g c)")
        bc = lambda v, n: v[:, None, :].to_broadcast([128, n, 128])

        for m in range(8):
            k, r = kT[:, m, :], rT[:, m, :]
            c1 = slice(m, m + 1)
            i, w, wf = wm.get()
            tw = [self.load(w[:, 0, :], D["w2"][:, m * 128:m * 128 + 128], wf),
                  self.load(w[:, 1, :], D["a2"][:, m * 128:m * 128 + 128], wf)]
            V.ts(kk, k, kkv[:, c1], None, MUL, None)
            t = V.tt(sg, kk, kk, MUL)
            for a, b in ((0, 512), (512, 768)):
                bi, ps, free = self.ps.get()
                t1 = T.mm(ps[:, 0:b - a], self.blk, sg[:, a:b], True, True, t, free, inc=True)
                t2 = V.ts(e2[:, a:b], ps[:, 0:b - a], 1e-24, None, MAX, None, t1)
                self.ps.done(bi, t2)
            V.rec(e2, e2)
            t = S.f(e2, e2, ACT.Sqrt, V.last())
            V.tt(kk, kk, e2, MUL, t)
            for d in range(2):
                rows = slice(64 * d, 64 * d + 64)
                for a, b in ((0, 512), (512, 768)):
                    for which, src, dst in ((0, wh, sg), (1, ah, av)):
                        bi, ps, free = self.ps.get()
                        t1 = T.mm(ps[:, 0:b - a], w[rows, which, :], src[rows, a:b], True, True, tw, free, V.last(),
                                  S.last(), inc=True)
                        o = which * 16 + d * 8 + m
                        t2 = S.f(dst[:, a:b], ps[:, 0:b - a], ACT.Sigmoid, t1, bias=wa0[:, o:o + 1])
                        self.ps.done(bi, t2)
                ts = S.last()
                if d == 1:
                    wm.done(i, T.last())
                if d == 0:
                    V.scan(B, cn["r128"], sg, ts, tl)
                    me, en = 63, 127
                else:
                    V.scan(B[:, ::-1], cn["r128"], sg[:, ::-1], ts, tl)
                    me, en = 64, 0
                V.cp(mid[:, 0, :], c3(B)[:, :, me])
                V.tt(end[:, 0, :], c3(B)[:, :, en], mid[:, 0, :], SUB)
                t = V.tt(c3(B), c3(B), mid[:, 0, :, None].to_broadcast([128, 6, 128]), SUB)
                S.f(mid[:, 1, :], mid[:, 0, :], ACT.Exp, t, scale=-C0)
                S.f(end[:, 1, :], end[:, 0, :], ACT.Exp, scale=-C0)
                te = S.f(e2, B, ACT.Exp, scale=C0)
                if d == 0:
                    for a, b in ((slice(0, 3), slice(1, 4)), (slice(4, 5), slice(5, 6)), (slice(5, 6), slice(0, 1))):
                        V.tt(em[:, a], end[:, 1, a], mid[:, 1, b], MUL, te)
                else:
                    V.tt(em[:, 1:6], end[:, 1, 1:6], mid[:, 1, 0:5], MUL, te)
                t = V.tt(sg, B, sg, SUB)
                t1 = S.f(aa, sg, ACT.Exp, t, scale=-C0)
                t2 = S.f(rr, B, ACT.Exp, scale=-C0)
                V.stt(aa, aa, -1.0, kk, MUL, MUL, t1)
                V.tt(rr, rr, r, MUL, t2)
                V.tt(bb, kk, av, MUL)
                V.tt(bb, bb, e2, MUL)
                V.ts(kd, av, 1.0, kav[:, c1], SUB, MUL)
                V.stt(kd, kd, 1.0, k, ADD, MUL)
                t = V.tt(ks, kd, e2, MUL)
                if d == 0:
                    V.cp(ksum, kd[:, 0:512])
                else:
                    V.tt(ksum, ksum, kd[:, 0:512], ADD)
                u = (lambda n: "u" + n) if d == 0 else (lambda n: "d" + n)
                dn = (lambda n: "d" + n) if d == 0 else (lambda n: "u" + n)
                strict, incl = ("lt", "le") if d == 0 else ("gt", "ge")
                zi, z, zf = ZZ.get()
                tz = V.set(z, 0.0, zf)
                batches = [(4, 5), (0, 1), (2, 3)] if d == 0 else [(5, 4), (3, 2), (1, 0)]
                for bn, items in enumerate(batches):
                    lat = bn > 0
                    tok = [slice(x * 128, x * 128 + 128) for x in items]
                    tops = V.last()
                    last_pe = T.last()

                    def products(lhs, rhs, outs):
                        for hd in range(2):
                            o = slice(64 * hd, 64 * hd + 64)
                            bi, ps, free = self.ps.get()
                            for it in range(2):
                                t = T.mm(ps[:, it * 128:it * 128 + 128], lhs[o, tok[it]], rhs[o, tok[it]], True, True,
                                         free, tops, inc=(it == 1))
                            pv = ps[:, 0:256].rearrange("p (i c) -> p i c", i=2)
                            for dst, mask in outs:
                                dv = dst[:, 2 * hd:2 * hd + 2, :]
                                if mask is None:
                                    t = S.cp(dv, pv, t)
                                else:
                                    t = V.tt(dv, pv, bc(cn[mask], 2), MUL, t)
                            self.ps.done(bi, t)

                    products(bb, aa, [(N, u("0"))])
                    products(aa, bb, [(Pf, None), (Pw, dn("0"))])
                    products(ks, aa, [(Aak, strict)])
                    if lat:
                        products(ks, rr, [(Ark, incl)])
                        products(bb, rr, [(Arb, incl)])
                    tpf = S.last()
                    bi, ps, free = self.ps.get()
                    for it in range(2):
                        T.tr(ps[:, it * 128:it * 128 + 128], bb[:, tok[it]], self.ident, free, tops)
                        t = T.tr(ps[:, 256 + it * 128:384 + it * 128], ks[:, tok[it]], self.ident, inc=(it == 1))
                    tbk = S.cp(BK.rearrange("p a i c -> p (a i c)"), ps, t)
                    self.ps.done(bi, tbk)
                    t = V.tt(Xm, N, bc(self.ident, 4), ADD)

                    def mul(l, r_, t):
                        bi, ps, free = self.ps.get()
                        for g in range(4):
                            tt = T.mm(ps[:, g * 128:g * 128 + 128], l[:, g, :], r_[:, g, :], True, True, t, free,
                                      inc=(g == 3))
                        return bi, ps, tt

                    for lev in range(3):
                        t = [V.last(), S.last()]
                        if lev < 2:
                            b1, p1, t1 = mul(Pw, N, t)
                        b2, p2, t2 = mul(N, Pw, t)
                        if lev < 2:
                            self.ps.done(b1, S.cp(m4(N), p1, t1, t2))
                        t3 = V.cp(m4(Pw), p2, t2)
                        self.ps.done(b2, t3)
                        b3, p3, t3 = mul(Pw, Xm, t3)
                        self.ps.done(b3, V.tt(m4(Xm), m4(Xm), p3, ADD, t3))
                    bi, ps, free = self.ps.get()
                    tx = V.last()
                    for g in range(4):
                        t = T.tr(ps[:, g * 128:g * 128 + 128], Xm[:, g, :], self.ident, free, tx, inc=(g == 3))
                    tt = S.cp(m4(XT), ps, t)
                    self.ps.done(bi, tt)
                    for lev in range(1, 4):
                        b1, p1, t1 = mul(Pf, Xm, [V.last(), tpf])
                        t2 = V.tt(N, p1.rearrange("p (g c) -> p g c", g=4), bc(cn[u(str(lev))], 4), MUL, t1, S.last())
                        self.ps.done(b1, t2)
                        b2, p2, t3 = mul(XT, N, [t2, tt])
                        if lev < 3:
                            b3, p3, t4 = mul(N, XT, [t2, tt])
                        tx = V.tt(m4(Xm), m4(Xm), p2, ADD, t3)
                        self.ps.done(b2, tx)
                        if lev < 3:
                            tt = V.tt(m4(XT), m4(XT), p3, ADD, t4)
                            self.ps.done(b3, tt)
                    tm = V.last()
                    for it, x in enumerate(items):
                        cs = tok[it]
                        ri, rh, rf = RH.get()
                        ui, uu, uf = UU.get()
                        bi, ps, free = self.ps.get()
                        T.mmx(ps[:, 0:128], aa[:, cs], z, True, False, tz, free, tops)
                        for hd in range(2):
                            o = slice(64 * hd, 64 * hd + 64)
                            vs = vR[:, x, m * 128 + 64 * hd:m * 128 + 64 * hd + 64]
                            t = T.mmx(ps[:, o], Aak[:, 2 * hd + it, :], vs, False, True, tm, inc=(hd == 1))
                        t = S.cp(rh, ps[:, 0:128], t, rf)
                        self.ps.done(bi, t)
                        bi, ps, free = self.ps.get()
                        for hd in range(2):
                            o = slice(64 * hd, 64 * hd + 64)
                            t1 = T.mm(ps[:, o], Xm[:, 2 * hd + it, :], rh[:, o], True, True, t, tm, free, inc=(hd == 1))
                        RH.done(ri, t1)
                        t = S.cp(uu, ps[:, 0:128], t1, uf)
                        self.ps.done(bi, t)
                        if lat:
                            by, py, fy = self.ps.get()
                        if lat:
                            T.mmx(py[:, 0:128], z, rr[:, cs], True, False, fy)
                            for hd in range(2):
                                o = slice(64 * hd, 64 * hd + 64)
                                vs = vR[:, x, m * 128 + 64 * hd:m * 128 + 64 * hd + 64]
                                T.mmx(py[o, 0:128], uu[:, o], Arb[:, 2 * hd + it, :], False, False, t)
                                ty = T.mmx(py[o, 0:128], vs, Ark[:, 2 * hd + it, :], False, True, inc=(hd == 1))
                        if not (bn == 2 and it == 1):
                            bz, pz, fz = self.ps.get()
                            T.mm(pz[:, 0:128], BK[:, 0, it, :], uu, True, False, t, fz, tbk)
                            tzz = T.mm(pz[:, 0:128], BK[:, 1, it, :], vR[:, x, m * 128:m * 128 + 128], False, True, inc=True)
                            nzi, nz, nzf = ZZ.get()
                            t = V.stt(zt, pz[:, 0:128], em[:, x:x + 1], self.blk, MUL, MUL, tzz)
                            self.ps.done(bz, t)
                            tz = V.stt(nz, z, em[:, x:x + 1], zt, MUL, ADD, nzf)
                            ZZ.done(zi, tz, T.last())
                            zi, z = nzi, nz
                        UU.done(ui, T.last())
                        if lat:
                            if d == 0:
                                t = V.cp(yT[:, cs], py[:, 0:128], ty)
                            else:
                                t = V.tt(yT[:, cs], yT[:, cs], py[:, 0:128], ADD, ty)
                            self.ps.done(by, t)
                    V.wait(T.last())
                ZZ.done(zi, V.last(), T.last())
                V.wait(T.last())
                S.wait(T.last())
            bi, ps, free = self.ps.get()
            t = T.mm(ps, self.blk, yT, True, True, V.last(), free, inc=True)
            t1 = V.stt(yT, ps, -1.0 / 64, yT, MUL, ADD, t)
            self.ps.done(bi, t1)
            t = V.tt(tA, yT, yT, MUL)
            bi, ps, free = self.ps.get()
            t = T.mm(ps, self.blk, tA, True, True, t, free, inc=True)
            ta, tb = self.rstd(tB, ps, 64, 64e-5, t, tB)
            self.ps.done(bi, ta)
            V.stt(yT, yT, lnw[:, c1], tB, MUL, MUL, tb)
            V.tt(tA, r[:, 0:512], ksum, MUL)
            t = V.ts(tA, tA, rkv[:, c1], None, MUL, None)
            bi, ps, free = self.ps.get()
            t = T.mm(ps, self.blk, tA, True, True, t, free, inc=True)
            t1 = V.ts(yT, yT, lnb[:, c1], None, ADD, None)
            t2 = S.cp(tB, ps, t, t1)
            self.ps.done(bi, t2)
            bi, ps, free = self.ps.get()
            for x in range(4):
                t = T.tr(ps[:, x * 128:x * 128 + 128], vR[:, x, m * 128:m * 128 + 128], self.ident, free, inc=(x == 3))
            t1 = V.tt(tB, tB, ps, MUL, t2, t)
            self.ps.done(bi, t1)
            V.tt(rT[:, m, 0:512], yT, tB, ADD)

    def block2(self):
        D, T, V, S, G = self.D, self.T, self.V, self.S, self.G
        X = self.X
        p, tp = self.adaln(D["ada_w_2"][0], 2, 2)
        LP, CP = p[:, 0, :], p[:, 1, :]
        n2 = self.alloc(34)
        tn = self.load(n2[:, 0:33], D["n2"])
        V.wait(tn), S.wait(tn)
        V.tt(LP[:, 8:16], LP[:, 8:16], n2[:, 0:8], MUL)
        V.tt(CP[:, 8:16], CP[:, 8:16], n2[:, 0:8], MUL)
        tp = V.tt(LP[:, 32:40], LP[:, 32:40], n2[:, 8:16], MUL)
        low = self.top
        W = D["w_in_2"]
        h = self.alloc(8, 768)
        og = self.alloc(4, 512)
        mark = self.top
        c2 = self.alloc(8, 256)
        tc = self.load(c2, D["ctx2T"].rearrange("(k p) t -> p k t", p=128))
        th1, _ = self.modulate(h[:, :, 0:512], X, 512, LP[:, 8:16], LP[:, 0:8], tp)
        self.fence()
        th2, _ = self.modulate(h[:, :, 512:768], c2, 256, CP[:, 8:16], CP[:, 0:8], [tp, tc])
        th = [th1, th2]
        self.fence()
        self.top = mark
        self.gla(h, og, th, n2)
        self.fence()
        self.top = mark
        mg = self.alloc(16, 512)
        LAT = [(0, 512)]
        self.linT(h, W, 0, 8, 2080, 2048, LAT, lambda m, pi, ps, tok: S.f(mg[:, m, :], ps, ACT.Sigmoid, tok), th)
        mark = self.top
        pT = self.alloc(4, 512)
        mx = self.alloc(4, 512)
        pw = self.alloc(4, 128)
        cnt = self.const("cnt")
        self.load(pw, D["pool_w"].rearrange("g c d -> c g d"))
        tl = self.all_loads()
        self.linT(h, W, 0, 8, 1568, 512, LAT, lambda m, pi, ps, tok: S.cp(pT[:, m, :], ps, tok), th)
        tpt = S.last()
        CA, CB = self.alloc(8, 96), self.alloc(8, 96)
        RA, RB = self.alloc(24, 64), self.alloc(24, 64)
        for b in (CA, CB, RA, RB):
            V.set(b, 0.0)
        pl = self.sbring(2, 512)
        for g in range(4):
            w = 2 ** (g + 1)
            u = pT[:, g, :].rearrange("p (r c) -> p r c", c=64)
            a, b, n = CA, CB, 96
            V.cp(a[:, :, 16:80], u, tpt)
            V.set(a[:, :, 0:16], 0.0)
            V.set(a[:, :, 80:96], 0.0)
            for l in range(g + 1):
                s = 2 ** l
                n -= s
                V.tt(b[:, :, 0:n], a[:, :, 0:n], a[:, :, s:s + n], ADD)
                a, b = b, a
            o = 16 - w // 2
            src, a, b, n = a, RA, RB, 24
            V.cp(a[:, 8:16, :], src[:, :, o:o + 64])
            V.set(a[:, 0:8, :], 0.0)
            V.set(a[:, 16:24, :], 0.0)
            for l in range(g + 1):
                s = 2 ** l
                n -= s
                V.tt(b[:, 0:n, :], a[:, 0:n, :], a[:, s:s + n, :], ADD)
                a, b = b, a
            o = 8 - w // 2
            i, q, qf = pl.get()
            qv = q.rearrange("p (r c) -> p r c", c=64)
            cv = cnt[:, g * 512:g * 512 + 512].rearrange("p (r c) -> p r c", c=64)
            V.tt(qv, a[:, o:o + 8, :], cv, MUL, tl, qf)
            t = V.tt(qv, qv, u, SUB)
            bi, ps, free = self.ps.get()
            t = T.mm(ps, pw[:, g, :], q, True, True, t, free, tl, inc=True)
            pl.done(i, t)
            self.ps.done(bi, V.ts(mx[:, g, :], ps, n2[:, 25 + g:26 + g], None, MUL, None, t))
        tm = V.last()
        self.linT(og, D["w_gla"], 0, 4, 0, 1024, LAT,
                  lambda m, pi, ps, tok: V.tt(mg[:, m, :], mg[:, m, :], ps, MUL, tok, S.last()), tm)
        self.linT(mx, D["w_poolp"], 0, 4, 0, 1024, LAT,
                  lambda m, pi, ps, tok: V.tt(mg[:, 8 + m, :], mg[:, 8 + m, :], ps, MUL, tok), tm)
        for m in range(8):
            t = V.tt(mg[:, m, :], mg[:, m, :], mg[:, 8 + m, :], ADD)
        self.linT(mg, D["w_out_2"], 0, 8, 0, 1024, LAT,
                  lambda m, pi, ps, tok: V.stt(X[:, m, :], ps, LP[:, 16 + m:17 + m], X[:, m, :], MUL, ADD, tok), t)
        tx = V.last()
        self.fence()
        self.top = low
        self.moe(LP, tx)
        self.fence()
        self.top = low
        o = self.alloc(8, 512)
        self.modulate(o, X, 512, n2[:, 16:24], None, V.last())
        self.finish(o, V.last())

    def gla(self, h, og, th, n2):
        D, T, V, S, G = self.D, self.T, self.V, self.S, self.G
        W = D["w_in_2"]
        BOTH, LAT = [(0, 512), (512, 768)], [(0, 512)]
        kT, vR, qT = self.alloc(2, 768), self.alloc(6, 512), self.alloc(2, 512)
        rl = self.alloc(2, 768)
        gs = self.alloc(4, 512)
        rw = self.alloc(8, 32)
        du = self.alloc(2, 256)
        cn = {n: self.const(n) for n in ("r64", "le64", "ge64")}
        self.load(rw, W[:, 768:800].rearrange("(k p) c -> p k c", p=128))
        self.load(du[0:16, :, :], D["dup"].rearrange("d r c -> r d c"))
        tl = self.all_loads()

        def cpT(dst):
            def ev(m, pi, ps, tok):
                a, b = BOTH[pi]
                return S.cp(dst[:, m, a:b], ps, tok)
            return ev

        self.linT(h, W, 0, 8, 0, 256, BOTH, cpT(kT), th)
        self.linR(h, 6, W, 8, 256, 512, lambda x, ps, tok: S.cp(vR[:, x, :], ps, tok), th)
        for d in range(2):
            for a, b in BOTH:
                bi, ps, free = self.ps.get()
                for k in range(8):
                    t = T.mm(ps[0:16, 0:b - a], rw[:, k, d * 16:d * 16 + 16], h[:, k, a:b], k == 0, k == 7, free, tl,
                             inc=(k == 7))
                self.ps.done(bi, S.cp(rl[0:16, d, a:b], ps[0:16, 0:b - a], t))
        self.linT(h, W, 0, 8, 800, 256, LAT,
                  lambda m, pi, ps, tok: S.f(qT[:, m, :], ps, ACT.Copy, tok, scale=0.125), th)

        def ev_g(m, pi, ps, tok):
            t = S.f(gs[:, m, :], ps, ACT.Sigmoid, tok)
            return V.tt(gs[:, m, :], gs[:, m, :], ps, MUL, t)

        self.linT(h, W, 0, 8, 1056, 512, LAT, ev_g, th)
        t0 = S.last()
        q1 = self.alloc(4, 512)
        ST = [self.alloc(8, 128) for _ in range(4)]
        SC = [self.alloc(4, 128) for _ in range(8)]
        for s in SC:
            V.set(s, 0.0, t0)
        la, B, kw, KW = self.alloc(768), self.alloc(768), self.alloc(768), self.alloc(6, 128)
        qm, km = self.alloc(512), self.alloc(512)
        e1 = self.alloc(768)
        mid, dec = self.alloc(12), self.alloc(12)
        tmp = self.sbring(2, 128)
        U32 = mybir.dt.uint32
        c6 = lambda v: v.rearrange("p (c t) -> p c t", t=64)
        for d in range(2):
            for m in range(2):
                dm = 2 * d + m
                for a, b in BOTH:
                    bi, ps, free = self.ps.get()
                    t = T.mm(ps[:, 0:b - a], du[0:16, d, m * 128:m * 128 + 128], rl[0:16, d, a:b], True, True, free, tl,
                             S.last(), inc=True)
                    t = V.ts(la[:, a:b], ps[:, 0:b - a], n2[:, 29 + dm:30 + dm], None, ADD, None, t)
                    self.ps.done(bi, t)
                t = S.f(e1, la, ACT.Abs, t)
                S.f(e1, e1, ACT.Exp, scale=-1.0)
                t = S.f(e1, e1, ACT.Ln, bias=1.0)
                V.stt(la, la, 0.0, e1, MIN, SUB, t)
                if d == 0:
                    V.scan(B, cn["r64"], la, tl)
                    me, en = 31, 63
                else:
                    V.scan(B[:, ::-1], cn["r64"], la[:, ::-1], tl)
                    me, en = 32, 0
                end = c6(B)[:, :, en:en + 1].to_broadcast([128, 12, 64])
                t = V.tt(c6(e1), end, c6(B), SUB)
                t = S.f(e1, e1, ACT.Exp, t, scale=1.0 / 16)
                S.f(dec, c6(B)[:, :, en], ACT.Exp, scale=1.0 / 16)
                t1 = S.f(q1[:, dm, :], B[:, 0:512], ACT.Exp, scale=1.0 / 16)
                tk = V.tt(kw, kT[:, m, :], e1, MUL, t)
                V.tt(q1[:, dm, :], q1[:, dm, :], qT[:, m, :], MUL, t1)
                V.cp(mid, c6(B)[:, :, me])
                t = V.tt(c6(B[:, 0:512]), c6(B[:, 0:512]), mid[:, 0:8, None].to_broadcast([128, 8, 64]), SUB)
                t1 = S.f(qm, B[:, 0:512], ACT.Exp, t, T.last(), scale=1.0 / 16)
                t2 = S.f(km, B[:, 0:512], ACT.Exp, scale=-1.0 / 16)
                V.tt(qm, qm, qT[:, m, :], MUL, t2)
                tq = V.tt(km, km, kT[:, m, 0:512], MUL)
                for x0, x1 in ((0, 4), (4, 6)):
                    bi, ps, free = self.ps.get()
                    for x in range(x0, x1):
                        t = T.tr(ps[:, (x - x0) * 128:(x - x0) * 128 + 128], kw[:, x * 128:x * 128 + 128], self.ident,
                                 free, tk, inc=(x == x1 - 1))
                    t = S.cp(KW[:, x0:x1, :], ps[:, 0:(x1 - x0) * 128].rearrange("p (x c) -> p x c", c=128), t)
                    self.ps.done(bi, t)
                kv = {}
                banks = {}
                for grp in ("ctx", "lat"):
                    xs = (4, 5) if grp == "ctx" else (0, 1, 2, 3)
                    for par in range(2):
                        bi, ps, free = self.ps.get()
                        r = slice(64 * par, 64 * par + 64)
                        for x in xs:
                            cc = (x - xs[0]) * 128
                            for hh in range(2):
                                o = 64 * hh
                                hd = 2 * m + hh
                                t1 = T.mm(ps[o:o + 64, cc:cc + 128], KW[r, x, o:o + 64], vR[r, x, hd * 128:hd * 128 + 128],
                                          True, True, t, free, inc=(x == xs[-1] and hh == 1))
                        for x in xs:
                            cc = (x - xs[0]) * 128
                            kv[2 * x + par] = (ps[:, cc:cc + 128], t1)
                        banks[grp, par] = bi
                order = [8, 9, 10, 11, 0, 1, 2, 3, 4, 5, 6, 7] if d == 0 else [11, 10, 9, 8, 7, 6, 5, 4, 3, 2, 1, 0]
                prev = None
                for n, x in enumerate(order):
                    if n == 11:
                        break
                    nx = order[n + 1]
                    if nx < 8:
                        dst, i = ST[dm][:, nx, :], None
                        tf = None
                    else:
                        i, dst, tf = tmp.get()
                    ps, tkv = kv[x]
                    if prev is None:
                        t = V.cp(dst, ps, tkv, tf)
                    else:
                        t = V.stt(dst, prev, dec[:, x:x + 1], ps, MUL, ADD, tkv, tf)
                    if i is not None:
                        tmp.done(i, t)
                    prev = dst
                for b in banks.values():
                    self.ps.done(b, V.last())
                mask = cn["le64" if d == 0 else "ge64"]
                for hh in range(2):
                    o = slice(64 * hh, 64 * hh + 64)
                    bi, ps, free = self.ps.get()
                    for x in range(4):
                        c = slice(x * 128, x * 128 + 128)
                        t = T.mm(ps[:, c], km[o, c], qm[o, c], True, True, tq, free, inc=(x == 3))
                    sc = SC[4 * d + 2 * m + hh]
                    mk = mask.bitcast(U32)[:, None, :].to_broadcast([128, 4, 128])
                    pv = ps.rearrange("p (x c) -> p x c", x=4)
                    t = V.add(lambda e, sc=sc, mk=mk, pv=pv: e.copy_predicated(sc, mk, pv), t)
                    self.ps.done(bi, t)
                V.wait(T.last()), S.wait(T.last())
        ts = V.last()
        ob = Ring([la[:, 0:512], B[:, 0:512]])
        sb2 = Ring([e1[:, 0:512], kw[:, 0:512]])
        for ring in (ob, sb2):
            for i in range(2):
                ring.done(i, ts)
        for hd in range(4):
            m, hh = hd // 2, hd % 2
            o = slice(64 * hh, 64 * hh + 64)
            bi, ps, free = self.ps.get()
            for x in range(4):
                c = slice(x * 128, x * 128 + 128)
                T.mmx(ps[:, c], vR[:, x, hd * 128:hd * 128 + 128], SC[hd][:, x, :], True, False, ts, free)
                T.mmx(ps[:, c], vR[:, x, hd * 128:hd * 128 + 128], SC[4 + hd][:, x, :], False, False)
                for d in range(2):
                    for n in (2 * x, 2 * x + 1):
                        t = T.mmx(ps[:, n * 64:n * 64 + 64], ST[2 * d + m][o, n, :], q1[o, 2 * d + m, n * 64:n * 64 + 64],
                                  False, d == 1, inc=(d == 1 and n % 2 == 1))
            i, q, qf = ob.get()
            j, s, sf = sb2.get()
            t1 = S.cp(q, ps, t, qf)
            self.ps.done(bi, t1)
            t2 = S.f(s, q, ACT.Square, sf)
            bi, ps, free = self.ps.get()
            t = T.mm(ps, self.ones, s, True, True, t2, free, inc=True)
            ta, tb = self.rstd(s, ps, 128, 1e-6, t, s)
            self.ps.done(bi, ta)
            V.stt(q, q, n2[:, 24:25], s, MUL, MUL, tb)
            t = V.tt(og[:, hd, :], q, gs[:, hd, :], MUL)
            ob.done(i, t)
            sb2.done(j, t)

    def moe(self, LP, tx):
        D, T, V, S, G = self.D, self.T, self.V, self.S, self.G
        X = self.X
        Y = self.alloc(8, 1024)
        y_at = self.top - 8192
        keep = self.top
        self.top = y_at
        Sel = self.alloc(4, 16, 64)
        hR = self.alloc(4, 1024)
        self.top = keep
        SW = self.alloc(8, 512)
        xs = self.alloc(8, 1024)
        mark = self.top
        h = self.alloc(8, 512)
        th, _ = self.modulate(h, X, 512, LP[:, 32:40], LP[:, 24:32], tx)
        self.fence()
        rt = self.alloc(8, 16)
        io, slot, e2 = self.const("iota64"), self.const("slot"), self.const("e2")
        e2 = e2.rearrange("p (g c) -> p g c", g=8)
        self.load(rt, D["router"].rearrange("(k p) c -> p k c", p=128))
        tl = self.all_loads()
        af = self.alloc(4, 16)
        z = self.alloc(4, 4)
        aT, wk, ms, rk, on = (self.alloc(512) for _ in range(5))
        m8 = self.alloc(8)
        rT = self.alloc(4, 16)
        for x in range(4):
            bi, ps, free = self.ps.get()
            for k in range(8):
                t = T.mm(ps[:, 0:16], h[:, k, x * 128:x * 128 + 128], rt[:, k, :], k == 0, k == 7, free, tl, th,
                         inc=(k == 7))
            V.red(z[:, x, 0:1], ps[:, 0:16], MAX, t, neg=True)
            t = V.ts(af[:, x, :], ps[:, 0:16], z[:, x, 0:1], None, ADD, None)
            self.ps.done(bi, t)
            t = S.f(af[:, x, :], af[:, x, :], ACT.Exp, t, acc=z[:, x, 1:2])
            V.rec(z[:, x, 2:3], z[:, x, 1:2], t)
            t = V.ts(af[:, x, :], af[:, x, :], z[:, x, 2:3], None, MUL, None)
            bi, ps, free = self.ps.get()
            t = T.tr(ps[0:16, 0:128], af[:, x, :], self.ident, t, free, inc=True)
            t = V.cp(aT[0:16, x * 128:x * 128 + 128], ps[0:16, 0:128], t)
            self.ps.done(bi, t)
        a16, w16, m16, r16 = aT[0:16, :], wk[0:16, :], ms[0:16, :], rk[0:16, :]
        V.cp(w16, a16)
        for r in range(8):
            V.add(lambda e: e.max(m8[0:16, :], w16))
            V.add(lambda e: e.match_replace(w16, m8[0:16, :], w16, -1.0))
        V.ts(m16, w16, -1.0, None, EQ, None)
        V.set(on[0:16, :], 1.0)
        V.scan(r16, on[0:16, :], m16)
        V.tt(r16, r16, m16, MUL)
        t = V.ts(r16, r16, -1.0, None, ADD, None)
        bi, ps, free = self.ps.get()
        for x in range(4):
            t1 = T.tr(ps[:, x * 16:x * 16 + 16], rk[0:16, x * 128:x * 128 + 128], self.ident[0:16, 0:16], t, free,
                      inc=(x == 3))
        t1 = V.cp(rT, ps[:, 0:64].rearrange("p (x e) -> p x e", x=4), t1)
        self.ps.done(bi, t1)
        for x in range(4):
            tsel = V.tt(Sel[:, x, :, :], rT[:, x, :, None].to_broadcast([128, 16, 64]),
                        io[:, None, :].to_broadcast([128, 16, 64]), EQ, tl)
        ab = self.sbring(2, 512)
        for g in range(8):
            i, a, af_ = ab.get()
            bi, ps, free = self.ps.get()
            t1 = T.mm(ps, e2[0:16, g, :], aT[0:16, :], True, True, free, t, tl, inc=True)
            t1 = S.cp(a, ps, t1, af_)
            self.ps.done(bi, t1)
            bi, ps, free = self.ps.get()
            t2 = T.mm(ps, e2[0:16, g, :], rk[0:16, :], True, True, free, inc=True)
            t2 = V.stt(SW[:, g, :], ps, slot[:, 0:1], a, EQ, MUL, t2, t1)
            self.ps.done(bi, t2)
            ab.done(i, t2)
        tsw = V.last()
        for x in range(4):
            for k0 in (0, 4):
                bi, ps, free = self.ps.get()
                for k in range(4):
                    t = T.tr(ps[:, k * 128:k * 128 + 128], h[:, k0 + k, x * 128:x * 128 + 128], self.ident, free,
                             inc=(k == 3))
                t = S.cp(hR[:, x, k0 * 128:k0 * 128 + 512], ps, t)
                self.ps.done(bi, t)
        th = S.last()
        for k in range(8):
            for eg in range(2):
                bi, ps, free = self.ps.get()
                for x in range(4):
                    t = T.mm(ps, hR[:, x, k * 128:k * 128 + 128],
                             Sel[:, x, eg * 8:eg * 8 + 8, :].rearrange("p e s -> p (e s)"), x == 0, x == 3, free, th, tsel,
                             inc=(x == 3))
                t = V.cp(xs[:, k, eg * 512:eg * 512 + 512], ps, t)
                self.ps.done(bi, t)
        txs = V.last()
        self.fence()
        self.top = mark
        ac = self.sbring(2, 1024)
        aTr = self.sbring(2, 8, 64)
        for e in range(16):
            i, a, aw = ac.get()
            for c in range(2):
                pss = []
                for w in (D["wg"], D["wu"]):
                    wi, wp, tw = self.panel(w[e][:, c * 512:c * 512 + 512], 8, 512)
                    bi, ps, free = self.ps.get()
                    for k in range(8):
                        t = T.mm(ps[0:64, :], xs[:, k, e * 64:e * 64 + 64], wp[:, k, :], k == 0, k == 7, free, tw, txs,
                                 inc=(k == 7))
                    self.wring.done(wi, t)
                    pss.append((bi, ps, t))
                (b1, p1, t1), (b2, p2, t2) = pss
                av = a[0:64, c * 512:c * 512 + 512]
                t = S.f(av, p1[0:64, :], ACT.Sigmoid, t1, aw)
                t = V.tt(av, av, p1[0:64, :], MUL, t)
                self.ps.done(b1, t)
                t = V.tt(av, av, p2[0:64, :], MUL, t2)
                self.ps.done(b2, t)
            j, at_, jw = aTr.get()
            bi, ps, free = self.ps.get()
            for k in range(8):
                t1 = T.tr(ps[:, k * 64:k * 64 + 64], a[0:64, k * 128:k * 128 + 128], self.ident[0:64, 0:64], t, free,
                          inc=(k == 7))
            ac.done(i, t1)
            t = S.cp(at_, ps.rearrange("p (k s) -> p k s", k=8), t1, jw)
            self.ps.done(bi, t)
            o = 64 * (e % 2)
            for c in range(2):
                wi, wp, tw = self.panel(D["wd"][e][:, c * 512:c * 512 + 512], 8, 512)
                bi, ps, free = self.ps.get()
                for k in range(8):
                    t1 = T.mm(ps[o:o + 64, :], at_[:, k, :], wp[:, k, :], k == 0, k == 7, free, tw, t, inc=(k == 7))
                self.wring.done(wi, t1)
                t2 = V.cp(Y[o:o + 64, e // 2, c * 512:c * 512 + 512], ps[o:o + 64, :], t1)
                self.ps.done(bi, t2)
            aTr.done(j, t1)
        ty = V.last()
        for m in range(8):
            bi, ps, free = self.ps.get()
            for g in range(8):
                t = T.mm(ps, Y[:, g, m * 128:m * 128 + 128], SW[:, g, :], g == 0, g == 7, free, ty, tsw, inc=(g == 7))
            t = V.stt(X[:, m, :], ps, LP[:, 40 + m:41 + m], X[:, m, :], MUL, ADD, t)
            self.ps.done(bi, t)


def program(nc, D, out, stages=("L0", "L1", "L2")):
    Program(nc, D, stages, out).build()


def kernel(**inputs):
    import concourse.bacc as bacc
    from concourse.bass_utils import run_bass_kernel_spmd

    nc = bacc.Bacc("TRN2", target_bir_lowering=False, num_devices=1)
    arrays = layout_inputs(inputs)
    D = {n: nc.dram_tensor("in_" + n, a.shape, F32, kind="ExternalInput").ap() for n, a in arrays.items()}
    out = nc.dram_tensor("out_T", (1024, 512), F32, kind="ExternalOutput").ap()
    program(nc, D, out)
    r = run_bass_kernel_spmd(nc, [{"in_" + n: a for n, a in arrays.items()}], core_ids=[0])
    return np.ascontiguousarray(r.results[0]["out_T"].T).reshape(1, 512, 1024)
```

```python
from contextlib import ExitStack

import numpy as np
import concourse.bass as bass
from concourse import mybir

F32 = mybir.dt.float32
F32R = mybir.dt.float32r
ALU = mybir.AluOpType
ACT = mybir.ActivationFunctionType
AX = mybir.AxisListType
MUL, ADD, SUB, MAX, MIN = ALU.mult, ALU.add, ALU.subtract, ALU.max, ALU.min
EQ, GE, GT = ALU.is_equal, ALU.is_ge, ALU.is_gt
NR = 3
TOTAL = 53200
LOW = 18304
NEG = -1.0e30


class Queue:

    def __init__(self, sem, chained):
        self.sem, self.n, self.items, self.seen, self.chained = sem, 0, [], {}, chained
        self.key, self.base, self.lasts = None, 0, {}

    def wait(self, *tokens):
        for t in tokens:
            if isinstance(t, (list, tuple)) and not (len(t) == 2 and isinstance(t[1], int)):
                self.wait(*t)
            elif t is not None and self.seen.get(id(t[0]), 0) < t[1]:
                self.seen[id(t[0])] = t[1]
                self.items.append((t[0], t[1]))

    def add(self, fn, *tokens, inc=True):
        self.wait(*tokens)
        if self.chained:
            self.wait(self.last())
        if inc:
            self.n += 1
            self.lasts[self.key] = self.n
        self.items.append((fn, inc))
        return (self.sem, self.n) if inc else None

    def last(self):
        v = self.lasts.get(self.key, self.base)
        return (self.sem, v) if v else None

    def everything(self):
        return (self.sem, self.n) if self.n else None

    def play(self, e):
        for a, b in self.items:
            if callable(a):
                i = a(e)
                if b is True:
                    i.then_inc(self.sem, 1)
            else:
                e.wait_ge(a, b)


class Vec(Queue):
    def tt(self, o, a, b, op, *w, **k):
        return self.add(lambda e: e.tensor_tensor(o, a, b, op), *w, **k)

    def ts(self, o, a, s1, s2, op0, op1, *w, **k):
        if s2 is None:
            return self.add(lambda e: e.tensor_scalar(o, a, s1, None, op0), *w, **k)
        return self.add(lambda e: e.tensor_scalar(o, a, s1, s2, op0, op1), *w, **k)

    def stt(self, o, a, s, b, op0, op1, *w, **k):
        return self.add(lambda e: e.scalar_tensor_tensor(out=o, in0=a, scalar=s, in1=b, op0=op0, op1=op1), *w, **k)

    def cp(self, o, a, *w, **k):
        return self.add(lambda e: e.tensor_copy(o, a), *w, **k)

    def rec(self, o, a, *w, **k):
        return self.add(lambda e: e.reciprocal(o, a), *w, **k)

    def red(self, o, a, op, *w, neg=False, **k):
        return self.add(lambda e: e.tensor_reduce(o, a, AX.X, op, negate=neg), *w, **k)

    def scan(self, o, a, b, *w, **k):
        return self.add(lambda e: e.tensor_tensor_scan(o, a, b, 0.0, MUL, ADD), *w, **k)

    def set(self, o, v, *w, **k):
        return self.add(lambda e: e.memset(o, v), *w, **k)


class Act(Queue):

    def __init__(self, sem, chained, nc):
        super().__init__(sem, chained)
        self.nc, self.ln_exp = nc, False

    def tables(self, fn):
        if fn in (ACT.Ln, ACT.Exp) and not self.ln_exp:
            self.items.append((lambda e: e.add_instruction(mybir.InstLoadActFuncSet(
                name=self.nc.get_next_instruction_name(), engine=e.engine, act_func_set_id=6)), False))
            self.ln_exp = True
        if fn in (ACT.Sigmoid, ACT.Tanh, ACT.Sqrt):
            self.ln_exp = False

    def fine_ln(self, o, a, *w, **k):
        self.wait(*w)
        self.items.append((lambda e: e.add_instruction(mybir.InstLoadActFuncSet(
            name=self.nc.get_next_instruction_name(), engine=e.engine, act_func_set_id=5)), False))
        self.ln_exp = True
        t = self.f(o, a, ACT.Ln, **k)
        self.ln_exp = False
        return t

    def f(self, o, a, fn, *w, bias=0.0, scale=1.0, acc=None, **k):
        self.wait(*w)
        self.tables(fn)
        if acc is not None:
            return self.add(lambda e: e.activation(o, a, fn, bias=bias, scale=scale, accum_out=acc), *w, **k)
        return self.add(lambda e: e.activation(o, a, fn, bias=bias, scale=scale), *w, **k)

    def cp(self, o, a, *w, **k):
        return self.add(lambda e: e.activation(o, a, ACT.Copy), *w, **k)


class Ten(Queue):
    def mm(self, o, l, r, start, stop, *w, inc=False):
        return self.add(lambda e: e.matmul(o, l, r, start=start, stop=stop), *w, inc=inc)

    def mmx(self, o, l, r, start, stop, *w, inc=False):
        return self.add(lambda e: e.matmul(o, l, r, start=start, stop=stop, skip_group_check=True), *w, inc=inc)

    def tr(self, o, a, ident, *w, inc=False):
        return self.add(lambda e: e.transpose(o, a, ident), *w, inc=inc)


class Ring:

    def __init__(self, bufs):
        self.bufs, self.free, self.order = bufs, [[] for _ in bufs], list(range(len(bufs)))

    def get(self):
        i = self.order.pop(0)
        return i, self.bufs[i], self.free[i]

    def done(self, i, *tokens):
        self.free[i] = [t for t in tokens if t is not None]
        self.order.append(i)


def layout_constants():
    cols, at = [], {}

    def put(name, a):
        a = np.asarray(a, np.float32).reshape(128, -1)
        at[name] = (sum(c.shape[1] for c in cols), a.shape[1])
        cols.append(a)

    i = np.arange(128)
    ident = np.eye(128)
    put("ident", ident)
    put("ones", np.ones((128, 128)))
    four = np.zeros((128, 2))
    four[[0, 32, 64, 96], 0] = four[[1, 33, 65, 97], 1] = 1
    put("four", four)
    put("blk", (i[:, None] // 64 == i[None, :] // 64))
    le = (i[:, None] <= i[None, :]).astype(np.float32)
    put("le", le)
    put("ge", le.T)
    put("lt", le - ident)
    put("gt", le.T - ident)
    put("mle", np.where(le > 0, 0.0, NEG))
    put("mge", np.where(le.T > 0, 0.0, NEG))
    c = i % 64
    st = np.clip(c - 8, 0, 48)[:, None]
    j = np.arange(64)[None, :]
    put("nam", np.where((j >= st) & (j < st + 16), 0.0, NEG))
    b16 = (i[:, None] // 16 == i[None, :] // 16)
    b32 = (i[:, None] // 32 == i[None, :] // 32)
    b64 = (i[:, None] // 64 == i[None, :] // 64)
    up = le - ident
    dn = up.T
    for n, m in (("0", b16), ("1", b32 & ~b16), ("2", b64 & ~b32), ("3", ~b64)):
        put("u" + n, up * m)
        put("d" + n, dn * m)
    put("le64", le * b64)
    put("ge64", le.T * b64)
    tok = np.arange(512)
    inv = 10000.0 ** (-np.arange(32, dtype=np.float32) / 32)
    ang = np.stack([(tok // 64)[:, None] * inv, (tok % 64)[:, None] * inv], 1)
    rope = np.stack([np.cos(ang), np.sin(ang)], 1).astype(np.float32)
    put("rope", rope.reshape(4, 128, 2 * 2 * 32).transpose(1, 0, 2))
    t = np.arange(768)
    put("r128", np.broadcast_to(t % 128 != 0, (128, 768)))
    put("r64", np.broadcast_to(t % 64 != 0, (128, 768)))
    cnt = []
    for w in (2, 4, 8, 16):
        q = np.arange(64)
        cc = np.clip(q + w // 2, 0, 64) - np.clip(q - w // 2, 0, 64)
        q = np.arange(8)
        cr = np.clip(q + w // 2, 0, 8) - np.clip(q - w // 2, 0, 8)
        cnt.append(1.0 / (cr[:, None] * cc[None, :]))
    put("cnt", np.broadcast_to(np.stack(cnt).reshape(1, -1), (128, 2048)))
    put("iota64", np.broadcast_to(np.arange(64), (128, 64)))
    put("slot", np.stack([i % 64, i % 64], 1))
    e2 = np.zeros((128, 8, 128))
    for p in range(8):
        for q in range(128):
            e2[2 * p + q // 64, p, q] = 1
    put("e2", e2)
    return np.concatenate(cols, 1).astype(np.float32), at


def column(v, n):
    return np.ascontiguousarray(np.asarray(v).reshape(n, 128).T)


def layout_inputs(a):
    A = {k: np.asarray(v) for k, v in a.items()}
    o = {}
    o["xT"] = np.ascontiguousarray(A["x"][0].T)
    o["ctxT"] = np.ascontiguousarray(A["ctx"][0].T)
    o["ctx2T"] = np.ascontiguousarray(A["ctx_2"][0].T)
    o["cc"] = np.stack([column(A["c"][0], 8), column(A["c_ctx"], 8),
                        column(A["c_2"][0], 8), column(A["c_ctx_2"], 8)], 2)
    o["ada_w"] = A["ada_w"]
    o["ada_w_2"] = A["ada_w_2"]
    o["ada_b"] = np.concatenate([column(A["ada_b"][0], 48), column(A["ada_b"][1], 48),
                                 column(A["ada_b_2"][0], 48)], 1)
    o["ab_w_in"] = A["ab_w_in"][0]
    o["ab_w_out"] = A["ab_w_out"][0]
    o["gate_b"] = np.broadcast_to(A["ab_gate_b"][0][None], (128, 16))
    o["qkn"] = np.stack([np.tile(A["na_q_norm"][0], 2), np.tile(A["na_k_norm"][0], 2)], 1)
    rp = np.pad(A["na_rpb"][0], ((0, 0), (0, 0), (64, 64)))
    wide = np.stack([rp[:, :, 79 - c:143 - c] for c in range(64)], 1)
    o["rpb"] = np.concatenate([wide[:, :, 1:15], wide[:, :, 0:14]], 1)
    o["hn"] = np.ascontiguousarray(A["ml_head_norm"][0].T)
    o["mu"] = np.concatenate([column(A["rw_mu"][0, s], 8) for s in range(6)], 1)
    o["rkv"] = A["rw_w_rkv"][0]
    o["w0a0"] = np.concatenate([column(A["rw_w0"][0, 0], 8), column(A["rw_w0"][0, 1], 8),
                                column(A["rw_a0"][0, 0], 8), column(A["rw_a0"][0, 1], 8)], 1)
    o["w1"] = A["rw_w1"][0]
    o["w2"] = A["rw_w2"][0].reshape(128, 1024)
    o["a1"] = A["rw_a1"][0]
    o["a2"] = A["rw_a2"][0].reshape(128, 1024)
    o["g1"] = A["rw_g1"][0]
    o["g2"] = A["rw_g2"][0]
    o["rwv"] = np.concatenate([column(A[n][0], 8) for n in
                               ("rw_k_k", "rw_k_a", "rw_r_k", "rw_lnx_w", "rw_lnx_b")], 1)
    o["w_o"] = A["rw_w_o"][0]
    o["mlp_w1"] = A["mlp_w1"]
    o["mlp_w2"] = A["mlp_w2"]
    o["n2"] = np.concatenate([column(A["norm1_g_2"][0], 8), column(A["norm2_g_2"][0], 8),
                              column(A["final_norm_g_2"], 8), column(A["gla_norm_g_2"][0], 1),
                              column(A["pool_scale_2"][0], 4), column(A["b_decay_2"][0, 0], 2),
                              column(A["b_decay_2"][0, 1], 2)], 1)
    o["w_in_2"] = A["w_in_2"][0]
    o["dup"] = A["w_decay_up_2"][0]
    o["w_gla"] = A["w_gla_proj_2"][0]
    o["pool_w"] = A["pool_w_2"][0]
    o["w_poolp"] = A["w_pool_proj_2"][0]
    o["w_out_2"] = A["w_out_2"][0]
    o["router"] = A["w_router_2"][0]
    o["wg"] = A["w_gate_e_2"][0]
    o["wu"] = A["w_up_e_2"][0]
    o["wd"] = A["w_down_e_2"][0]
    o["consts"] = layout_constants()[0]
    return {k: np.ascontiguousarray(v) for k, v in o.items()}


class Program:
    def __init__(self, nc, D, stages, out):
        self.nc, self.D, self.out = nc, D, out
        self.stages = stages

    def build(self):
        nc = self.nc
        with ExitStack() as ctx:
            self.ctx = ctx
            self.top, self.size, self.peak, self.starts, self.parts = 0, TOTAL, 0, [], []
            self.nparts = 0
            self.enter(LOW)
            self.psum = [ctx.enter_context(nc.psum_tensor(f"ps{i}", [128, 512], F32)) for i in range(8)]
            s = {n: ctx.enter_context(nc.semaphore("s_" + n)) for n in ("pe", "dve", "act", "pool", "sp")}
            self.T = Ten(s["pe"], False)
            self.V = Vec(s["dve"], True)
            self.S = Act(s["act"], True, nc)
            self.G = Vec(s["pool"], True)
            self.Q = Queue(s["sp"], False)
            self.ps = Ring([p[:, :] for p in self.psum])
            self.w_at = self.top
            self.wslots = [self.alloc(4096) for _ in range(NR)]
            self.wsem = [ctx.enter_context(nc.semaphore(f"s_w{i}")) for i in range(NR)]
            self.wcount = [0] * NR
            self.wring = Ring(self.wslots)
            self.lsem = [ctx.enter_context(nc.semaphore(f"s_l{i}")) for i in range(32)]
            self.lcount = [0] * 32
            self.li = self.hi = 0
            self.spill = nc.dram_tensor("spill", (128, 4096), F32, kind="Internal").ap()
            self.body()
            block = ctx.enter_context(nc.Block())
            for q, on in ((self.Q, block.sync), (self.T, block.tensor), (self.V, block.vector),
                          (self.S, block.scalar), (self.G, block.gpsimd)):
                on(self.player(q))
            while self.parts:
                self.leave()

    @staticmethod
    def player(q):
        def play(e):
            q.play(e)
        return play

    def enter(self, cols, dt=F32):
        at = sum(n for _, n, _, _ in self.parts)
        cm = self.nc.sbuf_tensor(f"part{self.nparts}", [128, cols], dt)
        self.nparts += 1
        self.parts.append((at, cols, cm.__enter__(), cm))
        self.top = at

    def leave(self):
        self.parts.pop()[3].__exit__(None, None, None)

    def alloc(self, *shape):
        n = int(np.prod(shape))
        at, cols, tensor, _ = next(p for p in self.parts if p[0] <= self.top < p[0] + p[1])
        if self.top + n > at + cols:
            raise RuntimeError(f"SBUF: {self.top + n} columns of {at + cols}")
        o = self.top
        self.top += n + n % 2
        self.peak = max(self.peak, self.top)
        if self.top > self.size:
            raise RuntimeError(f"SBUF: {self.top} columns of {self.size}")
        v = tensor[:, o - at:o - at + n]
        if len(shape) == 2:
            v = v.rearrange("p (a b) -> p a b", a=shape[0])
        if len(shape) == 3:
            v = v.rearrange("p (a b c) -> p a b c", a=shape[0], b=shape[1])
        self.starts.append((tensor, o - at, v))
        return v

    def sbring(self, n, *shape):
        return Ring([self.alloc(*shape) for _ in range(n)])

    def fence(self, slots=False):
        t = [q.everything() for q in (self.T, self.V, self.S, self.G)]
        t += [(s, c) for s, c in zip(self.lsem, self.lcount) if c]
        if slots:
            t += [(s, c) for s, c in zip(self.wsem, self.wcount) if c]
            self.Q.wait(t)
        for q in (self.T, self.V, self.S, self.G):
            q.wait(t)
            q.base, q.lasts = q.n, {}
        return t

    def slot(self, tokens):
        self.wsem.append(self.ctx.enter_context(self.nc.semaphore(f"s_w{len(self.wsem)}")))
        self.wcount.append(0)
        self.wring.bufs.append(self.alloc(4096))
        self.wring.free.append(tokens)
        self.wring.order.append(len(self.wsem) - 1)

    def load(self, dst, src, *w, q=None):
        if q is None:
            q = self.G
            i = self.li % 24
            self.li += 1
        else:
            i = 24 + self.hi % 8
            self.hi += 1
        sem = self.lsem[i]
        if self.lcount[i]:
            q.wait((sem, self.lcount[i]))
        self.lcount[i] += 16
        q.wait(*w)
        q.items.append((lambda e: e.dma_start(dst, src).then_inc(sem, 16), "dma"))
        return (sem, self.lcount[i])

    def panel(self, src, kt, cols):
        i, buf, w = self.wring.get()
        v = buf[:, 0:kt * cols].rearrange("p (k c) -> p k c", k=kt)
        self.Q.wait(w)
        self.wcount[i] += 16
        sem = self.wsem[i]
        s = src.rearrange("(k p) c -> p k c", p=128)
        self.Q.items.append((lambda e: e.dma_start(v, s).then_inc(sem, 16), "dma"))
        return i, v, (sem, self.wcount[i])

    @staticmethod
    def of(ready, k):
        return ready[k] if isinstance(ready, dict) else ready

    def linT(self, h, W, k0, kt, c0, ncol, parts, evac, ready, panel=512):
        last = None
        for c in range(0, ncol, panel):
            n = min(panel, ncol - c)
            i, w, tw = self.panel(W[k0:k0 + kt * 128, c0 + c:c0 + c + n], kt, n)
            for m in range(0, n, 128):
                mw = min(128, n - m)
                for pi, (a, b) in enumerate(parts):
                    bi, ps, free = self.ps.get()
                    for k in range(kt):
                        last = self.T.mm(ps[0:mw, 0:b - a], w[:, k, m:m + mw], h[:, k, a:b], k == 0, k == kt - 1,
                                         free, tw, self.of(ready, k), inc=(k == kt - 1))
                    self.ps.done(bi, evac((c + m) // 128, pi, ps[0:mw, 0:b - a], last))
            self.wring.done(i, last)
        return last

    def linR(self, h, tiles, W, kt, c0, n, evac, ready, starts=None):
        i, w, tw = self.panel(W[0:kt * 128, c0:c0 + n], kt, n)
        last = None
        for x in range(tiles):
            bi, ps, free = self.ps.get()
            for k in range(kt):
                o = starts[x] if starts else x * 128
                last = self.T.mm(ps[:, 0:n], h[:, k, o:o + 128], w[:, k, :], k == 0, k == kt - 1,
                                 free, tw, self.of(ready, k), inc=(k == kt - 1))
            self.ps.done(bi, evac(x, ps[:, 0:n], last))
        self.wring.done(i, last)
        return last

    def ada(self, W, ci, bi):
        out = self.mod[bi].rearrange("p j m -> p m j")
        nxt = self.panel(W[:, 0:512], 8, 512)
        for c in range(12):
            i, w, tw = nxt
            if c < 11:
                nxt = self.panel(W[:, c * 512 + 512:c * 512 + 1024], 8, 512)
            yield
            got = [self.ps.get() for _ in range(4)]
            for k in range(2):
                for j, (b, ps, free) in enumerate(got):
                    t = self.T.mm(ps[32 * j:32 * j + 32, :], self.sc[:, 4 * k + j, ci, :], w[:, 4 * k + j, :],
                                  k == 0, k == 1, free, tw, self.t_sc, inc=(k == 1))
                    if k == 1:
                        got[j] = (b, ps, t)
            self.wring.done(i, t)
            r, row, rf = self.rows.get()
            te = []
            for j, (b, ps, t) in enumerate(got):
                te.append((self.V if j % 2 else self.S).cp(row[32 * j:32 * j + 32, :], ps[32 * j:32 * j + 32, :], t, rf))
                self.ps.done(b, te[-1])
            yield
            b, ps, free = self.ps.get()
            for m in range(4):
                t = self.T.mm(ps[:, m * 2:m * 2 + 2], row[:, m * 128:m * 128 + 128], self.four, True, True, free, te,
                              inc=(m == 3))
            self.rows.done(r, t)
            t = self.V.tt(out[:, c * 4:c * 4 + 4, :], ps[:, 0:8].rearrange("p (m j) -> p m j", j=2),
                          self.adab[:, bi * 48 + c * 4:bi * 48 + c * 4 + 4, None].to_broadcast([128, 4, 2]),
                          ADD, t, self.t_par)
            self.ps.done(b, t)
            self.mod_done[bi] = (c, t)
            yield

    def background(self):
        if self.later:
            key = self.V.key
            if not self.turn(self.later[0], "ada"):
                self.later.pop(0)
            self.as_stream(key)

    def need(self, bi, c):
        while self.mod_done[bi] is None or self.mod_done[bi][0] < c:
            self.background()
        if c == 11:
            while self.later and len(self.later) > 2 - bi:
                self.background()
        return self.mod_done[bi][1]

    def rstd(self, dst, ps, n, eps, tok, fine=False):
        if fine:
            t = self.S.fine_ln(dst, ps, tok, scale=1.0 / n, bias=self.eps[:, 0:1])
        else:
            t = self.S.f(dst, ps, ACT.Ln, tok, scale=1.0 / n, bias=self.eps[:, 0:1])
        return t, self.S.f(dst, dst, ACT.Exp, scale=-0.5)

    def modulate(self, items, scratch, ready):
        T, V, S = self.T, self.V, self.S
        sq = Ring([scratch[:, j * 512:j * 512 + 512] for j in range(3)])
        at = 1536
        rs, tr = [], []
        V.wait(ready), S.wait(ready)
        for h, x, n, s1, sh in items:
            bi, ps, free = self.ps.get()
            for k in range(8):
                i, s, sf = sq.get()
                s = s[:, 0:n]
                t = V.tt(s, x[:, k, :], x[:, k, :], MUL, sf) if k % 2 else S.f(s, x[:, k, :], ACT.Square, sf)
                t = T.mm(ps[:, 0:n], self.ones, s, k == 0, k == 7, t, free, self.t_con, inc=True)
                sq.done(i, t)
            r = scratch[:, at:at + n]
            at += n
            t, t2 = self.rstd(r, ps[:, 0:n], 1024, 1e-6, t, fine=True)
            self.ps.done(bi, t)
            rs.append(r)
            tr.append(t2)
        done = {}
        for k in range(8):
            done[k] = []
            for (h, x, n, s1, sh), r, t2 in zip(items, rs, tr):
                t = V.stt(h[:, k, :], x[:, k, :], s1[:, k:k + 1], r, MUL, MUL, t2)
                if sh is not None:
                    t = S.f(h[:, k, :], h[:, k, :], ACT.Identity, t, bias=sh[:, k:k + 1])
                done[k].append(t)
        return done

    def split_tiles(self, products):
        S, V = self.S, self.V
        for W, k0 in products:
            for n in range(8):
                c, m = divmod(n, 4)
                if m == 0:
                    i, w, tw = self.panel(W[k0:k0 + 1024, c * 512:c * 512 + 512], 8, 512)
                j, (wh, wl), wf = self.WR.get()
                src = w[:, :, m * 128:m * 128 + 128]
                ts = S.cp(wh, src, tw, wf)
                tv = V.tt(wl, src, wh, SUB, ts, tw, wf)
                if m == 3:
                    self.wring.done(i, ts, tv)
                yield j, wh, wl, [ts, tv]

    def linS(self, h, tiles, made, parts, evac, ready):
        T = self.T
        hh, hl = h
        kt = 8
        for n in range(8):
            j, wh, wl, tw = made.pop(0)
            got = []
            for a, b in parts:
                bi, ps, free = self.ps.get()
                for k in range(kt):
                    T.mm(ps[:, 0:b - a], wh[:, k, :], hh[:, k, a:b], k == 0, False, free, tw, self.of(ready, k))
                    T.mm(ps[:, 0:b - a], wh[:, k, :], hl[:, k, a:b], False, False)
                    last = T.mm(ps[:, 0:b - a], wl[:, k, :], hh[:, k, a:b], False, k == kt - 1, inc=(k == kt - 1))
                got.append((bi, ps[:, 0:b - a], last))
            self.WR.done(j, last)
            nxt = next(tiles, None)
            if nxt:
                made.append(nxt)
            for pi, (bi, ps, t) in enumerate(got):
                self.ps.done(bi, evac(n, pi, ps, t))
        return last

    def mlp(self, l, items):
        V, S, T = self.V, self.S, self.T
        self.fence()
        at, cols, _, _ = self.parts[-1]
        self.leave()
        self.enter(3840)
        scratch = self.alloc(2304)
        tmp = self.sbring(3, 512)
        self.enter(cols - 3840, F32R)
        n = sum(T_ for _, T_, _ in items)
        h = (self.alloc(8, n), self.alloc(8, n))
        hid = (self.alloc(8, n), self.alloc(8, n))
        self.WR = Ring([(self.alloc(8, 128), self.alloc(8, 128)) for _ in range(2)])
        parts, o = [], 0
        for _, T_, _ in items:
            parts.append((o, o + T_))
            o += T_
        W1, W2 = self.D["mlp_w1"][l], self.D["mlp_w2"][l]
        tiles = self.split_tiles([p for q in range(4) for p in ((W1[:, q * 1024:q * 1024 + 1024], 0), (W2, q * 1024))])
        made = [next(tiles), next(tiles)]
        sq = Ring([scratch[:, j * 512:j * 512 + 512] for j in range(3)])
        rs, tr, o = [], [], 1536
        for x, T_, p in items:
            bi, ps, free = self.ps.get()
            for k in range(8):
                i, s, sf = sq.get()
                s = s[:, 0:T_]
                t = V.tt(s, x[:, k, :], x[:, k, :], MUL, sf) if k % 2 else S.f(s, x[:, k, :], ACT.Square, sf)
                t = T.mm(ps[:, 0:T_], self.ones, s, k == 0, k == 7, t, free, inc=True)
                sq.done(i, t)
            r = scratch[:, o:o + T_]
            o += T_
            t, t2 = self.rstd(r, ps[:, 0:T_], 1024, 1e-6, t, fine=True)
            self.ps.done(bi, t)
            rs.append(r)
            tr.append(t2)
        ready = {}
        for k in range(8):
            ready[k] = []
            for (x, T_, p), (a, b), r, t in zip(items, parts, rs, tr):
                i, s, sf = tmp.get()
                s = s[:, 0:T_]
                t = V.stt(s, x[:, k, :], p[:, 32 + k:33 + k], r, MUL, MUL, t, sf)
                ts = S.f(h[0][:, k, a:b], s, ACT.Identity, t, bias=p[:, 24 + k:25 + k])
                tv = V.stt(h[1][:, k, a:b], s, p[:, 24 + k:25 + k], h[0][:, k, a:b], ADD, SUB, ts)
                tmp.done(i, ts, tv)
                ready[k] += [ts, tv]
        free = None
        for q in range(4):
            th = {m: [] for m in range(8)}

            def evac(m, pi, ps, tok):
                a, b = parts[pi]
                i, s, sf = tmp.get()
                s = s[:, 0:b - a]
                t = S.f(s, ps, ACT.Relu, tok, sf)
                tv = V.tt(s, s, s, MUL, t)
                ts = S.cp(hid[0][:, m, a:b], s, tv, free)
                tv = V.tt(hid[1][:, m, a:b], s, hid[0][:, m, a:b], SUB, ts, free)
                tmp.done(i, ts, tv)
                th[m] += [ts, tv]
                return t

            self.linS(h, tiles, made, parts, evac, ready)

            def evac2(m, pi, ps, tok):
                x, _, p = items[pi]
                return V.stt(x[:, m, :], ps, p[:, 40 + m:41 + m], x[:, m, :], MUL, ADD, tok)

            free = self.linS(hid, tiles, made, parts, evac2, th)
        self.fence()
        self.leave()
        self.leave()
        self.enter(cols)

    def body(self):
        D, T, V, S, G = self.D, self.T, self.V, self.S, self.G
        _, at = layout_constants()
        self.at = at

        def const(name, q=None):
            o, n = at[name]
            v = self.alloc(n)
            self.load(v, D["consts"][:, o:o + n], q=q)
            return v

        self.const = const
        self.ident, self.ones, self.blk = (const(n, self.Q) for n in ("ident", "ones", "blk"))
        self.four = const("four", self.Q)
        self.X = self.alloc(8, 512)
        adab = self.alloc(144)
        self.adab = adab
        cc = self.alloc(8, 4)
        self.load(adab, D["ada_b"], q=self.Q)
        self.load(cc, D["cc"], q=self.Q)
        self.load(self.X, D["xT"].rearrange("(k p) t -> p k t", p=128), q=self.Q)
        tl = self.all_loads()
        self.t_con = self.t_par = tl
        self.sc = self.alloc(8, 2, 32)
        sg = self.alloc(8, 4)
        t = S.f(sg, cc, ACT.Sigmoid, tl)
        V.set(self.sc, 0.0)
        for j in range(2):
            self.t_sc = V.tt(self.sc[:, :, j, 0:2], cc[:, :, 2 * j:2 * j + 2], sg[:, :, 2 * j:2 * j + 2], MUL, t, tl)
        V.wait(tl), T.wait(tl), G.wait(tl)
        self.rows = self.sbring(1, 512)
        self.eps = self.alloc(2)
        V.set(self.eps, 1e-6)
        S.wait(V.last())
        self.mod = [self.alloc(2, 48) for _ in range(3)]
        self.mod_done = [None] * 3
        for bi in range(3):
            for o in (8, 32):
                b = self.adab[:, bi * 48 + o:bi * 48 + o + 8]
                self.t_par = V.ts(b, b, 1.0, None, ADD, None, tl)
        self.later = []
        if "L0" in self.stages:
            self.later.append(self.ada(D["ada_w"][0], 0, 0))
        if "L0" in self.stages or "L1" in self.stages:
            self.later.append(self.ada(D["ada_w"][1], 0, 1))
        self.later.append(self.ada(D["ada_w_2"][0], 1, 2))
        if "L0" in self.stages or "L1" in self.stages:
            self.enter(2048)
            self.C = self.alloc(8, 256)
            tc = self.load(self.C, D["ctxT"].rearrange("(k p) t -> p k t", p=128))
            if "L0" in self.stages:
                self.enter(TOTAL - LOW - 2048)
                self.layer0(tc)
                self.fence()
                self.leave()
            if "L1" in self.stages:
                self.enter(TOTAL - LOW - 2048)
                self.layer1(tc)
                self.fence()
                self.leave()
            self.leave()
        if "L2" in self.stages:
            self.enter(TOTAL - LOW)
            self.block2()
        else:
            self.finish(self.X, self.V.last())

    def finish(self, x, tok):
        t = self.load(self.out.rearrange("(k p) t -> p k t", p=128), x, tok)
        self.Q.wait(t)

    def all_loads(self):
        return [(s, c) for s, c in zip(self.lsem, self.lcount) if c]

    def layer0(self, tc):
        D, T, V, S, G = self.D, self.T, self.V, self.S, self.G
        X, C = self.X, self.C
        p, tp = self.mod[0], self.need(0, 3)
        LP, CP = p[:, 0, :], p[:, 1, :]
        PARTS = [(0, 512), (512, 768)]
        self.h_at = self.top
        h = self.alloc(8, 768)
        cat = self.alloc(8, 768)
        flat = cat.rearrange("p k t -> p (k t)")
        th = self.modulate([(h[:, :, 0:512], X, 512, LP[:, 8:16], LP[:, 0:8]),
                            (h[:, :, 512:768], C, 256, CP[:, 8:16], CP[:, 0:8])], flat, [tp, tc])
        W = D["ab_w_in"]
        mark = self.top
        qk = self.alloc(8, 768)
        va = self.alloc(6, 512)
        qkn = self.alloc(2)
        nam = self.const("nam")
        self.load(qkn, D["qkn"])
        tl = self.all_loads()
        mark2 = self.top
        sq = self.sbring(2, 512)
        rr = self.sbring(2, 512)

        def ev_qk(m, pi, ps, tok):
            a, b = PARTS[pi]
            n = b - a
            i, s, sf = sq.get()
            j, r, rf = rr.get()
            t0 = V.cp(qk[:, m, a:b], ps, tok)
            t = S.f(s[:, 0:n], qk[:, m, a:b], ACT.Square, t0, sf)

            def norm():
                bi, p2, free = self.ps.get()
                t1 = T.mm(p2[:, 0:n], self.blk, s[:, 0:n], True, True, t, free, inc=True)
                ta, tb = self.rstd(r[:, 0:n], p2[:, 0:n], 64, 1e-6, [t1, rf])
                self.ps.done(bi, ta)
                g = qkn[:, 0:1] if m < 4 else qkn[:, 1:2]
                t2 = V.stt(qk[:, m, a:b], qk[:, m, a:b], g, r[:, 0:n], MUL, MUL, tb, tl)
                sq.done(i, t2)
                rr.done(j, t2)

            while len(late) > 0:
                late.pop(0)()
            late.append(norm)
            return t0

        late = []

        self.linT(h, W, 0, 8, 0, 1024, PARTS, ev_qk, th)
        late.pop(0)()
        self.linR(h, 6, W, 8, 1024, 512, lambda x, ps, tok: S.cp(va[:, x, :], ps, tok), th)
        tqk, tva = V.last(), S.last()
        self.fence()
        self.top = mark2
        SS = self.sbring(4, 768)
        PTr = self.sbring(4, 6, 128)
        BM = self.sbring(4, 14, 64)
        st = self.sbring(4, 4)
        DG = self.sbring(4, 128)

        def softmax_rows(n, parts_ps, tps, bias, tb):
            i, s, sf = SS.get()
            off = 0
            reads = []
            for (ps, w), bm in zip(parts_ps, bias):
                if bm is not None:
                    t = V.stt(s[:, off:off + w].rearrange("p (a b) -> p a b", b=64),
                              ps[:, 0:w].rearrange("p (a b) -> p a b", b=64), 0.125, bm, MUL, ADD, tps, tb, sf)
                else:
                    t = V.ts(s[:, off:off + w], ps[:, 0:w], 0.125, None, MUL, None, tps, sf)
                reads.append(t)
                off += w
            return i, s, t, reads

        def softmax_rest(s, n, t):
            k, z, zf = st.get()
            t = V.red(z[:, 0:1], s[:, 0:n], MAX, zf, neg=True)
            t = S.f(s[:, 0:n], s[:, 0:n], ACT.Exp, t, bias=z[:, 0:1], acc=z[:, 1:2])
            yield
            t = V.rec(z[:, 2:3], z[:, 1:2], t)
            j, dg, df = DG.get()
            t = V.ts(dg, self.ident, z[:, 2:3], None, MUL, None, df)
            st.done(k, t)
            return j, dg

        def head(hd):
            m, o = hd // 2, 64 * (hd % 2)
            bi, bm, bf = BM.get()
            tb = self.load(bm, D["rpb"][hd], bf)
            tb = V.tt(bm, bm, nam[:, None, :].to_broadcast([128, 14, 64]), ADD, tb, tl)
            for lat in (True, False):
                nq, nk = (4, 6) if lat else (2, 2)
                for qt in range(nq):
                    q0 = qt * 128 if lat else 512 + qt * 128
                    segs = [(0, 512), (512, 768)] if lat else [(512, 768)]
                    got = []
                    for a, b in segs:
                        x, ps, free = self.ps.get()
                        t = T.mm(ps[:, 0:b - a], qk[o:o + 64, m, q0:q0 + 128], qk[o:o + 64, 4 + m, a:b], True, True,
                                 free, tqk, inc=True)
                        got.append((x, ps, b - a))
                    bias = [bm[:, 6 - 2 * qt:14 - 2 * qt, :], None] if lat else [None]
                    si, s, tsm, reads = softmax_rows(128 * nk, [(ps, w) for _, ps, w in got], t, bias, tb)
                    for (x, _, _), r in zip(got, reads):
                        self.ps.done(x, r)
                    j, dg = yield from softmax_rest(s, 128 * nk, t)
                    tsm = V.last()
                    yield
                    pi, PT, pf = PTr.get()
                    tev = []
                    tt = None
                    for k0 in range(0, nk, 4):
                        kn = min(4, nk - k0)
                        x, ps, free = self.ps.get()
                        for k in range(kn):
                            tt = T.mm(ps[:, k * 128:k * 128 + 128], s[:, (k0 + k) * 128:(k0 + k) * 128 + 128], dg,
                                      True, True, free, tsm, inc=(k == kn - 1))
                        dst = PT[:, k0:k0 + kn, :]
                        sv = ps[:, 0:kn * 128].rearrange("p (k c) -> p k c", c=128)
                        te = (S if k0 == 0 else V).cp(dst, sv, tt, pf)
                        tev.append(te)
                        self.ps.done(x, te)
                    SS.done(si, tt)
                    DG.done(j, tt)
                    yield
                    x, ps, free = self.ps.get()
                    for k in range(nk):
                        kt = k if lat else 4 + k
                        t = T.mm(ps[o:o + 64, 0:128], va[:, kt, hd * 64:hd * 64 + 64], PT[:, k, :], k == 0, k == nk - 1,
                                 free, tev, tva, inc=(k == nk - 1))
                    PTr.done(pi, t)
                    self.ps.done(x, S.cp(cat[o:o + 64, m, q0:q0 + 128], ps[o:o + 64, 0:128], t))
            BM.done(bi, V.last())

        def heads(par):
            for hd in range(par, 8, 4):
                yield from head(hd)

        self.side_by_side([heads(i) for i in range(4)], leave=1)
        self.need(1, 11)
        self.fence()
        self.top = mark
        self.mlstm(h, cat, th)
        self.fence()
        self.top = mark

        def ev_o(m, pi, ps, tok):
            xs, g = (X, LP) if pi == 0 else (C, CP)
            return V.stt(xs[:, m, :], ps, g[:, 16 + m:17 + m], xs[:, m, :], MUL, ADD, tok)

        self.linT(cat, D["ab_w_out"], 0, 8, 0, 1024, PARTS, ev_o, [V.last(), S.last()])
        tx = V.last()
        self.mlp(0, [(X, 512, LP), (C, 256, CP)])

    def mlstm(self, h, cat, th):
        D, T, V, S, G = self.D, self.T, self.V, self.S, self.G
        W = D["ab_w_in"]
        R = 768
        kr = self.alloc(6, 512)
        vr = self.alloc(6, 512)
        og = self.alloc(4, 768)
        qT = self.alloc(4, 768)
        kT = self.alloc(4, 768)
        Gt = self.alloc(6, 16)
        cn = {n: self.const(n) for n in ("le", "ge", "mle", "mge")}
        gb, hn = self.alloc(16), self.alloc(4)
        mark = self.top
        gw = self.alloc(8, 16)
        rope = self.const("rope")
        rope = rope.rearrange("p (x c d) -> p x c d", x=4, c=2)
        self.load(gb, D["gate_b"])
        self.load(hn, D["hn"])
        self.load(gw, W[:, 3584:3600].rearrange("(k p) c -> p k c", p=128))
        tl = self.all_loads()
        qr = self.sbring(2, 512)
        tp = self.alloc(4, 256)

        def v4(x, half):
            return x.rearrange("p (h r u d) -> p h r u d", h=4, r=2, u=2)[:, :, :, half, :]

        def rope_to(dst, x, ps, tok, w):
            cs = [rope[:, x, c, :].rearrange("p (r d) -> p r d", r=2) for c in range(2)]
            a = tp
            ts = []
            for hh in range(4):
                xv = ps[:, hh * 128:hh * 128 + 128].rearrange("p (r u d) -> p r u d", r=2, u=2)
                tv = a[:, :, hh * 64:hh * 64 + 64].rearrange("p j (r d) -> p j r d", r=2)
                for j, (u, c) in enumerate(((0, 0), (1, 1), (0, 1), (1, 0))):
                    t = V.tt(tv[:, j, :, :], xv[:, :, u, :], cs[c], MUL, tok, tl)
            dv = dst.rearrange("p (g u d) -> p g u d", u=2, d=32)
            av = a.rearrange("p j (g d) -> p j g d", d=32)
            V.tt(dv[:, :, 0, :], av[:, 0, :, :], av[:, 1, :, :], SUB, w)
            V.tt(dv[:, :, 1, :], av[:, 2, :, :], av[:, 3, :, :], ADD)
            return t

        def to_T(dst, x, src, t, scale):
            b, ps, free = self.ps.get()
            for hh in range(4):
                tt = T.tr(ps[:, hh * 128:hh * 128 + 128], src[:, hh * 128:hh * 128 + 128], self.ident, free, t,
                          inc=(hh == 3))
            te = S.f(dst[:, :, x * 128:x * 128 + 128], ps.rearrange("p (h c) -> p h c", h=4), ACT.Copy, tt, scale=scale)
            self.ps.done(b, te)
            return tt

        late = []

        def ev_q(x, ps, tok):
            i, q, qf = qr.get()
            if x < 4:
                t = rope_to(q, x, ps, tok, qf)
            else:
                t = V.cp(q, ps, tok, qf)
            tq = V.last()
            while late:
                late.pop(0)()
            late.append(lambda: qr.done(i, to_T(qT, x, q, tq, 128.0 ** -0.5)))
            return t

        def ev_k(x, ps, tok):
            t = rope_to(kr[:, x, :], x, ps, tok, None) if x < 4 else V.cp(kr[:, x, :], ps, tok)
            tk = V.last()
            while late:
                late.pop(0)()
            late.append(lambda: to_T(kT, x, kr[:, x, :], tk, 1.0))
            return t

        self.linR(h, 6, W, 8, 1536, 512, ev_q, th)
        self.linR(h, 6, W, 8, 2048, 512, ev_k, th)
        self.linR(h, 6, W, 8, 2560, 512, lambda x, ps, tok: S.cp(vr[:, x, :], ps, tok), th)
        while late:
            late.pop(0)()
        PARTS = [(0, 512), (512, 768)]

        def ev_o(m, pi, ps, tok):
            a, b = PARTS[pi]
            t = S.f(og[:, m, a:b], ps, ACT.Sigmoid, tok)
            V.ts(og[:, m, a:b], og[:, m, a:b], hn[:, m:m + 1], None, MUL, None, t, tl)
            return t

        self.linT(h, W, 0, 8, 3072, 512, PARTS, ev_o, th)
        for x in range(6):
            b, ps, free = self.ps.get()
            for k in range(8):
                t = T.mm(ps[:, 0:16], h[:, k, x * 128:x * 128 + 128], gw[:, k, :], k == 0, k == 7, free, tl, inc=(k == 7))
            t = V.tt(Gt[:, x, :], ps[:, 0:16], gb, ADD, t, tl)
            self.ps.done(b, t)
        self.fence()
        self.top = mark
        keep = self.top, self.size
        self.top, self.size = self.h_at, self.h_at + 6144
        HS = self.alloc(6, 512)
        dg = self.sbring(2, 4, 128)
        ex = self.sbring(2, 4, 128)
        pp = self.sbring(2, 4, 128)
        self.top, self.size = keep
        A = lambda: self.alloc(6, 8)
        I, Fg, B, BT, IB, M1, MA, MX, ML, MS, WI, WS, DC, EM, NMX = (A() for _ in range(15))
        g4 = lambda a: a.rearrange("p x (d h) -> p x d h", d=2)
        t = S.f(Gt, Gt, ACT.Tanh, V.last(), scale=1.0 / 15.0)
        gv = Gt.rearrange("p x (d k h) -> p x d k h", d=2, k=2)
        for d in range(2):
            V.ts(g4(I)[:, :, d, :], gv[:, :, d, 0, :], 15.0, None, MUL, None, t)
            t2 = S.f(g4(Fg)[:, :, d, :], gv[:, :, d, 1, :], ACT.Exp, scale=-15.0)
        t = S.f(Fg, Fg, ACT.Ln, bias=1.0)
        t = V.ts(Fg, Fg, -1.0, None, MUL, None, t)
        b, ps, free = self.ps.get()
        bv = ps[:, 0:96].rearrange("p (j x h) -> p j x h", j=4, h=4)
        for d, n in ((0, "le"), (1, "ge")):
            T.mmx(bv[:, d, :, :], cn[n], g4(Fg)[:, :, d, :], True, True, free, t, tl)
            t1 = T.mmx(bv[:, 2 + d, :, :], self.ones, g4(Fg)[:, :, d, :], True, True, inc=True)
        for d in range(2):
            V.cp(g4(B)[:, :, d, :], bv[:, d, :, :], t1)
            t = V.cp(g4(BT)[:, :, d, :], bv[:, 2 + d, :, :])
        self.ps.done(b, t)
        t = V.tt(IB, I, B, SUB)

        def rows_of(col):
            i, d, df = dg.get()
            t = G.tt(d, self.ident[:, None, :].to_broadcast([128, 4, 128]), col[:, :, None].to_broadcast([128, 4, 128]),
                     MUL, df)
            yield
            b, ps, free = self.ps.get()
            t = T.mm(ps, self.ones, d.rearrange("p h c -> p (h c)"), True, True, t, free, inc=True)
            dg.done(i, t)
            return b, ps.rearrange("p (h c) -> p h c", h=4), t

        tib = t

        def maxima(d):
            V.wait(tib), G.wait(tib)
            for x in range(6):
                b, ps, t = yield from rows_of(g4(IB)[:, x, d, :])
                yield
                V.red(g4(MA)[:, x, d, :], ps, MAX, t)
                i, e, ef = ex.get()
                t = V.tt(e, ps, cn["mge" if d == 0 else "mle"][:, None, :].to_broadcast([128, 4, 128]), ADD, ef)
                self.ps.done(b, t)
                t = V.red(g4(M1)[:, x, d, :], e, MAX)
                ex.done(i, t)
                yield

        self.side_by_side([maxima(0), maxima(1)], leave=0)
        V.wait(V.everything())
        order = {0: [4, 5, 0, 1, 2, 3], 1: [5, 4, 3, 2, 1, 0]}
        for d in range(2):
            for n, x in enumerate(order[d]):
                ms = g4(MS)[:, x, d, :]
                if n == 0:
                    V.set(ms, 0.0)
                V.tt(g4(ML)[:, x, d, :], g4(MA)[:, x, d, :], ms, MAX)
                if n < 5:
                    V.tt(g4(MS)[:, order[d][n + 1], d, :], g4(BT)[:, x, d, :], g4(ML)[:, x, d, :], ADD)
        V.tt(MX, M1, MS, MAX)
        V.tt(WI, MS, MX, SUB)
        V.tt(WS, IB, ML, SUB)
        V.tt(DC, MS, ML, SUB)
        V.tt(EM, B, MX, ADD)
        t = V.ts(NMX, MX, -1.0, None, MUL, None)
        S.f(WI, WI, ACT.Exp, t)
        S.f(WS, WS, ACT.Exp)
        S.f(DC, DC, ACT.Exp)
        tg = S.f(EM, EM, ACT.Exp, scale=-1.0)
        V.wait(tg)
        Cst = self.alloc(8, 128)
        Nst = self.alloc(8)
        V.set(Cst, 0.0)
        tz = V.set(Nst, 0.0)
        nm = self.sbring(2, 4, 128)
        kw = self.sbring(2, 4, 128)
        dn = self.sbring(2, 8)
        done = {}
        tst = [tz, tz]
        ts0 = [V.last(), S.last()]

        def scan(d):
            for q in (T, V, S, G):
                q.wait(ts0)
            for n in range(6):
                x = order[d][n]
                xs = slice(x * 128, x * 128 + 128)
                c = lambda a: g4(a)[:, x, d, :]
                k, w, wf = kw.get()
                tkw = G.tt(w, kr[:, x, :].rearrange("p (h c) -> p h c", h=4), c(WS)[:, :, None].to_broadcast([128, 4, 128]),
                           MUL, wf)
                b, ps, t = yield from rows_of(c(MX))
                yield
                i, e, ef = ex.get()
                t = V.tt(e, cn["mle" if d == 0 else "mge"][:, None, :].to_broadcast([128, 4, 128]), ps, SUB, t, ef)
                self.ps.done(b, t)
                for hh in range(4):
                    te = S.f(e[:, hh, :], e[:, hh, :], ACT.Exp, t, bias=c(IB)[:, hh:hh + 1])
                yield
                b, ps, free = self.ps.get()
                for hh in range(4):
                    t = T.mm(ps[:, hh * 128:hh * 128 + 128], kT[:, hh, xs], qT[:, hh, xs], True, True, free, S.last(),
                             inc=(hh == 3))
                j, p, pf = pp.get()
                tpp = V.tt(p, ps.rearrange("p (h c) -> p h c", h=4), e, MUL, t, te, pf)
                self.ps.done(b, tpp)
                ex.done(i, tpp)
                yield
                b1, p1, f1 = self.ps.get()
                b2, p2, f2 = self.ps.get()
                b3, p3, f3 = self.ps.get()
                b4, p4, f4 = self.ps.get()
                for hh in range(4):
                    hs = slice(hh * 128, hh * 128 + 128)
                    T.mm(p1[:, hs], p[:, hh, :], vr[:, x, hs], True, True, tpp, f1)
                    T.mm(p2[:, hs], qT[:, hh, xs], Cst[:, 4 * d + hh, :], True, True, tst[d], f2)
                    T.mm(p3[:, hh:hh + 1], p[:, hh, :], self.ones[:, 0:1], True, True, f3)
                    tm = T.mm(p3[:, 4 + hh:5 + hh], qT[:, hh, xs], Nst[:, 4 * d + hh:4 * d + hh + 1], True, True, inc=True)
                pp.done(j, tm)
                for hh in range(4):
                    hs = slice(hh * 128, hh * 128 + 128)
                    T.mm(p4[:, hs], w[:, hh, :], vr[:, x, hs], True, True, tkw, f4)
                    tu = T.mm(p3[:, 8 + hh:9 + hh], w[:, hh, :], self.ones[:, 0:1], True, True, inc=True)
                kw.done(k, tu)
                cs = Cst[:, 4 * d:4 * d + 4, :]
                V.tt(cs, cs, c(DC)[:, :, None].to_broadcast([128, 4, 128]), MUL, tm)
                t = V.tt(cs, cs, p4.rearrange("p (h c) -> p h c", h=4), ADD, tu)
                self.ps.done(b4, t)
                ns = Nst[:, 4 * d:4 * d + 4]
                V.tt(ns, ns, c(DC), MUL)
                t = V.tt(ns, ns, p3[:, 8:12], ADD)
                tst[d] = t
                j, q, qf = nm.get()
                t = V.tt(q, p2.rearrange("p (h c) -> p h c", h=4), c(WI)[:, :, None].to_broadcast([128, 4, 128]), MUL, qf)
                self.ps.done(b2, t)
                t = V.tt(q, q, p1.rearrange("p (h c) -> p h c", h=4), ADD)
                self.ps.done(b1, t)
                z, dd, df = dn.get()
                V.tt(dd[:, 0:4], p3[:, 4:8], c(WI), MUL, df)
                t = V.tt(dd[:, 0:4], dd[:, 0:4], p3[:, 0:4], ADD)
                self.ps.done(b3, t)
                t = S.f(dd[:, 0:4], dd[:, 0:4], ACT.Abs, t)
                V.tt(dd[:, 0:4], dd[:, 0:4], c(EM), MAX, t)
                V.rec(dd[:, 0:4], dd[:, 0:4])
                rd = dd[:, 0:4, None].to_broadcast([128, 4, 128])
                hv = HS[:, x, :].rearrange("p (h c) -> p h c", h=4)
                if x in done:
                    V.tt(q, q, rd, MUL)
                    t = V.tt(hv, hv, q, ADD, done[x])
                else:
                    t = V.tt(hv, q, rd, MUL)
                    done[x] = t
                nm.done(j, t)
                dn.done(z, t)
                yield

        self.side_by_side([scan(0), scan(1)], leave=0)
        self.need(2, 11)
        for q in (T, V, S, G):
            q.wait(V.everything())
        def tail(par):
            for x in range(par, 6, 2):
                hv = HS[:, x, :].rearrange("p (h c) -> p h c", h=4)
                j, q, qf = nm.get()
                z, dd, df = dn.get()
                V.tt(q, hv, hv, MUL, qf)
                V.red(dd[:, 0:4], q, ADD, df)
                V.ts(dd[:, 0:4], dd[:, 0:4], 1.0 / 128, 1e-6, MUL, ADD)
                t = V.rec(dd[:, 0:4], dd[:, 0:4])
                t = S.f(dd[:, 4:8], dd[:, 0:4], ACT.Sqrt, t)
                t = V.tt(q, hv, dd[:, 4:8, None].to_broadcast([128, 4, 128]), MUL, t)
                dn.done(z, t)
                yield
                b, ps, free = self.ps.get()
                for hh in range(4):
                    t2 = T.tr(ps[:, hh * 128:hh * 128 + 128], q[:, hh, :], self.ident, t, free, inc=(hh == 3))
                nm.done(j, t2)
                xs = slice(x * 128, x * 128 + 128)
                t = V.tt(cat[:, 4:8, xs], ps.rearrange("p (h c) -> p h c", h=4), og[:, :, xs], MUL, t2)
                self.ps.done(b, t)
                yield

        self.side_by_side([tail(0), tail(1)])

    def layer1(self, tc):
        D, T, V, S, G = self.D, self.T, self.V, self.S, self.G
        X, C = self.X, self.C
        p, tp = self.mod[1], self.need(1, 11)
        LP, CP = p[:, 0, :], p[:, 1, :]
        vec = self.alloc(40)
        wa0 = self.alloc(32)
        self.load(vec, D["rwv"])
        self.load(wa0, D["w0a0"])
        gh = self.alloc(2, 512)
        mix = self.alloc(8, 772)
        rT = self.alloc(8, 768)
        k_at = self.top
        kT = self.alloc(8, 768)
        mark = self.top
        hp = self.alloc(8, 772)
        xx_at = self.top
        keep = self.top
        self.top = k_at
        w1 = self.alloc(8, 128)
        a1 = self.alloc(8, 128)
        g1 = self.alloc(8, 160)
        mu = self.alloc(48)
        self.top = keep
        for d in range(2):
            self.load(w1[:, :, d * 64:d * 64 + 64], D["w1"][d].rearrange("(k p) r -> p k r", p=128))
            self.load(a1[:, :, d * 64:d * 64 + 64], D["a1"][d].rearrange("(k p) r -> p k r", p=128))
        self.load(g1, D["g1"].rearrange("(k p) r -> p k r", p=128))
        for c in (0, 513, 514, 771):
            tz = V.set(hp[:, :, c:c + 1], 0.0)
        V.wait(tz)
        self.modulate([(hp[:, :, 1:513], X, 512, LP[:, 8:16], LP[:, 0:8]),
                       (hp[:, :, 515:771], C, 256, CP[:, 8:16], CP[:, 0:8])], mix.rearrange("p k t -> p (k t)"), [tp, tc])
        V.wait(S.last())
        self.load(self.spill, X.rearrange("p k t -> p (k t)"), [S.last(), V.last()], q=self.Q)
        xx = self.alloc(8, 772)
        mu = self.C_view(0, 48)
        self.load(mu, D["mu"], S.last(), V.last())
        wh, ah = self.C_view(64, 768), self.C_view(832, 768)
        tl = self.all_loads()
        for k in range(8):
            V.tt(xx[:, k, 1:771], hp[:, k, 0:770], hp[:, k, 2:772], ADD)
            V.stt(xx[:, k, 1:771], xx[:, k, 1:771], 0.5, hp[:, k, 1:771], MUL, SUB)

        def blend(dst, s, w):
            return {k: V.stt(dst[:, k, 1:771], xx[:, k, 1:771], mu[:, s * 8 + k:s * 8 + k + 1], hp[:, k, 1:771],
                             MUL, ADD, self.of(w, k), tl) for k in range(8)}

        def hidden(jobs, parts, t):
            got = [(j, p, self.ps.get()) for j in jobs for p in parts]
            tm = {}
            for k in range(8):
                for (w, m0, mw, dst, fn), (a, b, o), (bi, ps, free) in got:
                    tm[k] = T.mm(ps[0:mw, 0:b - a], w[:, k, m0:m0 + mw], mix[:, k, a:b], k == 0, k == 7, free,
                                 self.of(t, k), tl, inc=True)
            for (w, m0, mw, dst, fn), (a, b, o), (bi, ps, free) in got:
                self.ps.done(bi, S.f(dst[0:mw, o:o + b - a], ps[0:mw, 0:b - a], fn, tm[7]))
            return tm

        HP = [(1, 513, 0), (515, 771, 512)]
        t = blend(mix, 1, None)
        t = hidden([(w1, 0, 128, wh, ACT.Tanh)], HP, t)
        t = blend(mix, 4, t)
        t = hidden([(a1, 0, 128, ah, ACT.Copy)], HP, t)
        t = blend(mix, 5, t)
        t = hidden([(g1, 0, 128, gh[:, 0, :], ACT.Sigmoid), (g1, 128, 32, gh[:, 1, :], ACT.Sigmoid)], HP[:1], t)
        parts = [(1, 513), (515, 771)]
        for s, dst, W in ((0, rT, D["rkv"][0]), (2, kT, D["rkv"][1])):
            t = blend(mix, s, t)

            def ev(m, pi, ps, tok):
                a, b = ((0, 512), (512, 768))[pi]
                return S.cp(dst[:, m, a:b], ps, tok)

            t = self.linT(mix, W, 0, 8, 0, 1024, parts, ev, t)
        tv = blend(xx, 3, None)
        self.fence()
        vR = self.region(mix, 6144).rearrange("p (x c) -> p x c", x=6)
        for c in range(2):
            self.linR(xx, 6, D["rkv"][2], 8, c * 512, 512,
                      lambda x, ps, tok: S.cp(vR[:, x, c * 512:c * 512 + 512], ps, tok), tv,
                      starts=[1, 129, 257, 385, 515, 643])
            self.fence()
        self.top = mark
        self.fence(slots=True)
        self.rwkv(rT, kT, vR, wh, ah, vec, wa0)
        self.fence(slots=True)
        tback = self.load(X.rearrange("p k t -> p (k t)"), self.spill, q=self.Q)
        V.wait(tback)
        self.top = mark
        g2 = self.alloc(2, 1024)
        t = [self.load(g2[:, 0, :], D["g2"][0:128, :]), self.load(g2[0:32, 1, :], D["g2"][128:160, :])]
        for m in range(8):
            bi, ps, free = self.ps.get()
            T.mm(ps, g2[:, 0, m * 128:m * 128 + 128], gh[:, 0, :], True, False, t, free)
            tm = T.mm(ps, g2[0:32, 1, m * 128:m * 128 + 128], gh[0:32, 1, :], False, True, inc=True)
            tg = V.tt(rT[:, m, 0:512], rT[:, m, 0:512], ps, MUL, tm)
            self.ps.done(bi, tg)

        def ev_o(m, pi, ps, tok):
            return V.stt(X[:, m, :], ps, LP[:, 16 + m:17 + m], X[:, m, :], MUL, ADD, tok)

        self.linT(rT, D["w_o"], 0, 8, 0, 1024, [(0, 512)], ev_o, tg)
        tx = V.last()
        self.mlp(1, [(X, 512, LP)])

    def C_view(self, o, n):
        return self.region(self.C, 2048)[:, o:o + n]

    def region(self, v, n):
        for tensor, start, a in self.starts:
            if a is v:
                return tensor[:, start:start + n]
        raise RuntimeError("not a buffer")

    def rwkv(self, rT, kT, vR, wh, ah, vec, wa0):
        D, T, V, S, G = self.D, self.T, self.V, self.S, self.G
        C0 = float(np.exp(np.float32(-0.5)))
        self.bk1 = self.alloc(512)
        keep = self.top, self.size
        self.top, self.size = self.w_at, self.w_at + NR * 4096
        cn = {n: self.const(n) for n in ("u0", "d0", "u1", "d1", "u2", "d2", "u3", "d3", "lt", "gt", "le", "ge")}
        tl = self.all_loads()
        for q in (T, V, S, G):
            q.wait(tl)
        kkv, kav, rkv, lnw, lnb = (vec[:, i * 8:i * 8 + 8] for i in range(5))
        c2 = lambda v: v.rearrange("p (c t) -> p c t", t=128)
        m4 = lambda v: v.rearrange("p g c -> p (g c)")
        bc = lambda v, n: v[:, None, :].to_broadcast([128, n, 128])

        class Dir:
            pass

        xv = self.X
        bk = [self.rows.bufs[0], self.bk1]
        dirs = []
        for d in range(2):
            s = Dir()
            s.mats = [self.alloc(4, 128) for _ in range(4)]
            s.sets = Ring([tuple(self.alloc(4, 128) for _ in range(4)) + (self.alloc(2, 2, 128),),
                           tuple(xv[:, 4 * d + j, :].rearrange("p (g c) -> p g c", g=4) for j in range(4))
                           + (bk[d].rearrange("p (a i c) -> p a i c", a=2, i=2),)])
            s.solved = []
            s.RH, s.UU, s.ZZ = self.sbring(1, 128), self.sbring(2, 128), self.sbring(2, 128)
            s.zt, s.zm = self.alloc(128), self.alloc(128)
            s.tmp = [self.alloc(256) for _ in range(6)]
            s.ops = self.sbring(2, 4, 256)
            s.me = self.sbring(2, 2, 2)
            s.wm = self.sbring(2, 2, 128)
            s.made = []
            dirs.append(s)
            ybufs = [self.alloc(512) for _ in range(2)]
            if d == 0:
                y0bufs = ybufs
                self.top, self.size = keep
        Yr = Ring(y0bufs + ybufs)
        KR = self.sbring(4, 512)
        yy, kr = {}, {}

        def prep(d, m, lo):
            s = dirs[d]
            hi = lo + 256
            rows = slice(64 * d, 64 * d + 64)
            c1 = slice(m, m + 1)
            sg, B, av, e2, kd, kk = s.tmp
            k, r = kT[:, m, lo:hi], rT[:, m, lo:hi]
            if lo == 512:
                i, w, wf = s.wm.get()
                tw = [self.load(w[rows, 0, :], D["w2"][rows, m * 128:m * 128 + 128], wf),
                      self.load(w[rows, 1, :], D["a2"][rows, m * 128:m * 128 + 128], wf)]
                s.w = (i, w, tw)
            i, w, tw = s.w
            while not (s.ops.order and s.me.order and KR.order):
                yield
            oi, ops, of = s.ops.get()
            mi, me, mf = s.me.get()
            aa, bb, ks, rr = (ops[:, j, :] for j in range(4))
            t = V.ts(kk, k, kkv[:, c1], None, MUL, None)
            bi, ps, free = self.ps.get()
            T.mm(ps[:, 0:256], w[rows, 0, :], wh[rows, lo:hi], True, True, tw, free, S.last())
            tm = T.mm(ps[:, 256:512], w[rows, 1, :], ah[rows, lo:hi], True, True, inc=True)
            if lo == ((256, 0)[d]):
                s.wm.done(i, tm)
            S.f(sg, ps[:, 0:256], ACT.Sigmoid, tm, V.last(), bias=wa0[:, d * 8 + m:d * 8 + m + 1])
            ts = S.f(av, ps[:, 256:512], ACT.Sigmoid, bias=wa0[:, 16 + d * 8 + m:17 + d * 8 + m])
            self.ps.done(bi, ts)
            yield
            t = V.tt(e2, kk, kk, MUL)
            yield
            bi, ps, free = self.ps.get()
            t1 = T.mm(ps[:, 0:256], self.blk, e2, True, True, t, free, inc=True)
            yield
            t2 = V.ts(e2, ps[:, 0:256], 1e-24, None, MAX, None, t1)
            self.ps.done(bi, t2)
            for c in range(2):
                a, b = c * 128, c * 128 + 128
                if d == 0:
                    tb = V.scan(B[:, a:b], self.ones, sg[:, a:b], ts)
                else:
                    tb = V.scan(B[:, a:b][:, ::-1], self.ones, sg[:, a:b][:, ::-1], ts)
            yield
            S.f(e2, e2, ACT.Ln, t2, scale=2.0 ** 16)
            te = S.f(e2, e2, ACT.Exp, scale=-0.5, bias=float(8 * np.log(2.0)))
            mt, en = (63, 127) if d == 0 else (64, 0)
            V.cp(me[:, 0, :], c2(B)[:, :, mt], mf, of)
            V.tt(me[:, 1, :], c2(B)[:, :, en], me[:, 0, :], SUB)
            tb = V.tt(c2(B), c2(B), me[:, 0, :, None].to_broadcast([128, 2, 128]), SUB)
            tk = V.tt(kk, kk, e2, MUL, te)
            yield
            S.f(me, me, ACT.Exp, tb, scale=-C0)
            te = S.f(e2, B, ACT.Exp, tk, scale=C0)
            tr = S.f(rr, B, ACT.Exp, of, scale=-C0)
            t = V.tt(sg, B, sg, SUB)
            ta = S.f(aa, sg, ACT.Exp, t, scale=-C0)
            tr = G.tt(rr, rr, r, MUL, tr)
            yield
            tq = V.ts(kd, av, 1.0, kav[:, c1], SUB, MUL)
            tq = G.tt(av, kk, av, MUL, tq)
            tkd = V.stt(kd, kd, 1.0, k, ADD, MUL)
            V.stt(aa, aa, -1.0, kk, MUL, MUL, ta)
            V.tt(bb, av, e2, MUL, te, tq)
            tv = V.tt(ks, kd, e2, MUL)
            if lo < 512:
                if (d, m) not in kr:
                    kr[d, m] = KR.get()
                ki, kb, kf = kr[d, m]
                G.tt(kb[:, lo:hi], kd, r, MUL, tkd, kf)
            tg = G.last()
            V.wait(tg), S.wait(tg)
            s.gt = tg
            s.made.append((oi, aa, bb, ks, rr, mi, me, [tv, tr, tg, S.last()]))
            yield

        def solve(d):
            s = dirs[d]
            N, Pw, Pf, XT = s.mats
            u = (lambda n: "u" + n) if d == 0 else (lambda n: "d" + n)
            dn = (lambda n: "d" + n) if d == 0 else (lambda n: "u" + n)
            strict, incl = ("lt", "le") if d == 0 else ("gt", "ge")
            batches = [(4, 5), (0, 1), (2, 3)] if d == 0 else [(5, 4), (3, 2), (1, 0)]
            for n in range(24):
                items = batches[n % 3]
                while not (s.made and s.sets.order):
                    yield
                oi, aa, bb, ks, rr, mi, me, tops = s.made.pop(0)
                si, (Xm, Aak, Ark, Arb, BK), sf = s.sets.get()
                V.wait(tops, sf), S.wait(tops, sf)
                lo = min(items) * 128
                lat = n % 3 > 0
                tok = [slice(x * 128 - lo, x * 128 - lo + 128) for x in items]

                def products(lhs, rhs, outs):
                    for hd in range(2):
                        o = slice(64 * hd, 64 * hd + 64)
                        bi, ps, free = self.ps.get()
                        for it in range(2):
                            t = T.mm(ps[:, it * 128:it * 128 + 128], lhs[o, tok[it]], rhs[o, tok[it]], True, True,
                                     free, tops, inc=(it == 1))
                        pv = ps[:, 0:256].rearrange("p (i c) -> p i c", i=2)
                        for dst, mask in outs:
                            dv = dst[:, 2 * hd:2 * hd + 2, :]
                            if mask is None:
                                t = S.cp(dv, pv, t, tprev)
                            else:
                                t = V.tt(dv, pv, bc(cn[mask], 2), MUL, t, tprev)
                        self.ps.done(bi, t)

                tprev = [T.last(), S.last()]
                products(bb, aa, [(N, u("0"))])
                t0 = V.last()
                products(aa, bb, [(Pf, None), (Pw, dn("0"))])
                tp0, tpf = V.last(), S.last()
                yield
                txm = V.tt(Xm, N, bc(self.ident, 4), ADD)
                products(ks, aa, [(Aak, strict)])
                bi, ps, free = self.ps.get()
                for it in range(2):
                    T.tr(ps[:, it * 128:it * 128 + 128], bb[:, tok[it]], self.ident, free, tops)
                    t = T.tr(ps[:, 256 + it * 128:384 + it * 128], ks[:, tok[it]], self.ident, inc=(it == 1))
                tbk = S.cp(BK.rearrange("p a i c -> p (a i c)"), ps, t, tprev)
                self.ps.done(bi, tbk)
                yield

                def mul(l, r_, t):
                    bi, ps, free = self.ps.get()
                    for g in range(4):
                        tt = T.mm(ps[:, g * 128:g * 128 + 128], l[:, g, :], r_[:, g, :], True, True, t, free,
                                  inc=(g == 3))
                    return bi, ps, tt

                for lev in range(3):
                    t = [t0, tp0]
                    if lev < 2:
                        b1, p1, t1 = mul(Pw, N, t)
                    b2, p2, t2 = mul(N, Pw, t)
                    if lev < 2:
                        t0 = V.cp(m4(N), p1, t1, t2)
                        self.ps.done(b1, t0)
                    tp0 = t3 = S.cp(m4(Pw), p2, t2)
                    self.ps.done(b2, t3)
                    if lat and lev == 0:
                        products(ks, rr, [(Ark, incl)])
                    if lat and lev == 1:
                        products(bb, rr, [(Arb, incl)])
                    yield
                    b3, p3, t3 = mul(Pw, Xm, [t3, txm])
                    txm = V.tt(m4(Xm), m4(Xm), p3, ADD, t3)
                    self.ps.done(b3, txm)
                    if lev == 2:
                        yield
                bi, ps, free = self.ps.get()
                tx = V.last()
                for g in range(4):
                    t = T.tr(ps[:, g * 128:g * 128 + 128], Xm[:, g, :], self.ident, free, tx, inc=(g == 3))
                tt = S.cp(m4(XT), ps, t)
                self.ps.done(bi, tt)
                for lev in range(1, 4):
                    b1, p1, t1 = mul(Pf, Xm, [V.last(), tpf])
                    t2 = V.tt(N, p1.rearrange("p (g c) -> p g c", g=4), bc(cn[u(str(lev))], 4), MUL, t1)
                    self.ps.done(b1, t2)
                    yield
                    b2, p2, t3 = mul(XT, N, [t2, tt])
                    if lev < 3:
                        b3, p3, t4 = mul(N, XT, [t2, tt])
                    tx = V.tt(m4(Xm), m4(Xm), p2, ADD, t3)
                    self.ps.done(b2, tx)
                    if lev < 3:
                        tt = V.tt(m4(XT), m4(XT), p3, ADD, t4)
                        self.ps.done(b3, tt)
                    yield
                s.solved.append((oi, aa, rr, mi, me, tops, si, (Xm, Aak, Ark, Arb, BK), [V.last(), S.last()]))
                yield

        def stream(d, m):
            s = dirs[d]
            zi, z, zf = s.ZZ.get()
            tz = V.set(z, 0.0, zf)
            batches = [(4, 5), (0, 1), (2, 3)] if d == 0 else [(5, 4), (3, 2), (1, 0)]
            for bn, items in enumerate(batches):
                while not s.solved:
                    yield
                oi, aa, rr, mi, me, tops, si, (Xm, Aak, Ark, Arb, BK), tm = s.solved.pop(0)
                V.wait(tops)
                lo = min(items) * 128
                lat = bn > 0
                tok = [slice(x * 128 - lo, x * 128 - lo + 128) for x in items]
                for it, x in enumerate(items):
                    cs = tok[it]
                    xl = (x * 128 - lo) // 128
                    vm = vR[:, x, m * 128:m * 128 + 128]
                    if it == 0:
                        tz = V.ts(s.zm, z, me[:, 0, xl:xl + 1], None, MUL, None, T.last())
                        yield
                    z_ = s.zm
                    ri, rh, rf = s.RH.get()
                    ui, uu, uf = s.UU.get()
                    bi, ps, free = self.ps.get()
                    T.mmx(ps[:, 0:128], aa[:, cs], z_, True, False, tz, free, tops)
                    for hd in range(2):
                        o = slice(64 * hd, 64 * hd + 64)
                        t = T.mmx(ps[:, o], Aak[:, 2 * hd + it, :], vm[:, o], False, True, tm, inc=(hd == 1))
                    t = S.cp(rh, ps[:, 0:128], t, rf)
                    self.ps.done(bi, t)
                    yield
                    bi, ps, free = self.ps.get()
                    for hd in range(2):
                        o = slice(64 * hd, 64 * hd + 64)
                        t1 = T.mm(ps[:, o], Xm[:, 2 * hd + it, :], rh[:, o], True, True, t, tm, free, inc=(hd == 1))
                    s.RH.done(ri, t1)
                    t = S.cp(uu, ps[:, 0:128], t1, uf)
                    self.ps.done(bi, t)
                    yield
                    if not (bn == 2 and it == 1):
                        bz, pz, fz = self.ps.get()
                        T.mm(pz[:, 0:128], BK[:, 0, it, :], uu, True, False, t, fz)
                        tzz = T.mm(pz[:, 0:128], BK[:, 1, it, :], vm, False, True, inc=True)
                        nzi, nz, nzf = s.ZZ.get()
                        en = me[:, 1, xl:xl + 1]
                        t2 = V.stt(s.zt, pz[:, 0:128], en, self.blk, MUL, MUL, tzz)
                        self.ps.done(bz, t2)
                        tz = V.stt(nz, z_, en, s.zt, MUL, ADD, nzf)
                        s.ZZ.done(zi, tz)
                        zi, z = nzi, nz
                    if lat:
                        if (d, m) not in yy:
                            while not Yr.order:
                                yield
                            yy[d, m] = Yr.get()
                        yi, yb, yf = yy[d, m]
                        by, py, fy = self.ps.get()
                        T.mmx(py[:, 0:128], z_, rr[:, cs], True, False, fy)
                        for hd in range(2):
                            o = slice(64 * hd, 64 * hd + 64)
                            T.mmx(py[o, 0:128], uu[:, o], Arb[:, 2 * hd + it, :], False, False, t)
                            ty = T.mmx(py[o, 0:128], vm[:, o], Ark[:, 2 * hd + it, :], False, True, inc=(hd == 1))
                        self.ps.done(by, S.cp(yb[:, x * 128:x * 128 + 128], py[:, 0:128], ty, yf))
                    s.UU.done(ui, T.last())
                    V.wait(T.last())
                    if it == 0:
                        xn = (items[1] * 128 - lo) // 128
                        tz = V.ts(s.zm, z, me[:, 0, xn:xn + 1], None, MUL, None)
                    yield
                s.ops.done(oi, T.last())
                s.sets.done(si, T.last())
                s.me.done(mi, V.last())
            s.ZZ.done(zi, V.last(), T.last())
            s.tail = [V.last(), S.last(), G.last(), T.last()]

        def ahead(d):
            s = dirs[d]
            for m in range(8):
                for lo in ((512, 0, 256) if d == 0 else (512, 256, 0)):
                    while s.made:
                        yield
                    yield from prep(d, m, lo)

        def epilogue(m, tails):
            c1 = slice(m, m + 1)
            r = rT[:, m, 0:512]
            (y0i, y0, _), (y1i, y1, _) = yy[0, m], yy[1, m]
            (k0i, k0, _), (k1i, k1, _) = kr[0, m], kr[1, m]
            tA, tB = y1, k1
            V.tt(y0, y0, y1, ADD, tails)
            t = V.tt(k0, k0, k1, ADD)
            t = V.ts(k0, k0, rkv[:, c1], None, MUL, None)
            yield
            bi, ps, free = self.ps.get()
            t = T.mm(ps, self.blk, y0, True, True, V.last(), free, inc=True)
            t1 = V.stt(y0, ps, -1.0 / 64, y0, MUL, ADD, t)
            self.ps.done(bi, t1)
            yield
            t = S.f(tA, y0, ACT.Square, t1, V.last())
            yield
            bi, ps, free = self.ps.get()
            t = T.mm(ps, self.blk, tA, True, True, t, free, inc=True)
            ta = V.ts(tB, ps, 1.0 / 64, 64e-5, MUL, ADD, t, S.last())
            self.ps.done(bi, ta)
            t = S.f(tB, tB, ACT.Ln, ta)
            tb = S.f(tB, tB, ACT.Exp, scale=-0.5)
            yield
            V.stt(y0, y0, lnw[:, c1], tB, MUL, MUL, tb)
            bi, ps, free = self.ps.get()
            t = T.mm(ps, self.blk, k0, True, True, V.last(), free, inc=True)
            t1 = V.ts(y0, y0, lnb[:, c1], None, ADD, None)
            t2 = S.cp(tB, ps, t, t1)
            self.ps.done(bi, t2)
            yield
            bi, ps, free = self.ps.get()
            for x in range(4):
                t = T.tr(ps[:, x * 128:x * 128 + 128], vR[:, x, m * 128:m * 128 + 128], self.ident, free, inc=(x == 3))
            t1 = V.tt(tB, tB, ps, MUL, t2, t)
            self.ps.done(bi, t1)
            t = V.tt(r, y0, tB, ADD)
            for i in (y0i, y1i):
                Yr.done(i, t)
            for i in (k0i, k1i):
                KR.done(i, t, T.last())

        preps = [ahead(0), ahead(1)]
        solves = [solve(0), solve(1)]
        for d in range(2):
            while not dirs[d].made:
                self.turn(preps[d], ("prep", d))
        ep = None
        for m in range(8):
            gens = [stream(d, m) for d in range(2)]
            alive = [True, True]
            step = 0
            while any(alive):
                for d in range(2):
                    self.turn(solves[d], ("solve", d))
                    self.turn(preps[d], ("prep", d))
                for d in range(2):
                    if alive[d]:
                        alive[d] = self.turn(gens[d], ("stream", d))
                if ep is not None and step % 3 == 2 and not self.turn(ep, ("ep", 0)):
                    ep = None
                step += 1
            while ep is not None and self.turn(ep, ("ep", 0)):
                pass
            ep = epilogue(m, dirs[0].tail + dirs[1].tail + [dirs[0].gt, dirs[1].gt])
        while self.turn(ep, ("ep", 0)):
            pass
        self.as_stream(None)

    def side_by_side(self, gens, leave=9):
        gens = [(i, g) for i, g in enumerate(gens)]
        while gens:
            gens = [(i, g) for i, g in gens if self.turn(g, ("side", i))]
            self.as_stream(None)
            if len(self.later) > leave:
                self.background()
        self.as_stream(None)

    def turn(self, g, key):
        self.as_stream(key)
        return next(g, "end") != "end"

    def as_stream(self, key):
        for q in (self.T, self.V, self.S, self.G):
            q.key = key

    def block2(self):
        D, T, V, S, G = self.D, self.T, self.V, self.S, self.G
        X = self.X
        p, tp = self.mod[2], self.need(2, 11)
        LP, CP = p[:, 0, :], p[:, 1, :]
        n2 = self.alloc(34)
        tn = self.load(n2[:, 0:33], D["n2"])
        V.wait(tn, tp), S.wait(tn)
        V.tt(LP[:, 8:16], LP[:, 8:16], n2[:, 0:8], MUL)
        V.tt(CP[:, 8:16], CP[:, 8:16], n2[:, 0:8], MUL)
        tp = V.tt(LP[:, 32:40], LP[:, 32:40], n2[:, 8:16], MUL)
        low = self.top
        W = D["w_in_2"]
        h = self.alloc(8, 768)
        og = self.alloc(4, 512)
        mark = self.top
        c2 = self.alloc(8, 256)
        tc = self.load(c2, D["ctx2T"].rearrange("(k p) t -> p k t", p=128))
        th = self.modulate([(h[:, :, 0:512], X, 512, LP[:, 8:16], LP[:, 0:8]),
                            (h[:, :, 512:768], c2, 256, CP[:, 8:16], CP[:, 0:8])], self.alloc(2304), [tp, tc])
        self.fence()
        self.top = mark
        self.gla(h, og, th, n2)
        self.fence()
        self.top = mark
        mg = self.alloc(16, 512)
        LAT = [(0, 512)]
        mark = self.top
        pT = self.alloc(4, 512)
        mx = self.alloc(4, 512)
        pw = self.alloc(4, 128)
        cnt = self.const("cnt")
        self.load(pw, D["pool_w"].rearrange("g c d -> c g d"))
        tl = self.all_loads()
        self.linT(h, W, 0, 8, 1568, 512, LAT, lambda m, pi, ps, tok: S.cp(pT[:, m, :], ps, tok), th)
        tpt = S.last()
        CA, CB = self.alloc(8, 96), self.alloc(8, 96)
        RA, RB = self.alloc(24, 64), self.alloc(24, 64)
        for b in (CA, CB, RA, RB):
            V.set(b, 0.0)
        pl = [self.alloc(512) for _ in range(4)]
        tpl = []
        for g in range(4):
            w = 2 ** (g + 1)
            u = pT[:, g, :].rearrange("p (r c) -> p r c", c=64)
            a, b, n = CA, CB, 96
            V.cp(a[:, :, 16:80], u, tpt)
            V.set(a[:, :, 0:16], 0.0)
            V.set(a[:, :, 80:96], 0.0)
            for l in range(g + 1):
                s = 2 ** l
                n -= s
                V.tt(b[:, :, 0:n], a[:, :, 0:n], a[:, :, s:s + n], ADD)
                a, b = b, a
            o = 16 - w // 2
            src, a, b, n = a, RA, RB, 24
            V.cp(a[:, 8:16, :], src[:, :, o:o + 64])
            V.set(a[:, 0:8, :], 0.0)
            V.set(a[:, 16:24, :], 0.0)
            for l in range(g + 1):
                s = 2 ** l
                n -= s
                V.tt(b[:, 0:n, :], a[:, 0:n, :], a[:, s:s + n, :], ADD)
                a, b = b, a
            o = 8 - w // 2
            q = pl[g]
            qv = q.rearrange("p (r c) -> p r c", c=64)
            cv = cnt[:, g * 512:g * 512 + 512].rearrange("p (r c) -> p r c", c=64)
            V.tt(qv, a[:, o:o + 8, :], cv, MUL, tl)
            tpl.append(V.tt(qv, qv, u, SUB))
        self.linT(h, W, 0, 8, 2080, 2048, LAT, lambda m, pi, ps, tok: S.f(mg[:, m, :], ps, ACT.Sigmoid, tok), th)
        for g in range(4):
            bi, ps, free = self.ps.get()
            t = T.mm(ps, pw[:, g, :], pl[g], True, True, tpl[g], free, tl, inc=True)
            self.ps.done(bi, V.ts(mx[:, g, :], ps, n2[:, 25 + g:26 + g], None, MUL, None, t))
        tm = V.last()
        self.linT(og, D["w_gla"], 0, 4, 0, 1024, LAT,
                  lambda m, pi, ps, tok: V.tt(mg[:, m, :], mg[:, m, :], ps, MUL, tok, S.last()), tm)
        self.linT(mx, D["w_poolp"], 0, 4, 0, 1024, LAT,
                  lambda m, pi, ps, tok: V.tt(mg[:, 8 + m, :], mg[:, 8 + m, :], ps, MUL, tok), tm)
        for m in range(8):
            t = V.tt(mg[:, m, :], mg[:, m, :], mg[:, 8 + m, :], ADD)
        self.linT(mg, D["w_out_2"], 0, 8, 0, 1024, LAT,
                  lambda m, pi, ps, tok: V.stt(X[:, m, :], ps, LP[:, 16 + m:17 + m], X[:, m, :], MUL, ADD, tok), t)
        tx = V.last()
        self.fence()
        self.top = low
        self.moe(LP, tx)
        self.fence()
        self.top = low
        o = self.alloc(8, 512)
        self.modulate([(o, X, 512, n2[:, 16:24], None)], self.alloc(2048), V.last())
        self.finish(o, V.last())

    def gla(self, h, og, th, n2):
        D, T, V, S, G = self.D, self.T, self.V, self.S, self.G
        W = D["w_in_2"]
        BOTH, LAT = [(0, 512), (512, 768)], [(0, 512)]
        kT, vR, qT = self.alloc(2, 768), self.alloc(6, 512), self.alloc(2, 512)
        rl = self.alloc(2, 768)
        gs = self.alloc(4, 512)
        rw = self.alloc(8, 32)
        du = self.alloc(2, 256)
        cn = {n: self.const(n) for n in ("r64", "le64", "ge64")}
        self.load(rw, W[:, 768:800].rearrange("(k p) c -> p k c", p=128))
        self.load(du[0:16, :, :], D["dup"].rearrange("d r c -> r d c"))
        tl = self.all_loads()

        def cpT(dst):
            def ev(m, pi, ps, tok):
                a, b = BOTH[pi]
                return S.cp(dst[:, m, a:b], ps, tok)
            return ev

        self.linT(h, W, 0, 8, 0, 256, BOTH, cpT(kT), th)
        self.linR(h, 6, W, 8, 256, 512, lambda x, ps, tok: S.cp(vR[:, x, :], ps, tok), th)
        for d in range(2):
            for a, b in BOTH:
                bi, ps, free = self.ps.get()
                for k in range(8):
                    t = T.mm(ps[0:16, 0:b - a], rw[:, k, d * 16:d * 16 + 16], h[:, k, a:b], k == 0, k == 7, free, tl,
                             inc=(k == 7))
                self.ps.done(bi, S.cp(rl[0:16, d, a:b], ps[0:16, 0:b - a], t))
        self.linT(h, W, 0, 8, 800, 256, LAT,
                  lambda m, pi, ps, tok: S.f(qT[:, m, :], ps, ACT.Copy, tok, scale=0.125), th)

        def ev_g(m, pi, ps, tok):
            t = S.f(gs[:, m, :], ps, ACT.Sigmoid, tok)
            return V.tt(gs[:, m, :], gs[:, m, :], ps, MUL, t)

        gi, gw, tg = self.panel(W[:, 1056:1568], 8, 512)

        def gate(m):
            bi, ps, free = self.ps.get()
            for k in range(8):
                t = T.mm(ps, gw[:, k, m * 128:m * 128 + 128], h[:, k, 0:512], k == 0, k == 7, free, tg, inc=(k == 7))
            if m == 3:
                self.wring.done(gi, t)
            self.ps.done(bi, ev_g(m, 0, ps, t))

        t0 = S.last()
        q1 = self.alloc(4, 512)
        ST = [self.alloc(8, 128) for _ in range(4)]
        SC = [self.alloc(4, 128) for _ in range(8)]
        for s in SC:
            V.set(s, 0.0, t0)
        la, B, kw, KW = self.alloc(768), self.alloc(768), self.alloc(768), self.alloc(6, 128)
        qm, km = self.alloc(512), self.alloc(512)
        e1 = self.alloc(768)
        mid, dec = self.alloc(12), self.alloc(12)
        tmp = self.sbring(2, 128)
        U32 = mybir.dt.uint32
        c6 = lambda v: v.rearrange("p (c t) -> p c t", t=64)
        for d in range(2):
            for m in range(2):
                dm = 2 * d + m
                for a, b in BOTH:
                    bi, ps, free = self.ps.get()
                    t = T.mm(ps[:, 0:b - a], du[0:16, d, m * 128:m * 128 + 128], rl[0:16, d, a:b], True, True, free, tl,
                             S.last(), inc=True)
                    t = V.ts(la[:, a:b], ps[:, 0:b - a], n2[:, 29 + dm:30 + dm], None, ADD, None, t)
                    self.ps.done(bi, t)
                t = S.f(e1, la, ACT.Abs, t)
                S.f(e1, e1, ACT.Exp, scale=-1.0)
                t = S.f(e1, e1, ACT.Ln, bias=1.0)
                V.stt(la, la, 0.0, e1, MIN, SUB, t)
                if d == 0:
                    V.scan(B, cn["r64"], la, tl)
                    me, en = 31, 63
                else:
                    V.scan(B[:, ::-1], cn["r64"], la[:, ::-1], tl)
                    me, en = 32, 0
                end = c6(B)[:, :, en:en + 1].to_broadcast([128, 12, 64])
                t = V.tt(c6(e1), end, c6(B), SUB)
                t = S.f(e1, e1, ACT.Exp, t, scale=1.0 / 16)
                S.f(dec, c6(B)[:, :, en], ACT.Exp, scale=1.0 / 16)
                t1 = S.f(q1[:, dm, :], B[:, 0:512], ACT.Exp, scale=1.0 / 16)
                tk = V.tt(kw, kT[:, m, :], e1, MUL, t)
                V.tt(q1[:, dm, :], q1[:, dm, :], qT[:, m, :], MUL, t1)
                V.cp(mid, c6(B)[:, :, me])
                t = V.tt(c6(B[:, 0:512]), c6(B[:, 0:512]), mid[:, 0:8, None].to_broadcast([128, 8, 64]), SUB)
                t1 = S.f(qm, B[:, 0:512], ACT.Exp, t, T.last(), scale=1.0 / 16)
                t2 = S.f(km, B[:, 0:512], ACT.Exp, scale=-1.0 / 16)
                V.tt(qm, qm, qT[:, m, :], MUL, t2)
                tq = V.tt(km, km, kT[:, m, 0:512], MUL)
                gate(dm)
                for x0, x1 in ((0, 4), (4, 6)):
                    bi, ps, free = self.ps.get()
                    for x in range(x0, x1):
                        t = T.tr(ps[:, (x - x0) * 128:(x - x0) * 128 + 128], kw[:, x * 128:x * 128 + 128], self.ident,
                                 free, tk, inc=(x == x1 - 1))
                    t = S.cp(KW[:, x0:x1, :], ps[:, 0:(x1 - x0) * 128].rearrange("p (x c) -> p x c", c=128), t)
                    self.ps.done(bi, t)
                kv = {}
                banks = {}
                for grp in ("ctx", "lat"):
                    xs = (4, 5) if grp == "ctx" else (0, 1, 2, 3)
                    for par in range(2):
                        bi, ps, free = self.ps.get()
                        r = slice(64 * par, 64 * par + 64)
                        for x in xs:
                            cc = (x - xs[0]) * 128
                            for hh in range(2):
                                o = 64 * hh
                                hd = 2 * m + hh
                                t1 = T.mm(ps[o:o + 64, cc:cc + 128], KW[r, x, o:o + 64], vR[r, x, hd * 128:hd * 128 + 128],
                                          True, True, t, free, inc=(x == xs[-1] and hh == 1))
                        for x in xs:
                            cc = (x - xs[0]) * 128
                            kv[2 * x + par] = (ps[:, cc:cc + 128], t1)
                        banks[grp, par] = bi
                order = [8, 9, 10, 11, 0, 1, 2, 3, 4, 5, 6, 7] if d == 0 else [11, 10, 9, 8, 7, 6, 5, 4, 3, 2, 1, 0]
                prev = None
                for n, x in enumerate(order):
                    if n == 11:
                        break
                    nx = order[n + 1]
                    if nx < 8:
                        dst, i = ST[dm][:, nx, :], None
                        tf = None
                    else:
                        i, dst, tf = tmp.get()
                    ps, tkv = kv[x]
                    if prev is None:
                        t = V.cp(dst, ps, tkv, tf)
                    else:
                        t = V.stt(dst, prev, dec[:, x:x + 1], ps, MUL, ADD, tkv, tf)
                    if i is not None:
                        tmp.done(i, t)
                    prev = dst
                for b in banks.values():
                    self.ps.done(b, V.last())
                mask = cn["le64" if d == 0 else "ge64"]
                for hh in range(2):
                    o = slice(64 * hh, 64 * hh + 64)
                    bi, ps, free = self.ps.get()
                    for x in range(4):
                        c = slice(x * 128, x * 128 + 128)
                        t = T.mm(ps[:, c], km[o, c], qm[o, c], True, True, tq, free, inc=(x == 3))
                    sc = SC[4 * d + 2 * m + hh]
                    mk = mask.bitcast(U32)[:, None, :].to_broadcast([128, 4, 128])
                    pv = ps.rearrange("p (x c) -> p x c", x=4)
                    t = V.add(lambda e, sc=sc, mk=mk, pv=pv: e.copy_predicated(sc, mk, pv), t)
                    self.ps.done(bi, t)
                V.wait(T.last()), S.wait(T.last())
        ts = V.last()
        ob = Ring([la[:, 0:512], B[:, 0:512]])
        sb2 = Ring([e1[:, 0:512], kw[:, 0:512]])
        ob.free, sb2.free = [[ts], [ts]], [[ts], [ts]]
        for hd in range(4):
            m, hh = hd // 2, hd % 2
            o = slice(64 * hh, 64 * hh + 64)
            bi, ps, free = self.ps.get()
            for x in range(4):
                c = slice(x * 128, x * 128 + 128)
                T.mmx(ps[:, c], vR[:, x, hd * 128:hd * 128 + 128], SC[hd][:, x, :], True, False, ts, free)
                T.mmx(ps[:, c], vR[:, x, hd * 128:hd * 128 + 128], SC[4 + hd][:, x, :], False, False)
                for d in range(2):
                    for n in (2 * x, 2 * x + 1):
                        t = T.mmx(ps[:, n * 64:n * 64 + 64], ST[2 * d + m][o, n, :], q1[o, 2 * d + m, n * 64:n * 64 + 64],
                                  False, d == 1, inc=(d == 1 and n % 2 == 1))
            i, q, qf = ob.get()
            j, s, sf = sb2.get()
            t1 = S.cp(q, ps, t, qf)
            self.ps.done(bi, t1)
            t2 = S.f(s, q, ACT.Square, sf)
            bi, ps, free = self.ps.get()
            t = T.mm(ps, self.ones, s, True, True, t2, free, inc=True)
            ta, tb = self.rstd(s, ps, 128, 1e-6, t)
            self.ps.done(bi, ta)
            V.stt(q, q, n2[:, 24:25], s, MUL, MUL, tb)
            t = V.tt(og[:, hd, :], q, gs[:, hd, :], MUL)
            ob.done(i, t)
            sb2.done(j, t)

    def moe(self, LP, tx):
        D, T, V, S, G = self.D, self.T, self.V, self.S, self.G
        X = self.X
        Y = self.alloc(8, 1024)
        y_at = self.top - 8192
        keep = self.top
        self.top = y_at
        Sel = self.alloc(4, 16, 64)
        hR = self.alloc(4, 1024)
        self.top = keep
        SW = self.alloc(8, 512)
        xs = self.alloc(8, 1024)
        mark = self.top
        h = self.alloc(8, 512)
        th = self.modulate([(h, X, 512, LP[:, 32:40], LP[:, 24:32])], xs.rearrange("p k t -> p (k t)"), tx)
        slot, e2 = self.const("slot"), self.const("e2")
        aT, rk = self.alloc(512), self.alloc(512)
        ab = self.sbring(2, 512)
        self.top = mark + 8192
        rt = self.alloc(8, 16)
        io = self.const("iota64")
        e2 = e2.rearrange("p (g c) -> p g c", g=8)
        self.load(rt, D["router"].rearrange("(k p) c -> p k c", p=128))
        tl = self.all_loads()
        af = self.alloc(4, 16)
        z = self.alloc(4, 4)
        wk, ms, on = (self.alloc(512) for _ in range(3))
        m8 = self.alloc(8)
        rT = self.alloc(4, 16)
        def route(x):
            bi, ps, free = self.ps.get()
            for k in range(8):
                t = T.mm(ps[:, 0:16], h[:, k, x * 128:x * 128 + 128], rt[:, k, :], k == 0, k == 7, free, tl, th[k],
                         inc=(k == 7))
            yield
            V.red(z[:, x, 0:1], ps[:, 0:16], MAX, t, neg=True)
            t = V.ts(af[:, x, :], ps[:, 0:16], z[:, x, 0:1], None, ADD, None)
            self.ps.done(bi, t)
            t = S.f(af[:, x, :], af[:, x, :], ACT.Exp, t, acc=z[:, x, 1:2])
            yield
            V.rec(z[:, x, 2:3], z[:, x, 1:2], t)
            t = V.ts(af[:, x, :], af[:, x, :], z[:, x, 2:3], None, MUL, None)
            yield
            bi, ps, free = self.ps.get()
            t = T.tr(ps[0:16, 0:128], af[:, x, :], self.ident, t, free, inc=True)
            t = V.cp(aT[0:16, x * 128:x * 128 + 128], ps[0:16, 0:128], t)
            self.ps.done(bi, t)
            yield

        self.side_by_side([route(x) for x in range(4)])
        V.wait(V.everything())
        for x in range(4):
            for k0 in (0, 4):
                bi, ps, free = self.ps.get()
                for k in range(4):
                    t = T.tr(ps[:, k * 128:k * 128 + 128], h[:, k0 + k, x * 128:x * 128 + 128], self.ident, free, th[k0 + k],
                             inc=(k == 3))
                t = S.cp(hR[:, x, k0 * 128:k0 * 128 + 512], ps, t)
                self.ps.done(bi, t)
        thr = S.last()
        a16, w16, m16, r16 = aT[0:16, :], wk[0:16, :], ms[0:16, :], rk[0:16, :]
        V.cp(w16, a16)
        for r in range(8):
            V.add(lambda e: e.max(m8[0:16, :], w16))
            V.add(lambda e: e.match_replace(w16, m8[0:16, :], w16, -1.0))
        V.ts(m16, w16, -1.0, None, EQ, None)
        V.set(on[0:16, :], 1.0)
        V.scan(r16, on[0:16, :], m16)
        V.tt(r16, r16, m16, MUL)
        t = t_rk = V.ts(r16, r16, -1.0, None, ADD, None)
        bi, ps, free = self.ps.get()
        for x in range(4):
            t1 = T.tr(ps[:, x * 16:x * 16 + 16], rk[0:16, x * 128:x * 128 + 128], self.ident[0:16, 0:16], t, free,
                      inc=(x == 3))
        t1 = V.cp(rT, ps[:, 0:64].rearrange("p (x e) -> p x e", x=4), t1)
        self.ps.done(bi, t1)
        for x in range(4):
            tsel = V.tt(Sel[:, x, :, :], rT[:, x, :, None].to_broadcast([128, 16, 64]),
                        io[:, None, :].to_broadcast([128, 16, 64]), EQ, tl)
        def weights():
            for g in range(8):
                i, a, af_ = ab.get()
                bi, ps, free = self.ps.get()
                t1 = T.mm(ps, e2[0:16, g, :], aT[0:16, :], True, True, free, t_rk, tl, inc=True)
                t1 = S.cp(a, ps, t1, af_)
                self.ps.done(bi, t1)
                bi, ps, free = self.ps.get()
                t2 = T.mm(ps, e2[0:16, g, :], rk[0:16, :], True, True, free, inc=True)
                t2 = V.stt(SW[:, g, :], ps, slot[:, 0:1], a, EQ, MUL, t2, t1)
                self.ps.done(bi, t2)
                ab.done(i, t2)

        def gather(eg):
            for k in range(8):
                bi, ps, free = self.ps.get()
                for x in range(4):
                    t = T.mm(ps, hR[:, x, k * 128:k * 128 + 128],
                             Sel[:, x, eg * 8:eg * 8 + 8, :].rearrange("p e s -> p (e s)"), x == 0, x == 3, free, thr, tsel,
                             inc=(x == 3))
                t = (S if k % 2 else V).cp(xs[:, k, eg * 512:eg * 512 + 512], ps, t)
                self.ps.done(bi, t)

        gather(0)
        txs = [V.last(), S.last()]
        self.fence()
        self.top = mark
        self.slot(self.fence())
        self.top = mark + 8192
        ac = self.sbring(2, 1024)
        aTr = self.sbring(2, 8, 64)
        mult = lambda p: slice(64 * p, 64 * p + 64)
        waiting = []

        def scatter():
            ty = [V.last(), S.last()]
            for m in range(8):
                bi, ps, free = self.ps.get()
                for g in waiting:
                    t = T.mm(ps, Y[:, g, m * 128:m * 128 + 128], SW[:, g, :], g == waiting[0], g == waiting[-1],
                             free, ty, tsw, inc=(g == waiting[-1]))
                t = V.stt(X[:, m, :], ps, LP[:, 40 + m:41 + m], X[:, m, :], MUL, ADD, t)
                self.ps.done(bi, t)
            waiting.clear()

        for e in range(0, 16, 2):
            acs = [ac.get() for _ in range(2)]
            tas = [None, None]
            for c in range(2):
                pss = {}
                for w in ("wg", "wu"):
                    got = []
                    for p in range(2):
                        wi, wp, tw = self.panel(D[w][e + p][:, c * 512:c * 512 + 512], 8, 512)
                        got.append((wi, wp, tw, self.ps.get()))
                    for k in range(8):
                        for p, (wi, wp, tw, (bi, ps, free)) in enumerate(got):
                            t = T.mm(ps[mult(p), :], xs[:, k, (e + p) * 64:(e + p) * 64 + 64], wp[:, k, :], k == 0,
                                     k == 7, free, tw, txs, inc=(k == 7))
                            if k == 7:
                                self.wring.done(wi, t)
                                pss[w, p] = (bi, ps, t)
                for p in range(2):
                    o = mult(p)
                    (b1, p1, t1), (b2, p2, t2) = pss["wg", p], pss["wu", p]
                    av = acs[p][1][o, c * 512:c * 512 + 512]
                    t = S.f(av, p1[o, :], ACT.Sigmoid, t1, acs[p][2])
                    t = V.tt(av, av, p1[o, :], MUL, t)
                    self.ps.done(b1, t)
                    t = V.tt(av, av, p2[o, :], MUL, t2)
                    self.ps.done(b2, t)
                    tas[p] = t
            if e == 0:
                gather(1)
                weights()
                txs = tsw = [V.last(), S.last()]
                self.top = mark + 4096
                self.slot([V.last(), S.last(), T.last()])
            if len(waiting) == 2 or e == 14:
                scatter()
            ats = []
            for p in range(2):
                i, a, _ = acs[p]
                j, at_, jw = aTr.get()
                bi, ps, free = self.ps.get()
                for k in range(8):
                    t1 = T.tr(ps[:, k * 64:k * 64 + 64], a[mult(p), k * 128:k * 128 + 128],
                              self.ident[mult(p), mult(p)], tas[p], free, inc=(k == 7))
                ac.done(i, t1)
                t = S.cp(at_, ps.rearrange("p (k s) -> p k s", k=8), t1, jw)
                self.ps.done(bi, t)
                ats.append((j, at_, t))
            for c in range(2):
                got = []
                for p in range(2):
                    wi, wp, tw = self.panel(D["wd"][e + p][:, c * 512:c * 512 + 512], 8, 512)
                    got.append((wi, wp, tw, self.ps.get()))
                for k in range(8):
                    for p, (wi, wp, tw, (bi, ps, free)) in enumerate(got):
                        t = T.mm(ps[mult(p), :], ats[p][1][:, k, :], wp[:, k, :], k == 0, k == 7, free, tw, ats[p][2],
                                 inc=(k == 7))
                        if k == 7:
                            self.wring.done(wi, t)
                            got[p] = (bi, ps, t)
                V.wait(T.last()), S.wait(T.last())
                for p, (bi, ps, t) in enumerate(got):
                    t = (V if p else S).cp(Y[mult(p), e // 2, c * 512:c * 512 + 512], ps[mult(p), :], t)
                    self.ps.done(bi, t)
            for j, _, _ in ats:
                aTr.done(j, T.last())
            waiting.append(e // 2)
        scatter()


def program(nc, D, out, stages=("L0", "L1", "L2")):
    Program(nc, D, stages, out).build()


def kernel(**inputs):
    import concourse.bacc as bacc
    from concourse.bass_utils import run_bass_kernel_spmd

    nc = bacc.Bacc("TRN2", target_bir_lowering=False, num_devices=1)
    arrays = layout_inputs(inputs)
    D = {n: nc.dram_tensor("in_" + n, a.shape, F32, kind="ExternalInput").ap() for n, a in arrays.items()}
    out = nc.dram_tensor("out_T", (1024, 512), F32, kind="ExternalOutput").ap()
    program(nc, D, out)
    r = run_bass_kernel_spmd(nc, [{"in_" + n: a for n, a in arrays.items()}], core_ids=[0])
    return np.ascontiguousarray(r.results[0]["out_T"].T).reshape(1, 512, 1024)
```
